# Optimizing a Trainium2 kernel written in Bass

```python
import math
import jax
import jax.numpy as jnp
from jax import lax
import numpy as np
import jax, jax.numpy as jnp

D_MODEL = 1024
BATCH = 1
SEQ = 256
DEPTH = 1

N_MEM = 256
ATTN_HEADS = 8
ATTN_HEAD_DIM = D_MODEL // 16
DILATED_PATTERNS = ((128, 1), (512, 4), (2048, 16))
RET_HEADS = 4
RET_QK_DIM = D_MODEL // 16
RET_V_DIM = D_MODEL // 8
RET_CHUNK = 128
RET_BASE_EXP = 5
ATTN_WIDTH = ATTN_HEADS * ATTN_HEAD_DIM
RET_QK_WIDTH = RET_HEADS * RET_QK_DIM
RET_V_WIDTH = RET_HEADS * RET_V_DIM
MIX_WIDTH = ATTN_WIDTH + RET_V_WIDTH
IN_PROJ_COLS = 3 * ATTN_WIDTH + 2 * RET_QK_WIDTH + 2 * RET_V_WIDTH
MEM_HEADS = 4
MEM_HEAD_DIM = D_MODEL // MEM_HEADS
N_GROUPS = 4
EXPERTS_PER_GROUP = 8
N_EXPERTS = N_GROUPS * EXPERTS_PER_GROUP
EXPERT_TOP_K = 2
EXPERT_FF = D_MODEL // 2
MOE_BLOCK = 128
NORM_EPS = 1e-6
GN_EPS = 1e-5
NEG_INF = -1e30


def rms_norm(x, w, eps=NORM_EPS):
    xf = x.astype(jnp.float32)
    y = xf * lax.rsqrt(jnp.mean(xf * xf, axis=-1, keepdims=True) + eps)
    return (y * w.astype(jnp.float32)).astype(x.dtype)

def split_heads(t, n_heads, head_dim):
    b, s, _ = t.shape
    return t.reshape(b, s, n_heads, head_dim).transpose(0, 2, 1, 3)

def merge_heads(t):
    b, h, s, d = t.shape
    return t.transpose(0, 2, 1, 3).reshape(b, s, h * d)

def alibi_slopes(n_heads):
    exps = jnp.arange(1, n_heads + 1, dtype=jnp.float32)
    return jnp.exp2(-8.0 * exps / n_heads)

def dilated_window_attention(q, k, v, slopes, window, dilation):
    B, H, S, hd = q.shape
    half = window // (2 * dilation)
    L = S // dilation
    nb = -(-L // half)
    Lp = nb * half

    def to_sub(t):
        return t.reshape(B, H, L, dilation, hd).transpose(0, 1, 3, 2, 4)

    qs, ks, vs = to_sub(q), to_sub(k), to_sub(v)
    qb = jnp.pad(qs, ((0, 0), (0, 0), (0, 0), (0, Lp - L), (0, 0))).reshape(B, H, dilation, nb, half, hd)
    kv_pad = ((0, 0), (0, 0), (0, 0), (half, Lp - L + half), (0, 0))
    kp = jnp.pad(ks, kv_pad).reshape(B, H, dilation, nb + 2, half, hd)
    vp = jnp.pad(vs, kv_pad).reshape(B, H, dilation, nb + 2, half, hd)

    def band(t):
        return jnp.concatenate([t[:, :, :, 0:nb], t[:, :, :, 1:nb + 1], t[:, :, :, 2:nb + 2]], axis=4)

    kb, vb = band(kp), band(vp)
    s = jnp.einsum('bhrnqd,bhrnkd->bhrnqk', qb, kb, preferred_element_type=jnp.float32)
    qi = jnp.arange(half)
    kc = jnp.arange(3 * half)
    delta = kc[None, :] - half - qi[:, None]
    key_pos = jnp.arange(nb)[:, None] * half - half + kc[None, :]
    allowed = (jnp.abs(delta) <= half)[None] & ((key_pos >= 0) & (key_pos < L))[:, None, :]
    bias = -slopes[:, None, None] * (dilation * jnp.abs(delta)).astype(jnp.float32)
    s = s + bias[None, :, None, None]
    s = jnp.where(allowed[None, None, None], s, NEG_INF)
    m = jnp.max(s, axis=-1, keepdims=True)
    p = jnp.exp(s - m)
    denom = jnp.sum(p, axis=-1, keepdims=True)
    o = jnp.einsum('bhrnqk,bhrnkd->bhrnqd', p.astype(v.dtype), vb, preferred_element_type=jnp.float32) / denom
    lse = (m + jnp.log(denom))[..., 0]

    def from_sub(t):
        t = t.reshape((B, H, dilation, Lp) + t.shape[5:])[:, :, :, :L]
        t = jnp.moveaxis(t, 2, 3)
        return t.reshape((B, H, S) + t.shape[4:])

    return from_sub(o), from_sub(lse)

def retention_chunkwise(q, k, v, log_gamma, inclusive):
    B, H, S, dk = q.shape
    dv = v.shape[-1]
    C = RET_CHUNK
    nC = S // C
    qc = q.reshape(B, H, nC, C, dk)
    kc = k.reshape(B, H, nC, C, dk)
    vc = v.reshape(B, H, nC, C, dv)
    i = jnp.arange(C)
    lg = log_gamma[:, None]
    diff = i[:, None] - i[None, :]
    mask = diff >= 0 if inclusive else diff > 0
    decay_mat = jnp.where(mask[None], jnp.exp(lg[:, :, None] * jnp.maximum(diff, 0)[None]), 0.0)
    scores = jnp.einsum('bhnid,bhnjd->bhnij', qc, kc) * decay_mat[None, :, None]
    y_intra = jnp.einsum('bhnij,bhnje->bhnie', scores, vc)
    k_dec = jnp.exp(lg * (C - 1 - i)[None])
    chunk_kv = jnp.einsum('bhnjd,hj,bhnje->bhnde', kc, k_dec, vc)
    chunk_decay = jnp.exp(log_gamma * C)[None, :, None, None]

    def step(state, kv_n):
        return state * chunk_decay + kv_n, state

    _, prev = lax.scan(step, jnp.zeros((B, H, dk, dv), q.dtype), jnp.moveaxis(chunk_kv, 2, 0))
    prev = jnp.moveaxis(prev, 0, 2)
    q_dec = jnp.exp(lg * (i + 1)[None])
    y_cross = jnp.einsum('bhnid,hi,bhnde->bhnie', qc, q_dec, prev)
    return (y_intra + y_cross).reshape(B, H, S, dv)

def head_group_norm(y, w, eps=GN_EPS):
    mu = jnp.mean(y, axis=-1, keepdims=True)
    var = jnp.mean(jnp.square(y - mu), axis=-1, keepdims=True)
    return merge_heads((y - mu) * lax.rsqrt(var + eps)) * w.astype(jnp.float32)

def parallel_mixer(h, w_in, q_norm_w, k_norm_w, decay_f, decay_b, gn_w, w_out):
    f32 = jnp.float32
    proj = h @ w_in
    a3 = 3 * ATTN_WIDTH
    cuts = [ATTN_WIDTH, 2 * ATTN_WIDTH, a3, a3 + RET_QK_WIDTH, a3 + 2 * RET_QK_WIDTH,
            a3 + 2 * RET_QK_WIDTH + RET_V_WIDTH]
    aq, ak, av, rq, rk, rv, rg = jnp.split(proj, cuts, axis=-1)
    q = rms_norm(split_heads(aq, ATTN_HEADS, ATTN_HEAD_DIM), q_norm_w) * (ATTN_HEAD_DIM ** -0.5)
    k = rms_norm(split_heads(ak, ATTN_HEADS, ATTN_HEAD_DIM), k_norm_w)
    v = split_heads(av, ATTN_HEADS, ATTN_HEAD_DIM)
    slopes = alibi_slopes(ATTN_HEADS)
    outs, lses = [], []
    for window, dilation in DILATED_PATTERNS:
        o, lse = dilated_window_attention(q, k, v, slopes, window, dilation)
        outs.append(o)
        lses.append(lse)
    mix_w = jax.nn.softmax(jnp.stack(lses), axis=0)
    attn = jnp.einsum('pbhs,pbhsd->bhsd', mix_w, jnp.stack(outs))
    attn = merge_heads(attn).astype(h.dtype)
    qr = split_heads(rq, RET_HEADS, RET_QK_DIM).astype(f32)
    kr = split_heads(rk, RET_HEADS, RET_QK_DIM).astype(f32) * (RET_QK_DIM ** -0.5)
    vr = split_heads(rv, RET_HEADS, RET_V_DIM).astype(f32)
    lg_f = jax.nn.log_sigmoid(decay_f.astype(f32))
    lg_b = jax.nn.log_sigmoid(decay_b.astype(f32))
    y_f = retention_chunkwise(qr, kr, vr, lg_f, inclusive=True)
    flip = lambda t: jnp.flip(t, axis=2)
    y_b = flip(retention_chunkwise(flip(qr), flip(kr), flip(vr), lg_b, inclusive=False))
    ret = head_group_norm(y_f + y_b, gn_w)
    ret = (jax.nn.silu(rg.astype(f32)) * ret).astype(h.dtype)
    return jnp.concatenate([attn, ret], axis=-1) @ w_out

def memory_cross_attention(h, mem_h, w_mq, w_mkv, q_norm_w, k_norm_w, w_mo):
    q = rms_norm(split_heads(h @ w_mq, MEM_HEADS, MEM_HEAD_DIM), q_norm_w) * (MEM_HEAD_DIM ** -0.5)
    mk, mv = jnp.split(mem_h @ w_mkv, 2, axis=-1)
    k = rms_norm(split_heads(mk, MEM_HEADS, MEM_HEAD_DIM), k_norm_w)
    v = split_heads(mv, MEM_HEADS, MEM_HEAD_DIM)
    s = jnp.einsum('bhsd,bhmd->bhsm', q, k, preferred_element_type=jnp.float32)
    p = jax.nn.softmax(s, axis=-1)
    o = jnp.einsum('bhsm,bhmd->bhsd', p.astype(v.dtype), v)
    return merge_heads(o) @ w_mo

def hierarchical_moe(h, w_group, w_router, w1, w3, w2):
    B, S, D = h.shape
    N = B * S
    t = h.reshape(N, D)
    g_logits = jnp.einsum('nd,dg->ng', t, w_group, preferred_element_type=jnp.float32)
    g_prob = jax.nn.softmax(g_logits, axis=-1)
    grp = jnp.argmax(g_logits, axis=-1)
    g_gate = jnp.take_along_axis(g_prob, grp[:, None], axis=-1)
    e_logits = jnp.einsum('nd,gde->nge', t, w_router, preferred_element_type=jnp.float32)
    e_logits = jnp.take_along_axis(e_logits, grp[:, None, None], axis=1)[:, 0]
    top_vals, top_idx = lax.top_k(e_logits, EXPERT_TOP_K)
    gates = g_gate * jax.nn.softmax(top_vals, axis=-1)
    expert_id = grp[:, None] * EXPERTS_PER_GROUP + top_idx
    A = N * EXPERT_TOP_K
    e_flat = expert_id.reshape(A)
    tok_flat = jnp.repeat(jnp.arange(N, dtype=jnp.int32), EXPERT_TOP_K)
    gate_flat = gates.reshape(A)
    order = jnp.argsort(e_flat)
    e_sorted = e_flat[order]
    counts = jnp.bincount(e_flat, length=N_EXPERTS)
    starts = jnp.cumsum(counts) - counts
    pcounts = (counts + MOE_BLOCK - 1) // MOE_BLOCK * MOE_BLOCK
    pends = jnp.cumsum(pcounts)
    pstarts = pends - pcounts
    dest = pstarts[e_sorted] + jnp.arange(A) - starts[e_sorted]
    n_blocks = -(-(A + N_EXPERTS * MOE_BLOCK) // MOE_BLOCK)
    n_slots = n_blocks * MOE_BLOCK
    slot_tok = jnp.full((n_slots,), N, dtype=jnp.int32).at[dest].set(tok_flat[order])
    slot_gate = jnp.zeros((n_slots,), jnp.float32).at[dest].set(gate_flat[order])
    block_expert = jnp.clip(jnp.searchsorted(pends, jnp.arange(n_blocks) * MOE_BLOCK, side='right'),
                            0, N_EXPERTS - 1)
    t_pad = jnp.concatenate([t, jnp.zeros((1, D), t.dtype)], axis=0)

    def expert_block(args):
        toks, e = args
        xb = t_pad[toks]
        return (jax.nn.silu(xb @ w1[e]) * (xb @ w3[e])) @ w2[e]

    y_slots = lax.map(expert_block, (slot_tok.reshape(n_blocks, MOE_BLOCK), block_expert))
    y_slots = y_slots.reshape(n_slots, D) * slot_gate[:, None]
    y = jax.ops.segment_sum(y_slots, slot_tok, num_segments=N + 1)[:N]
    return y.astype(h.dtype).reshape(B, S, D)

def first_inputs(seed: int = 0) -> dict:
    key = jax.random.key(seed)
    ks = jax.random.split(key, 24)
    f32 = jnp.float32

    def normal(k, shape, scale):
        return jax.random.normal(k, shape, f32) * scale

    def gain(k, shape):
        return 1.0 + 0.05 * jax.random.normal(k, shape, f32)

    base_logit = jnp.log(jnp.exp2(RET_BASE_EXP + jnp.arange(RET_HEADS, dtype=f32)) - 1.0)
    return {
        'x': normal(ks[0], (BATCH, SEQ, D_MODEL), 1.0),
        'mem': normal(ks[1], (BATCH, N_MEM, D_MODEL), 1.0),
        'norm_mix_w': gain(ks[2], (DEPTH, D_MODEL)),
        'w_in': normal(ks[3], (DEPTH, D_MODEL, IN_PROJ_COLS), D_MODEL ** -0.5),
        'attn_q_norm_w': gain(ks[4], (DEPTH, ATTN_HEAD_DIM)),
        'attn_k_norm_w': gain(ks[5], (DEPTH, ATTN_HEAD_DIM)),
        'ret_decay_f': base_logit + 0.1 * jax.random.normal(ks[6], (DEPTH, RET_HEADS), f32),
        'ret_decay_b': base_logit + 0.1 * jax.random.normal(ks[7], (DEPTH, RET_HEADS), f32),
        'ret_gn_w': gain(ks[8], (DEPTH, RET_V_WIDTH)),
        'w_out': normal(ks[9], (DEPTH, MIX_WIDTH, D_MODEL), MIX_WIDTH ** -0.5),
        'norm_mem_w': gain(ks[10], (DEPTH, D_MODEL)),
        'norm_memkv_w': gain(ks[11], (DEPTH, D_MODEL)),
        'w_mq': normal(ks[12], (DEPTH, D_MODEL, D_MODEL), D_MODEL ** -0.5),
        'w_mkv': normal(ks[13], (DEPTH, D_MODEL, 2 * D_MODEL), D_MODEL ** -0.5),
        'mem_q_norm_w': gain(ks[14], (DEPTH, MEM_HEAD_DIM)),
        'mem_k_norm_w': gain(ks[15], (DEPTH, MEM_HEAD_DIM)),
        'w_mo': normal(ks[16], (DEPTH, D_MODEL, D_MODEL), D_MODEL ** -0.5),
        'norm_moe_w': gain(ks[17], (DEPTH, D_MODEL)),
        'w_group': normal(ks[18], (DEPTH, D_MODEL, N_GROUPS), D_MODEL ** -0.5),
        'w_router': normal(ks[19], (DEPTH, N_GROUPS, D_MODEL, EXPERTS_PER_GROUP), D_MODEL ** -0.5),
        'w_exp_gate': normal(ks[20], (DEPTH, N_EXPERTS, D_MODEL, EXPERT_FF), D_MODEL ** -0.5),
        'w_exp_up': normal(ks[21], (DEPTH, N_EXPERTS, D_MODEL, EXPERT_FF), D_MODEL ** -0.5),
        'w_exp_down': normal(ks[22], (DEPTH, N_EXPERTS, EXPERT_FF, D_MODEL), EXPERT_FF ** -0.5),
    }

def first_block(x, mem, norm_mix_w, w_in, attn_q_norm_w, attn_k_norm_w, ret_decay_f, ret_decay_b,
              ret_gn_w, w_out, norm_mem_w, norm_memkv_w, w_mq, w_mkv, mem_q_norm_w, mem_k_norm_w,
              w_mo, norm_moe_w, w_group, w_router, w_exp_gate, w_exp_up, w_exp_down):
    for l in range(DEPTH):
        x = x + parallel_mixer(rms_norm(x, norm_mix_w[l]), w_in[l], attn_q_norm_w[l], attn_k_norm_w[l],
                               ret_decay_f[l], ret_decay_b[l], ret_gn_w[l], w_out[l])
        x = x + memory_cross_attention(rms_norm(x, norm_mem_w[l]), rms_norm(mem, norm_memkv_w[l]),
                                       w_mq[l], w_mkv[l], mem_q_norm_w[l], mem_k_norm_w[l], w_mo[l])
        x = x + hierarchical_moe(rms_norm(x, norm_moe_w[l]), w_group[l], w_router[l],
                                 w_exp_gate[l], w_exp_up[l], w_exp_down[l])
    return x


DEPTH_2 = 2

HEAD_DIM = 64
BLK = 128
GRID_W = 64
WIN_HEADS = 4
WIN_KV_HEADS = 2
WINDOW = 128
MLA_HEADS = 4
MLA_Q_RANK = 256
MLA_KV_RANK = 128
MLA_NOPE = 64
MLA_ROPE = 32
MLA_V = 64
AX_HEADS = 4
AX_KV_HEADS = 2
DIFF_HEADS = 4
DIFF_QK = 32
DIFF_V = 64
A_COLS = (WIN_HEADS + 2 * WIN_KV_HEADS) * HEAD_DIM
B_COLS = MLA_Q_RANK + MLA_KV_RANK + MLA_ROPE
C_COLS = (AX_HEADS + 2 * AX_KV_HEADS) * HEAD_DIM
D_COLS = DIFF_HEADS * (4 * DIFF_QK + DIFF_V)
N_IN = A_COLS + B_COLS + C_COLS + D_COLS
D_MIX = WIN_HEADS * HEAD_DIM + MLA_HEADS * MLA_V + AX_HEADS * HEAD_DIM + DIFF_HEADS * DIFF_V
D_FF = 2816
ROPE_BASE = 10000.0
NORM_EPS_2 = 1e-5
NEG_INF_2 = -1e30


def _layer_norm(x, g, b):
    xf = x.astype(jnp.float32)
    mu = jnp.mean(xf, -1, keepdims=True)
    xc = xf - mu
    var = jnp.mean(xc * xc, -1, keepdims=True)
    y = xc * lax.rsqrt(var + NORM_EPS_2) * g.astype(jnp.float32) + b.astype(jnp.float32)
    return y.astype(x.dtype)

def _rms_norm(x, g):
    xf = x.astype(jnp.float32)
    y = xf * lax.rsqrt(jnp.mean(xf * xf, -1, keepdims=True) + NORM_EPS_2)
    return (y * g.astype(jnp.float32)).astype(x.dtype)

def _swiglu(h, w_gu, w_down):
    gate, up = jnp.split(h @ w_gu, 2, axis=-1)
    return (jax.nn.silu(gate) * up) @ w_down

def _alibi_slopes(n):
    return 2.0 ** (-8.0 * (jnp.arange(n, dtype=jnp.float32) + 1.0) / n)

def _rope_angles(pos, dim):
    inv = ROPE_BASE ** (-jnp.arange(0, dim, 2, dtype=jnp.float32) / dim)
    ang = pos.astype(jnp.float32)[:, None] * inv[None, :]
    return jnp.cos(ang), jnp.sin(ang)

def _apply_rope(x, cos, sin):
    c = cos[:, None, :]
    s = sin[:, None, :]
    x1, x2 = jnp.split(x.astype(jnp.float32), 2, axis=-1)
    return jnp.concatenate([x1 * c - x2 * s, x1 * s + x2 * c], -1).astype(x.dtype)

def _dense_attention(q, k, v, scale):
    B, S, Hq, Dk = q.shape
    Hkv = k.shape[2]
    G = Hq // Hkv
    nb = S // BLK
    qb = q.reshape(B, nb, BLK, Hkv, G, Dk).transpose(1, 0, 2, 3, 4, 5)

    def block(qi):
        s = jnp.einsum('bqhgd,bkhd->bhgqk', qi, k).astype(jnp.float32) * scale
        p = jax.nn.softmax(s, axis=-1)
        return jnp.einsum('bhgqk,bkhd->bqhgd', p.astype(v.dtype), v)

    o = lax.map(block, qb)
    return o.transpose(1, 0, 2, 3, 4, 5).reshape(B, S, Hq * v.shape[-1])

def _mixer_window(a, sink, slopes):
    B, S, _ = a.shape
    nb = S // BLK
    G = WIN_HEADS // WIN_KV_HEADS
    q, k, v = jnp.split(a, [WIN_HEADS * HEAD_DIM, (WIN_HEADS + WIN_KV_HEADS) * HEAD_DIM], axis=-1)
    qb = q.reshape(B, nb, BLK, WIN_KV_HEADS, G, HEAD_DIM)

    def band(t):
        tp = jnp.pad(t.reshape(B, S, WIN_KV_HEADS, HEAD_DIM), ((0, 0), (BLK, BLK), (0, 0), (0, 0)))
        tp = tp.reshape(B, nb + 2, BLK, WIN_KV_HEADS, HEAD_DIM)
        return jnp.concatenate([tp[:, :-2], tp[:, 1:-1], tp[:, 2:]], axis=2)

    kw = band(k)
    vw = band(v)
    s = jnp.einsum('bnqhgd,bnkhd->bnhgqk', qb, kw).astype(jnp.float32) * (HEAD_DIM ** -0.5)
    dist = jnp.abs(jnp.arange(BLK)[:, None] - jnp.arange(3 * BLK)[None, :] + BLK)
    kpos = jnp.arange(nb)[:, None] * BLK - BLK + jnp.arange(3 * BLK)[None, :]
    allowed = (dist <= WINDOW)[None] & ((kpos >= 0) & (kpos < S))[:, None, :]
    bias = -slopes.reshape(WIN_KV_HEADS, G, 1, 1) * dist.astype(jnp.float32)
    s = jnp.where(allowed[None, :, None, None], s + bias, NEG_INF_2)
    sink_logit = jnp.broadcast_to(sink.astype(jnp.float32).reshape(1, 1, WIN_KV_HEADS, G, 1, 1),
                                  s.shape[:-1] + (1,))
    p = jax.nn.softmax(jnp.concatenate([s, sink_logit], axis=-1), axis=-1)[..., :-1]
    o = jnp.einsum('bnhgqk,bnkhd->bnqhgd', p.astype(vw.dtype), vw)
    return o.reshape(B, S, WIN_HEADS * HEAD_DIM)

def _mixer_mla(b, q_norm_g, w_uq, kv_norm_g, w_ukv, pos):
    B, S, _ = b.shape
    c_q, c_kv, k_rope = jnp.split(b, [MLA_Q_RANK, MLA_Q_RANK + MLA_KV_RANK], axis=-1)
    q = (_rms_norm(c_q, q_norm_g) @ w_uq).reshape(B, S, MLA_HEADS, MLA_NOPE + MLA_ROPE)
    kv = (_rms_norm(c_kv, kv_norm_g) @ w_ukv).reshape(B, S, MLA_HEADS, MLA_NOPE + MLA_V)
    cos, sin = _rope_angles(pos, MLA_ROPE)
    q = jnp.concatenate([q[..., :MLA_NOPE], _apply_rope(q[..., MLA_NOPE:], cos, sin)], axis=-1)
    k_r = _apply_rope(k_rope[:, :, None, :], cos, sin)
    k = jnp.concatenate([kv[..., :MLA_NOPE], jnp.broadcast_to(k_r, (B, S, MLA_HEADS, MLA_ROPE))], axis=-1)
    v = kv[..., MLA_NOPE:]
    return _dense_attention(q, k, v, (MLA_NOPE + MLA_ROPE) ** -0.5)

def _mixer_axial(c, q_g, k_g):
    B, S, _ = c.shape
    q, k, v = jnp.split(c, [AX_HEADS * HEAD_DIM, (AX_HEADS + AX_KV_HEADS) * HEAD_DIM], axis=-1)
    q = _rms_norm(q.reshape(B, S, AX_HEADS, HEAD_DIM), q_g)
    k = _rms_norm(k.reshape(B, S, AX_KV_HEADS, HEAD_DIM), k_g)
    v = v.reshape(B, S, AX_KV_HEADS, HEAD_DIM)
    rows = S // GRID_W
    row = jnp.repeat(jnp.arange(rows, dtype=jnp.int32), GRID_W)
    col = jnp.tile(jnp.arange(GRID_W, dtype=jnp.int32), rows)
    half = HEAD_DIM // 2
    cr, sr = _rope_angles(row, half)
    cc, sc = _rope_angles(col, half)

    def axial(t):
        return jnp.concatenate([_apply_rope(t[..., :half], cr, sr), _apply_rope(t[..., half:], cc, sc)], axis=-1)

    return _dense_attention(axial(q), axial(k), v, HEAD_DIM ** -0.5)

def _mixer_diff(d, lam_params, subln_g, slopes, layer_idx):
    B, S, _ = d.shape
    H = DIFF_HEADS
    q, k, v = jnp.split(d, [H * 2 * DIFF_QK, H * 4 * DIFF_QK], axis=-1)
    q = q.reshape(B, S, H, 2, DIFF_QK)
    k = k.reshape(B, S, H, 2, DIFF_QK)
    v = v.reshape(B, S, H, DIFF_V)
    lam_init = 0.8 - 0.6 * math.exp(-0.3 * layer_idx)
    lp = lam_params.astype(jnp.float32)
    lam = jnp.exp(jnp.sum(lp[0] * lp[1])) - jnp.exp(jnp.sum(lp[2] * lp[3])) + lam_init
    nb = S // BLK
    qb = q.reshape(B, nb, BLK, H, 2, DIFF_QK).transpose(1, 0, 2, 3, 4, 5)
    kpos = jnp.arange(S)
    scale = DIFF_QK ** -0.5

    def block(args):
        qi, i = args
        tq = i * BLK + jnp.arange(BLK)
        dist = jnp.abs(tq[:, None] - kpos[None, :]).astype(jnp.float32)
        bias = -slopes[:, None, None] * dist
        s = jnp.einsum('bqhmd,bkhmd->bhmqk', qi, k).astype(jnp.float32) * scale + bias[None, :, None]
        p = jax.nn.softmax(s, axis=-1)
        w = p[:, :, 0] - lam * p[:, :, 1]
        return jnp.einsum('bhqk,bkhd->bqhd', w.astype(v.dtype), v)

    o = lax.map(block, (qb, jnp.arange(nb)))
    o = o.transpose(1, 0, 2, 3, 4).reshape(B, S, H, DIFF_V)
    o = _rms_norm(o, subln_g) * (1.0 - lam_init)
    return o.reshape(B, S, H * DIFF_V)

def _token_mixers(h, w_in, sink, mla_q_norm, mla_w_uq, mla_kv_norm, mla_w_ukv,
                  ax_q_norm, ax_k_norm, diff_lambda, diff_subln, w_out, layer_idx):
    S = h.shape[1]
    proj = h @ w_in
    a, b, c, d = jnp.split(proj, [A_COLS, A_COLS + B_COLS, A_COLS + B_COLS + C_COLS], axis=-1)
    pos = jnp.arange(S, dtype=jnp.int32)
    slopes = _alibi_slopes(WIN_HEADS + DIFF_HEADS)
    o_a = _mixer_window(a, sink, slopes[:WIN_HEADS])
    o_b = _mixer_mla(b, mla_q_norm, mla_w_uq, mla_kv_norm, mla_w_ukv, pos)
    o_c = _mixer_axial(c, ax_q_norm, ax_k_norm)
    o_d = _mixer_diff(d, diff_lambda, diff_subln, slopes[WIN_HEADS:], layer_idx)
    return jnp.concatenate([o_a, o_b, o_c, o_d], axis=-1) @ w_out

def second_inputs(seed: int = 0) -> dict:
    key = jax.random.key(seed)
    ks = jax.random.split(key, 20)
    f32 = jnp.float32
    beta = (8 * DEPTH_2) ** -0.25

    def nrm(k, shape, scale):
        return jax.random.normal(k, shape, f32) * scale

    return {
        "x": nrm(ks[0], (BATCH, SEQ, D_MODEL), 1.0),
        "w_in": nrm(ks[1], (DEPTH_2, D_MODEL, N_IN), D_MODEL ** -0.5),
        "win_sink": nrm(ks[2], (DEPTH_2, WIN_HEADS), 0.5),
        "mla_q_norm": 1.0 + nrm(ks[3], (DEPTH_2, MLA_Q_RANK), 0.02),
        "mla_w_uq": nrm(ks[4], (DEPTH_2, MLA_Q_RANK, MLA_HEADS * (MLA_NOPE + MLA_ROPE)), MLA_Q_RANK ** -0.5),
        "mla_kv_norm": 1.0 + nrm(ks[5], (DEPTH_2, MLA_KV_RANK), 0.02),
        "mla_w_ukv": nrm(ks[6], (DEPTH_2, MLA_KV_RANK, MLA_HEADS * (MLA_NOPE + MLA_V)), MLA_KV_RANK ** -0.5),
        "ax_q_norm": 1.0 + nrm(ks[7], (DEPTH_2, HEAD_DIM), 0.02),
        "ax_k_norm": 1.0 + nrm(ks[8], (DEPTH_2, HEAD_DIM), 0.02),
        "diff_lambda": nrm(ks[9], (DEPTH_2, 4, DIFF_QK), 0.1),
        "diff_subln": 1.0 + nrm(ks[10], (DEPTH_2, DIFF_V), 0.02),
        "w_out": nrm(ks[11], (DEPTH_2, D_MIX, D_MODEL), beta * D_MIX ** -0.5),
        "ffn_w_gu": nrm(ks[12], (DEPTH_2, 2, D_MODEL, 2 * D_FF), D_MODEL ** -0.5),
        "ffn_w_down": nrm(ks[13], (DEPTH_2, 2, D_FF, D_MODEL), beta * D_FF ** -0.5),
        "ln_g": 1.0 + nrm(ks[14], (DEPTH_2, 3, D_MODEL), 0.02),
        "ln_b": nrm(ks[15], (DEPTH_2, 3, D_MODEL), 0.02),
    }

def second_block(x, w_in, win_sink, mla_q_norm, mla_w_uq, mla_kv_norm, mla_w_ukv,
              ax_q_norm, ax_k_norm, diff_lambda, diff_subln, w_out,
              ffn_w_gu, ffn_w_down, ln_g, ln_b):
    alpha = (2 * DEPTH_2) ** 0.25
    for l in range(DEPTH_2):
        x = _layer_norm(alpha * x + 0.5 * _swiglu(x, ffn_w_gu[l, 0], ffn_w_down[l, 0]), ln_g[l, 0], ln_b[l, 0])
        mix = _token_mixers(x, w_in[l], win_sink[l], mla_q_norm[l], mla_w_uq[l], mla_kv_norm[l], mla_w_ukv[l],
                            ax_q_norm[l], ax_k_norm[l], diff_lambda[l], diff_subln[l], w_out[l], l)
        x = _layer_norm(alpha * x + mix, ln_g[l, 1], ln_b[l, 1])
        x = _layer_norm(alpha * x + 0.5 * _swiglu(x, ffn_w_gu[l, 1], ffn_w_down[l, 1]), ln_g[l, 2], ln_b[l, 2])
    return x


def setup_inputs(seed=0):
    out = dict(first_inputs(seed))
    for name, value in second_inputs(seed + 1).items():
        if name != "x":
            out[name + "_2"] = value
    return out


def reference(
    x, mem, norm_mix_w, w_in, attn_q_norm_w, attn_k_norm_w, ret_decay_f, ret_decay_b, ret_gn_w,
    w_out, norm_mem_w, norm_memkv_w, w_mq, w_mkv, mem_q_norm_w, mem_k_norm_w, w_mo, norm_moe_w,
    w_group, w_router, w_exp_gate, w_exp_up, w_exp_down, w_in_2, win_sink_2, mla_q_norm_2,
    mla_w_uq_2, mla_kv_norm_2, mla_w_ukv_2, ax_q_norm_2, ax_k_norm_2, diff_lambda_2,
    diff_subln_2, w_out_2, ffn_w_gu_2, ffn_w_down_2, ln_g_2, ln_b_2,
):
    x = first_block(
        x, mem, norm_mix_w, w_in, attn_q_norm_w, attn_k_norm_w, ret_decay_f, ret_decay_b,
        ret_gn_w, w_out, norm_mem_w, norm_memkv_w, w_mq, w_mkv, mem_q_norm_w, mem_k_norm_w,
        w_mo, norm_moe_w, w_group, w_router, w_exp_gate, w_exp_up, w_exp_down,
    )
    return second_block(
        x, w_in_2, win_sink_2, mla_q_norm_2, mla_w_uq_2, mla_kv_norm_2, mla_w_ukv_2,
        ax_q_norm_2, ax_k_norm_2, diff_lambda_2, diff_subln_2, w_out_2, ffn_w_gu_2,
        ffn_w_down_2, ln_g_2, ln_b_2,
    )


_drawn_inputs = setup_inputs


def setup_inputs(seed=0):
    import zlib

    import numpy as np

    out = dict(_drawn_inputs(seed))
    spreads = {}
    factors = {'attn_q_norm_w': 2.729,
     'mem_q_norm_w': 3.449,
     'mem_k_norm_w': 3.367,
     'win_sink_2': 8.0,
     'mla_q_norm_2': 8.0,
     'mla_kv_norm_2': 8.0,
     'ax_q_norm_2': 8.0,
     'ax_k_norm_2': 8.0,
     'diff_subln_2': 8.0}
    for name, (base, spread) in spreads.items():
        noise = np.random.default_rng([zlib.crc32(name.encode()), seed]).standard_normal(out[name].shape)
        drawn = base * np.exp(spread * noise) if base else spread * noise
        out[name] = jnp.asarray(drawn.astype(out[name].dtype))
    for name, factor in factors.items():
        out[name] = (out[name] * factor).astype(out[name].dtype)
    return out
```

```python
from contextlib import ExitStack

import numpy as np

import concourse.bass as bass
from concourse import mybir

F32 = mybir.dt.float32
F32R = mybir.dt.float32r
I32 = mybir.dt.int32
ALU = mybir.AluOpType
ACT = mybir.ActivationFunctionType
X = mybir.AxisListType.X

P = 128
S = 256
NT = S // P
D = 1024
KD = D // P
CH = 2048
SLOTS = 12
AH, AD = 8, 64
RH, RV = 4, 128
MH, MD = 4, 256
PROJ1 = 3 * AH * AD + 2 * RH * 64 + 2 * RH * RV
NE, EG, NG = 32, 8, 4
FE = 512
CAP = 32
TEAM = P // CAP
TEAMS = NE // TEAM
EPS1, EPS2, GN_EPS = 1e-6, 1e-5, 1e-5
NEG = -1e30
LAYERS = 2
DFF = 2816
FT = DFF // P
FTW = 3 * D
FSLOTS = SLOTS * CH // FTW
ALPHA = (2 * LAYERS) ** 0.25
PROJ2 = 2208
W3 = PROJ2 - 2 * D
A0, C0, D0, B0 = 0, 512, 1024, 1792
QW, KVW, ROPE = 256, 128, 32
BH, BQ = 4, 96
N_CONST = 11
LROW = 384 + 4 + 128 + 2
DENSE1, DENSE2 = 32, 14
UNITS1, UNITS2 = 12, 20
T1, T2 = 38, 27
TEAM_ORDER = [(0, "u"), (1, "u"), (0, "d"), (2, "u"), (1, "d"), (3, "u"), (2, "d"), (3, "d")]
TEAM_CHUNKS = [(e, c) for e, part in TEAM_ORDER for c in (range(4) if part == "u" else range(4, 6))]


def bc(ap, n):
    return ap.unsqueeze(len(ap.shape)).to_broadcast(list(ap.shape) + [n])


class Steps:

    def __init__(self, eng, sem):
        self.eng, self.sem, self.n, self.base = eng, sem, 0, 0

    def then(self, ins):
        ins.then_inc(self.sem, 1)
        self.n += 1
        return ins

    def sync(self):
        self.eng.wait_ge(self.sem, self.base + self.n)

    def link(self, ins):
        self.then(ins)
        self.sync()

    def pad(self, to):
        assert self.n <= to, self.n
        self.eng.sem_inc(self.sem, to - self.n)


def build(nc, d_x, d_mem, d_w1, d_we, d_wf, d_w2, d_cT1, d_row1, d_wr, d_cT2, d_row2, d_ln, d_tab, d_bias, d_out):
    ctx = ExitStack()
    with ctx:
        here = [16640]

        def at(name, offset, shape, dt=F32):
            return nc.alloc_sbuf_tensor_at(name, shape, dt, offset=offset)

        def sb(name, shape, dt=F32):
            size = int(np.prod(shape[1:])) * 4
            offset = here[0]
            here[0] += -(-size // 32) * 32
            return at(name, offset, shape, dt)

        ring = sb("ring", [P, SLOTS * CH])
        x = sb("x", [P, NT, D])
        xT = sb("xT", [P, KD, S])
        bias_at = here[0]
        bias = sb("bias", [P, 8, NT, S])
        ident = sb("ident", [P, P])
        before = sb("before", [P, P])
        ones = sb("ones", [P, P])
        iota = sb("iota", [P, S])
        rel = sb("rel", [P, 2, NT, S])
        desc = sb("desc", [P, NG + NE])
        rope = sb("rope", [P, NT, 96])
        colw = sb("colw", [P, 9, KD])
        row1 = sb("row1", [P, 8])
        wr = sb("wr", [P, KD, NG + NE])
        colw2 = sb("colw2", [P, KD + 3])
        row2 = sb("row2", [P, LROW])
        small = sb("small", [P, 256])
        zeros = sb("zeros", [P, 512], mybir.dt.bfloat16)
        minus_half = sb("minus_half", [P, 8])
        last_turn = sb("last_turn", [P, 1], I32)
        work = here[0]
        assert work + 59680 + 6144 <= nc.sbuf_usable_end, (work, nc.sbuf_usable_end)
        slot = [ring[:, s * CH:(s + 1) * CH] for s in range(SLOTS)]
        proj = at("proj", work, [P, NT, PROJ1])
        xn = at("xn", work, [P, NT, D])
        mq = at("mq", work + 8192, [P, NT, D])
        qkT = at("qkT", work + 24576, [P, 12, S])
        memT = at("memT", work + 24576, [P, KD, S])
        mqT = at("mqT", work + 24576, [P, KD, S])
        mkT = at("mkT", work + 36864, [P, KD, S])
        mv = at("mv", work + 45056, [P, NT, D])
        cat = at("cat", work + 53248, [P, NT, D])
        memt = at("memt", work + 53248, [P, NT, D])
        mk = at("mk", work + 53248, [P, NT, D])
        tmp = at("tmp", work + 61440, [P, D])
        dec = xT[:, 0:4, :].rearrange("p (b t) s -> p b t s", b=2)
        pT_at = xT[:, 4:8, :].rearrange("p (b t) s -> p b t s", b=2)
        xg = at("xg", work + 8192, [P, KD, P])
        yg = at("yg", work + 12288, [P, D])
        oh = at("oh", work + 16384, [P, NT, TEAM, CAP])
        ohg = at("ohg", work + 17408, [P, NT, TEAM, CAP])
        sT = at("sT", work + 18432, [P, S])
        hmid = at("hmid", work + 19456, [P, 2, P])
        hact = at("hact", work + 20480, [P, 2, P])
        hTe = at("hTe", work + 21504, [P, 2, P])
        route = at("route", work + 22528, [P, 5, NT, NE])
        chosen = at("chosen", work + 24576, [P, NT, NE])[:]
        gates = at("gates", work + 24832, [P, NT, NE])[:]
        ranks = at("ranks", work + 25088, [P, NT, NE])[:]
        wh = [at(f"wh{i}", work + i * 4 * FTW, [P, FTW], F32R) for i in range(2)]
        wl = [at(f"wl{i}", work + (2 + i) * 4 * FTW, [P, FTW], F32R) for i in range(2)]
        xh = at("xh", work + 16 * FTW, [P, KD, S], F32R)
        xl = at("xl", work + 16 * FTW + 8192, [P, KD, S], F32R)
        hh = [at(f"hh{i}", bias_at + i * 1024, [P, S], F32R) for i in range(2)]
        hl = [at(f"hl{i}", bias_at + 2048 + i * 1024, [P, S], F32R) for i in range(2)]
        sg = at("sg", bias_at + 4096, [P, 2, S])
        hf = at("hf", bias_at + 6144, [P, 2, S])
        ln = at("ln", bias_at + 8192, [P, 2, D])
        proj2 = at("proj2", work, [P, NT, PROJ2])
        qkT2 = at("qkT2", work + 17664, [P, 18, S])
        cT = at("cT", work + 36096, [P, 3, S])
        qm = at("qm", work + 39168, [P, NT, BH, BQ])
        km = at("km", work + 42240, [P, NT, BH, BQ])
        vm = at("vm", work + 45312, [P, NT, BH, 64])
        cat2 = at("cat2", work + 47360, [P, NT, D])
        lg2 = at("lg2", work + 55552, [P, 2, NT, S + 1])
        tmp2 = at("tmp2", work + 59680, [P, 1536])
        lg1 = at("lg1", work + 61440, [P, 2, NT, S])

        bank = [ctx.enter_context(nc.psum_tensor(f"bank{i}", [P, 512], F32)) for i in range(8)]

        def sem(name):
            return ctx.enter_context(nc.semaphore(name))

        consts_in = sem("consts_in")
        mem_in = sem("mem_in")
        bias_in = sem("bias_in")
        ln_in = sem("ln_in")
        row_in = sem("row_in")
        d_land = [sem(f"d_land{i}") for i in range(SLOTS)]
        e_land = [sem(f"e_land{i}") for i in range(SLOTS)]
        f_land = [sem(f"f_land{i}") for i in range(2)]
        out_done = sem("out_done")
        d_used = sem("d_used")
        e_used = sem("e_used")
        dve_step = sem("dve_step")
        act_step = sem("act_step")
        sumsq = sem("sumsq")
        var_ok = sem("var_ok")
        pow_ok = sem("pow_ok")
        pool_step = sem("pool_step")
        xn_ok = sem("xn_ok")
        t_src = sem("t_src")
        t_ps = sem("t_ps")
        t_out = sem("t_out")
        den_a = sem("den_a")
        den_v = sem("den_v")
        sc_ps = sem("sc_ps")
        lg_ok = sem("lg_ok")
        ex_ok = sem("ex_ok")
        pt_ps = sem("pt_ps")
        pt_ok = sem("pt_ok")
        pv_ps = sem("pv_ps")
        o_ok = sem("o_ok")
        rs_ps = sem("rs_ps")
        rd_in = sem("rd_in")
        rd_ok = sem("rd_ok")
        rp_ok = sem("rp_ok")
        rv_ps = sem("rv_ps")
        ro_ok = sem("ro_ok")
        lgam = sem("lgam")
        gate_ok = sem("gate_ok")
        r_ps = sem("r_ps")
        r_ok = sem("r_ok")
        r_ex = sem("r_ex")
        n_ok = sem("n_ok")
        m_oh = sem("m_oh")
        m_ga = sem("m_ga")
        m_xg = sem("m_xg")
        m_st = sem("m_st")
        m_sT = sem("m_sT")
        m_sg = sem("m_sg")
        m_h = sem("m_h")
        m_hp = sem("m_hp")
        m_hT = sem("m_hT")
        m_yA = sem("m_yA")
        m_yV = sem("m_yV")
        m_sc = sem("m_sc")
        x_ok = sem("x_ok")
        xh_ok = sem("xh_ok")
        xl_ok = sem("xl_ok")
        wh_ok = sem("wh_ok")
        wl_ok = sem("wl_ok")
        f_gu = sem("f_gu")
        f_sg = sem("f_sg")
        f_h = sem("f_h")
        f_dn = sem("f_dn")
        c_ps = sem("c_ps")
        c_a = sem("c_a")
        lam_in = sem("lam_in")
        lam_ex = sem("lam_ex")
        ln_ok = sem("ln_ok")

        block = ctx.enter_context(nc.Block())

        dve_loop = sem("dve_loop")
        rope_ok = sem("rope_ok")
        ax_ok = sem("ax_ok")
        kv_ok = sem("kv_ok")
        f_hv = sem("f_hv")
        z_ok = sem("z_ok")

        ss, rs = small[:, 0:2], small[:, 4:6]
        ssq = small[:, 8:40].rearrange("p (t h) -> p t h", t=NT)
        rsq = small[:, 40:72].rearrange("p (t h) -> p t h", t=NT)
        nmax = small[:, 72:76].rearrange("p (b t) -> p b t", b=2)
        den = small[:, 76:80].rearrange("p (b t) -> p b t", b=2)
        rden = small[:, 80:84].rearrange("p (b t) -> p b t", b=2)
        lgm = small[:, 84:92]
        lt = small[:, 92:132].rearrange("p (a h) -> p a h", h=8)
        bn = small[:, 132:156].rearrange("p (t c k) -> p t c k", t=NT, c=2)
        mean = small[:, 156:160].rearrange("p (t k) -> p t k", t=NT)
        lam2 = small[:, 160:162]
        nlam = small[:, 162:164]
        nrd = small[:, 164:168].rearrange("p (b t) -> p b t", b=2)
        gs = small[:, 168:232]

        def tok(i):
            return slice(i * P, (i + 1) * P)

        class Unit:

            def __init__(self, q, k, v, scale, out, bias=None, sink=None, half=None):
                self.q, self.k, self.v, self.scale, self.out = q, k, v, scale, out
                self.bias, self.sink, self.half = bias, sink, half
                self.dv = v[0].shape[-1]

        def head_rows(T, blk, first, n):
            return [T[first:first + n, blk, tok(i)] for i in range(NT)], T[first:first + n, blk, :]

        units1 = []
        for h in range(AH):
            rows = 64 * (h % 2)
            q, _ = head_rows(qkT, h // 2, rows, 64)
            _, k = head_rows(qkT, 4 + h // 2, rows, 64)
            c = 2 * AH * AD + h * AD
            units1.append(Unit([q], [k], [proj[:, t, c:c + AD] for t in range(NT)], AD ** -0.5,
                               cat[:, :, h * AD:(h + 1) * AD], bias=bias[:, h]))
        for h in range(MH):
            qs = [head_rows(mqT, 2 * h + b, 0, P)[0] for b in range(2)]
            ks = [head_rows(mkT, 2 * h + b, 0, P)[1] for b in range(2)]
            units1.append(Unit(qs, ks, [mv[:, t, h * MD:(h + 1) * MD] for t in range(NT)], MD ** -0.5,
                               cat[:, :, h * MD:(h + 1) * MD]))
        units2 = []
        for h in range(4):
            at_q, kv = [0, 2, 1, 3][h], h // 2
            q, _ = head_rows(qkT2, at_q // 2, 64 * (at_q % 2), 64)
            _, k = head_rows(qkT2, 2, 64 * kv, 64)
            c = A0 + 384 + 64 * kv
            units2.append(Unit([q], [k], [proj2[:, t, c:c + 64] for t in range(NT)], 64 ** -0.5,
                               cat2[:, :, h * 64:(h + 1) * 64], bias=bias[:, h], sink=row2[:, 384 + h:385 + h]))
        for n in range(8):
            h, m = n // 2, n % 2
            q, _ = head_rows(qkT2, 6 + n // 4, 32 * (n % 4), 32)
            _, k = head_rows(qkT2, 8 + n // 4, 32 * (n % 4), 32)
            c = D0 + 512 + 64 * h
            units2.append(Unit([q], [k], [proj2[:, t, c:c + 64] for t in range(NT)], 32 ** -0.5,
                               cat2[:, :, 768 + h * 64:768 + (h + 1) * 64], bias=bias[:, 4 + h], half=m))
        for h in range(4):
            at_q, kv = [0, 2, 1, 3][h], h // 2
            q, _ = head_rows(qkT2, 3 + at_q // 2, 64 * (at_q % 2), 64)
            _, k = head_rows(qkT2, 5, 64 * kv, 64)
            c = C0 + 384 + 64 * kv
            units2.append(Unit([q], [k], [proj2[:, t, c:c + 64] for t in range(NT)], 64 ** -0.5,
                               cat2[:, :, 512 + h * 64:512 + (h + 1) * 64]))
        for h in range(BH):
            q, _ = head_rows(qkT2, 10 + h, 0, BQ)
            _, k = head_rows(qkT2, 14 + h, 0, BQ)
            units2.append(Unit([q], [k], [vm[:, t, h, :] for t in range(NT)], BQ ** -0.5,
                               cat2[:, :, 256 + h * 64:256 + (h + 1) * 64]))

        PART1 = [0, 4, 8, 12, 16, 20, 24, 28, 32]
        PART2 = [0, 4, 8, 9, 10, 14]
        COPY1 = [1, 2, 3, 4, 5, 5, 6, 6]

        def tiles_in(s):
            return range(s * CH // FTW, ((s + 1) * CH - 1) // FTW + 1)

        def chunks_in(v):
            return range(v * FTW // CH, ((v + 1) * FTW - 1) // CH + 1)

        last_tile = {v % FSLOTS: v for v in range(FT)}
        D_AT = 9
        e0 = DENSE1 % SLOTS
        dense_slot = [(D_AT + c) % SLOTS for c in range(DENSE2)]
        last_dense = {s: c for c, s in enumerate(dense_slot)}

        def inverse_root(pool, dst):
            half = minus_half[:, 0:1]
            for _ in range(len(dst.shape) - 2):
                half = half.unsqueeze(1)
            pool.tensor_tensor(dst, dst, half.to_broadcast(list(dst.shape)), ALU.pow).then_inc(pow_ok, 1)

        LAST = {}
        for n_c, (e, c) in enumerate(TEAM_CHUNKS):
            LAST[e, "u" if c < 4 else "d"] = n_c + 1

        def load_turns(eng):
            eng.wait_ge(n_ok, 1)
            return eng.value_load(last_turn[0:1, 0:1], min_val=TEAMS - 1, max_val=TEAMS * (S // CAP) - 1)

        def pe_moe(pe, tokens):
            pe.wait_ge(xn_ok, 4)
            pe_T(pe, tokens(xn), 34)
            pe.wait_ge(t_out, 38)
            for i in range(NT):
                for k in range(KD):
                    ins = pe.matmul(bank[0][:, i * 64:i * 64 + NG + NE], xT[:, k, tok(i)], wr[:, k],
                                    start=(k == 0), stop=(k == KD - 1))
            ins.then_inc(r_ps, 1)
            pe.wait_ge(r_ok, 2)
            pe.matmul(bank[1][:, 0:NE], before[:], chosen[:, 0], start=True, stop=True)
            pe.matmul(bank[1][:, NE:2 * NE], ones[:], chosen[:, 0], start=True, stop=False)
            pe.matmul(bank[1][:, NE:2 * NE], before[:], chosen[:, 1], start=False, stop=True)
            pe.matmul(bank[1][:, 2 * NE:3 * NE], ones[:], chosen[:, 0], start=True, stop=False)
            pe.matmul(bank[1][:, 2 * NE:3 * NE], ones[:], chosen[:, 1], start=False, stop=True).then_inc(r_ps, 1)
            last = load_turns(pe)
            for b in range(4):
                ins = pe.matmul(bank[b][:], zeros[:, 0:P], zeros[:], start=True, stop=False, skip_group_check=True)
            ins.then_inc(m_sc, 1)
            with pe.Fori(0, last + 1) as it:
                pe.wait_ge(m_oh, it * 2 + 1)
                for half in range(2):
                    for k in range(4):
                        for i in range(NT):
                            ins = pe.matmul(bank[4 + half][:, k * P:(k + 1) * P],
                                            xn[:, i, (4 * half + k) * P:(4 * half + k + 1) * P],
                                            oh[:, i].rearrange("p e s -> p (e s)"), start=(i == 0), stop=(i == 1))
                    ins.then_inc(m_ga, 1)
                pe.wait_ge(m_oh, it * 2 + 2)
                for i in range(NT):
                    ins = pe.transpose(bank[7][:, tok(i)], ohg[:, i].rearrange("p e s -> p (e s)"), ident[:])
                ins.then_inc(m_st, 1)
                pe.wait_ge(m_xg, it * 2 + 2)
                j = 0
                for e, part in TEAM_ORDER:
                    if part == "u":
                        for c in range(4):
                            s = (e0 + j) % SLOTS
                            pe.wait_ge(e_land[s], (it * 2 + (j // SLOTS + 1)) * 16)
                            w = slot[s].rearrange("p (k q n) -> p k q n", k=2, q=4)
                            for kk in range(2):
                                k = 2 * c + kk
                                for q in range(4):
                                    ins = pe.matmul(bank[4 + e % 2][q * CAP:(q + 1) * CAP, 0:2 * P],
                                                    xg[:, k, e * CAP:(e + 1) * CAP], w[:, kk, q],
                                                    start=(k == 0), stop=(k == KD - 1), skip_group_check=True)
                            ins.then_inc(e_used, 1)
                            j += 1
                        continue
                    pe.wait_ge(m_h, it * 4 + (e + 1))
                    if e == 0:
                        pe.wait_ge(m_sT, it + 1)
                    pe.transpose(bank[7][:, 0:P], hmid[:, e % 2], ident[:]).then_inc(m_hp, 1)
                    pe.wait_ge(m_hT, it * 4 + (e + 1))
                    if e >= 1:
                        pe.wait_ge(m_yA, it * 4 + e)
                        pe.wait_ge(m_yV, it * 4 + e)
                    for c in range(2):
                        s = (e0 + j) % SLOTS
                        pe.wait_ge(e_land[s], (it * 2 + (j // SLOTS + 1)) * 16)
                        w = slot[s].rearrange("p (k q n) -> p k q n", k=2, q=4)
                        for kk in range(2):
                            k = 2 * c + kk
                            for q in range(4):
                                ins = pe.matmul(bank[6][q * CAP:(q + 1) * CAP, 0:2 * P],
                                                hTe[:, e % 2, k * CAP:(k + 1) * CAP], w[:, kk, q],
                                                start=(k == 0), stop=(k == 3), skip_group_check=True)
                        ins.then_inc(e_used, 1)
                        j += 1
                pe.wait_ge(m_yA, it * 4 + TEAM)
                pe.wait_ge(m_yV, it * 4 + TEAM)
                for i in range(NT):
                    for c in range(2):
                        ins = pe.matmul(bank[2 * i + c][:], sT[:, tok(i)], yg[:, c * 512:(c + 1) * 512],
                                        start=False, stop=False, skip_group_check=True)
                ins.then_inc(m_sc, 1)

        def out_rows(eng, it, e, quarters, copy, post):
            eng.wait_ge(e_used, it * 24 + LAST[e, "d"])
            for q in quarters:
                ins = copy(yg[e * CAP:(e + 1) * CAP, q * 2 * P:(q + 1) * 2 * P], bank[6][q * CAP:(q + 1) * CAP, 0:2 * P])
            ins.then_inc(post, 1)

        def act_moe(act, st):
            act.wait_ge(r_ok, 1)
            act.activation(gs[:, 0:10], gs[:, 0:10], ACT.Exp).then_inc(r_ex, 1)
            last = load_turns(act)

            def silu(it, e):
                act.wait_ge(e_used, it * 24 + LAST[e, "u"])
                act.activation(hact[:, e % 2], bank[4 + e % 2][:, 0:P], ACT.Silu).then_inc(m_sg, 1)

            def hidden_T(it, e):
                act.wait_ge(m_hp, it * 4 + (e + 1))
                act.activation(hTe[:, e % 2], bank[7][:, 0:P], ACT.Copy).then_inc(m_hT, 1)

            def out(it, e):
                out_rows(act, it, e, (0, 1), lambda o, i: act.activation(o, i, ACT.Copy), m_yA)

            with act.Fori(0, last + 1) as it:
                act.wait_ge(m_st, it + 1)
                act.wait_ge(m_sc, it + 1)
                act.activation(sT[:], bank[7][:, 0:S], ACT.Copy).then_inc(m_sT, 1)
                silu(it, 0)
                silu(it, 1)
                hidden_T(it, 0)
                out(it, 0)
                silu(it, 2)
                hidden_T(it, 1)
                out(it, 1)
                silu(it, 3)
                hidden_T(it, 2)
                out(it, 2)
                hidden_T(it, 3)
                out(it, 3)

        def dve_moe(dve, st):
            dve_T(dve, xT, KD, 34, colw[:, 8])
            el, em, key = route[:, 0], route[:, 1], route[:, 2]
            first, second = route[:, 3], route[:, 4]
            gl = gs[:, 16:24].rearrange("p (t g) -> p t g", t=NT)
            gd = gs[:, 0:8].rearrange("p (t g) -> p t g", t=NT)
            gkey = gs[:, 24:32].rearrange("p (t g) -> p t g", t=NT)
            top_g, top_k = gs[:, 32:34], gs[:, 34:36]
            v1, v2, ggate, p1, p2 = (gs[:, c:c + 2] for c in (36, 38, 40, 42, 44))
            desc_g = desc[:, 0:NG].unsqueeze(1).to_broadcast([P, NT, NG])
            desc_e = desc[:, NG:].unsqueeze(1).to_broadcast([P, NT, NE])
            dve.wait_ge(r_ps, 1)
            logits = bank[0][:, 0:P].rearrange("p (t n) -> p t n", t=NT)
            st.then(dve.tensor_copy(gl, logits[:, :, 0:NG]))
            st.link(dve.tensor_copy(el, logits[:, :, NG:NG + NE]))

            def first_max(top, key_, vals, order, n, onehot):
                st.link(dve.tensor_reduce(top, vals, X, ALU.max))
                st.link(dve.tensor_tensor(key_, vals, bc(top, n), ALU.is_equal))
                st.link(dve.tensor_tensor(key_, key_, order, ALU.mult))
                st.link(dve.tensor_reduce(top_k, key_, X, ALU.max))
                st.link(dve.tensor_tensor(onehot, key_, bc(top_k, n), ALU.is_equal))

            first_max(top_g, gkey, gl, desc_g, NG, gkey)
            st.then(dve.tensor_tensor(gd, gl, bc(top_g, NG), ALU.subtract))
            st.link(dve.tensor_scalar(gkey, gkey, -1.0, -NEG, ALU.add, ALU.mult))
            em4 = em.rearrange("p t (g e) -> p t g e", g=NG)
            st.link(dve.tensor_tensor(em4, el.rearrange("p t (g e) -> p t g e", g=NG), bc(gkey, EG), ALU.add))
            first_max(v1, key, em, desc_e, NE, first)
            st.link(dve.scalar_tensor_tensor(em, first, NEG, em, ALU.mult, ALU.add))
            first_max(v2, key, em, desc_e, NE, second)
            dve.tensor_tensor(gs[:, 8:10], v2, v1, ALU.subtract).then_inc(r_ok, 1)
            st.then(dve.tensor_tensor(chosen, first, second, ALU.add))
            st.sync()
            dve.wait_ge(r_ex, 1)
            dve.tensor_reduce(ggate, gd, X, ALU.add).then_inc(r_ok, 1)
            dve.wait_ge(r_ok, 2)
            st.then(dve.tensor_scalar(p1, gs[:, 8:10], 1.0, None, ALU.add))
            st.link(dve.reciprocal(ggate, ggate))
            st.link(dve.reciprocal(p1, p1))
            st.link(dve.tensor_tensor(p1, p1, ggate, ALU.mult))
            st.link(dve.tensor_tensor(p2, gs[:, 8:10], p1, ALU.mult))
            st.then(dve.tensor_tensor(gates, first, bc(p1, NE), ALU.mult))
            st.link(dve.tensor_tensor(key, second, bc(p2, NE), ALU.mult))
            st.then(dve.tensor_tensor(gates, gates, key, ALU.add))
            dve.wait_ge(r_ps, 2)
            rank = bank[1][:, 0:2 * NE].rearrange("p (t n) -> p t n", t=NT)
            st.link(dve.scalar_tensor_tensor(ranks, rank, 1.0, chosen, ALU.add, ALU.mult))
            st.link(dve.tensor_scalar(ranks, ranks, -1.0, None, ALU.add))
            st.link(dve.tensor_reduce(gs[:, 46:47], bank[1][:, 2 * NE:3 * NE], X, ALU.max))
            st.link(dve.tensor_scalar(gs[:, 48:56], iota[:, 0:S:CAP], gs[:, 46:47], float(TEAMS), ALU.is_lt, ALU.mult))
            st.link(dve.tensor_reduce(gs[:, 47:48], gs[:, 48:56], X, ALU.add))
            dve.tensor_scalar(last_turn[:], gs[:, 47:48], -1.0, None, ALU.add).then_inc(n_ok, 1)
            last = load_turns(dve)

            def hidden(it, e):
                dve.wait_ge(m_sg, it * 4 + (e + 1))
                dve.tensor_tensor(hmid[:, e % 2], hact[:, e % 2], bank[4 + e % 2][:, P:2 * P], ALU.mult).then_inc(m_h, 1)

            def out(it, e):
                out_rows(dve, it, e, (2, 3), dve.tensor_copy, m_yV)

            with dve.Fori(0, last + 1) as it:
                team, lap = it % TEAMS, it // TEAMS
                slots = iota[:, bass.ds(lap * CAP, CAP)].unsqueeze(1).to_broadcast([P, TEAM, CAP])
                for i in range(NT):
                    ins = dve.tensor_tensor(oh[:, i], bc(ranks[:, i, bass.ds(team * TEAM, TEAM)], CAP), slots, ALU.is_equal)
                    if i == 0:
                        ins.then_inc(dve_loop, 1)
                ins.then_inc(m_oh, 1)
                dve.wait_ge(dve_loop, it + 1)
                dve.wait_ge(m_oh, it * 2 + 1)
                for i in range(NT):
                    ins = dve.tensor_tensor(ohg[:, i], oh[:, i], bc(gates[:, i, bass.ds(team * TEAM, TEAM)], CAP), ALU.mult)
                ins.then_inc(m_oh, 1)
                for half in range(2):
                    dve.wait_ge(m_ga, it * 2 + (half + 1))
                    dve.tensor_tensor(xg[:, 4 * half:4 * half + 4], bank[4 + half][:].rearrange("p (k s) -> p k s", k=4),
                                      bc(colw[:, 8, 4 * half:4 * half + 4], P), ALU.mult).then_inc(m_xg, 1)
                hidden(it, 0)
                hidden(it, 1)
                dve.wait_ge(m_sc, it + 1)
                out(it, 0)
                hidden(it, 2)
                out(it, 1)
                hidden(it, 3)
                out(it, 2)
                out(it, 3)
            dve.wait_ge(m_sc, last + 2)
            for i in range(NT):
                for c in range(2):
                    ins = dve.tensor_tensor(x[:, i, c * 512:(c + 1) * 512], bank[2 * i + c][:],
                                            x[:, i, c * 512:(c + 1) * 512], ALU.add)
                    if i + c < 2:
                        st.then(ins)
            st.sync()
            ins.then_inc(x_ok, 1)

        FFN_W = 2 * FT
        DVE_PAD, POOL_PAD = 256, 48
        POW2, VAR1, VAR2 = 5, 7, 5
        fills1 = [sum(c % SLOTS == s for c in range(DENSE1)) for s in range(SLOTS)]
        fills2 = [dense_slot.count(s) for s in range(SLOTS)]

        def dense_ready(l, c):
            s = dense_slot[c]
            return s, (l * fills2[s] + fills1[s] + dense_slot[:c + 1].count(s)) * 16

        def ring_tile(v):
            return (v % FSLOTS) * FTW

        def layer_loads(sp):
            for p in range(2):
                sp.sem_inc(f_land[p], 16)
            with sp.Fori(0, LAYERS) as l:
                for f in range(2):
                    g = l * 2 + f

                    def tile(v, p):
                        sp.wait_ge(f_land[p], (g * (FT // 2) + v // 2 + 1) * 16)
                        sp.dma_start(ring[:, bass.ds(ring_tile(v), FTW)], d_wf[g * FT + v]).then_inc(f_land[p], 16)

                    for v in range(FSLOTS):
                        if f == 0:
                            sp.wait_ge(wl_ok, g * FFN_W + (2 * last_tile[v] + 2))
                        else:
                            sp.wait_ge(d_used, l * DENSE2 + (DENSE1 + 1 + max(last_dense[s] for s in chunks_in(v))))
                        tile(v, v % 2)
                    with sp.Fori(FSLOTS // 2, FT // 2) as i:
                        for p in range(2):
                            sp.wait_ge(wl_ok, g * FFN_W + i * 4 + (2 * p + FFN_W + 2 - 2 * FSLOTS))
                            sp.wait_ge(f_land[p], (g * (FT // 2) + i + 1) * 16)
                            sp.dma_start(ring[:, bass.ds(ring_tile(i * 2 + p), FTW)],
                                         d_wf[g * FT + i * 2 + p]).then_inc(f_land[p], 16)
                    if f == 0:
                        for c in range(DENSE2):
                            s = dense_slot[c]
                            if c < SLOTS:
                                sp.wait_ge(wl_ok, g * FFN_W + (FFN_W + 2 * max(last_tile[q] for q in tiles_in(s)) + 2))
                            else:
                                sp.wait_ge(d_used, l * DENSE2 + (DENSE1 + c - SLOTS + 1))
                            sp.dma_start(slot[s], d_w2[l * DENSE2 + c]).then_inc(d_land[s], 16)

        def pe_ffn(pe, l, f, tokens):
            g = l * 2 + f
            tb = l * T2 + (T1 + (0 if f == 0 else T2 - 4))
            pe.wait_ge(x_ok, l * 3 + (3 + 2 * f))
            pe_T(pe, tokens(x), tb)
            for b in range(4):
                ins = pe.matmul(bank[b][:], zeros[:, 0:P], zeros[:], start=True, stop=False, skip_group_check=True)
            ins.then_inc(f_dn, 1)
            pe.wait_ge(t_out, tb + 4)

            def up(t, p):
                pe.wait_ge(wl_ok, g * FFN_W + t * 2 + (FFN_W + 1))
                for m in range(2):
                    for k in range(KD):
                        cols = slice(k * 2 * P + m * P, k * 2 * P + (m + 1) * P)
                        for n, (w, v) in enumerate(((wh, xh), (wh, xl), (wl, xh))):
                            ins = pe.matmul(bank[4 + p][:, m * S:(m + 1) * S], w[p][:, cols], v[:, k],
                                            start=(k == 0 and n == 0), stop=(k == KD - 1 and n == 2))
                ins.then_inc(f_gu, 1)

            def down(t, p):
                pe.wait_ge(f_h, g * FT + t + 1)
                pe.wait_ge(wl_ok, g * FFN_W + t * 2 + (FFN_W + 2))
                for i in range(NT):
                    for v, w in ((hh, wh), (hl, wh), (hh, wl)):
                        for c in range(2):
                            ins = pe.matmul(bank[2 * i + c][:], v[p][:, tok(i)],
                                            w[p][:, 2 * D + c * 512:2 * D + (c + 1) * 512],
                                            start=False, stop=False, skip_group_check=True)
                ins.then_inc(f_dn, 1)

            up(0, 0)
            with pe.Fori(0, FT // 2 - 1) as i:
                for p in range(2):
                    up(i * 2 + (p + 1), 1 - p)
                    down(i * 2 + p, p)
            up(FT - 1, 1)
            down(FT - 2, 0)
            down(FT - 1, 1)

        def act_ffn(act, l, f):
            g = l * 2 + f
            tb = l * T2 + (T1 + (0 if f == 0 else T2 - 4))
            for j in range(4):
                act.wait_ge(t_ps, tb + (j + 1))
                act.activation(xh[:, 2 * j:2 * j + 2].rearrange("p k s -> p (k s)"), bank[4 + j][:], ACT.Copy)\
                   .then_inc(xh_ok, 1)
            if f == 1:
                load_ln(act, l, 2)

            def high(t, p, down):
                cols = slice(2 * D, FTW) if down else slice(0, 2 * D)
                n = cols.stop - cols.start
                act.activation(wh[p][:, cols], ring[:, bass.ds(ring_tile(t) + cols.start, n)], ACT.Copy).then_inc(wh_ok, 1)

            def landed(t, half, p):
                act.wait_ge(f_land[p], (g * (FT // 2) + half + 2) * 16)

            def silu(t, p):
                act.wait_ge(f_gu, g * FT + t + 1)
                act.activation(sg[:, p], bank[4 + p][:, 0:S], ACT.Silu).then_inc(f_sg, 1)

            def down_free(t):
                act.wait_ge(f_dn, g * (FT + 1) + t + 1)

            landed(0, 0, 0)
            high(0, 0, False)
            high(0, 0, True)
            landed(1, 0, 1)
            high(1, 1, False)
            with act.Fori(0, FT // 2 - 1) as i:
                for p in range(2):
                    silu(i * 2 + p, p)
                    down_free(i * 2 + p)
                    high(i * 2 + (p + 1), 1 - p, True)
                    landed(None, i + 1, p)
                    high(i * 2 + (p + 2), p, False)
            silu(FT - 2, 0)
            down_free(FT - 2)
            high(FT - 1, 1, True)
            silu(FT - 1, 1)

        def dve_ffn(dve, st, l, f):
            g = l * 2 + f
            tb = l * T2 + (T1 + (0 if f == 0 else T2 - 4))
            for j in range(4):
                dve.wait_ge(t_ps, tb + (j + 1))
                dve.wait_ge(xh_ok, g * 4 + (j + 1))
                dve.tensor_tensor(xl[:, 2 * j:2 * j + 2].rearrange("p k s -> p (k s)"), bank[4 + j][:],
                                  xh[:, 2 * j:2 * j + 2].rearrange("p k s -> p (k s)").bitcast(F32),
                                  ALU.subtract).then_inc(t_out, 1)

            def low(t, half, p, down):
                cols = slice(2 * D, FTW) if down else slice(0, 2 * D)
                n = cols.stop - cols.start
                dve.wait_ge(wh_ok, g * FFN_W + t * 2 + (2 if down else 1))
                dve.tensor_tensor(wl[p][:, cols], ring[:, bass.ds(ring_tile(t) + cols.start, n)],
                                  wh[p][:, cols].bitcast(F32), ALU.subtract).then_inc(wl_ok, 1)

            def hidden(t, p):
                dve.wait_ge(f_sg, g * FT + t + 1)
                dve.tensor_tensor(hf[:, p], sg[:, p], bank[4 + p][:, S:2 * S], ALU.mult).then_inc(f_hv, 1)
                dve.wait_ge(f_hv, (g * FT + t) * 2 + 1)
                dve.tensor_copy(hh[p][:], hf[:, p]).then_inc(f_hv, 1)
                dve.wait_ge(f_hv, (g * FT + t) * 2 + 2)
                dve.tensor_tensor(hl[p][:], hf[:, p], hh[p][:].bitcast(F32), ALU.subtract).then_inc(f_h, 1)

            low(0, 0, 0, False)
            low(0, 0, 0, True)
            low(1, 0, 1, False)
            st.then(dve.tensor_scalar(x[:], x[:], ALPHA, None, ALU.mult))
            with dve.Fori(0, FT // 2 - 1) as i:
                for p in range(2):
                    hidden(i * 2 + p, p)
                    low(i * 2 + (p + 1), 0, 1 - p, True)
                    low(i * 2 + (p + 2), 0, p, False)
            hidden(FT - 2, 0)
            low(FT - 1, 0, 1, True)
            hidden(FT - 1, 1)
            dve.wait_ge(f_dn, (g + 1) * (FT + 1))
            layer_norm(dve, st, l, 2 * f, 0.5)

        def load_ln(act, l, n):
            act.dma_start(ln[:].rearrange("p a d -> p (a d)"), d_ln[l * 3 + n]).then_inc(ln_in, 16)

        def layer_norm(dve, st, l, n, scale):
            st.sync()
            for i in range(NT):
                for c in range(2):
                    part = x[:, i, c * 512:(c + 1) * 512]
                    st.then(dve.scalar_tensor_tensor(part, bank[2 * i + c][:], scale, part, ALU.mult, ALU.add))
            st.sync()
            for i in range(NT):
                for c in range(2):
                    st.then(dve.bn_stats(bn[:, i, c], x[:, i, c * 512:(c + 1) * 512]))
            st.sync()
            st.then(dve.tensor_copy(nrd[:, 0, 0:1], bn[:, 0, 0, 0:1]))
            for i in range(NT):
                st.then(dve.bn_aggr(mean[:, i], bn[:, i].rearrange("p c k -> p (c k)")))
            st.sync()
            dve.tensor_scalar(rs, mean[:, :, 1], 1.0, EPS2, ALU.mult, ALU.add).then_inc(var_ok, 1)
            dve.wait_ge(pow_ok, l * POW2 + (POW1 + [1, 4, 5][n]))
            for i in range(NT):
                st.then(dve.tensor_scalar(x[:, i], x[:, i], mean[:, i, 0:1], rs[:, i:i + 1], ALU.subtract, ALU.mult))
            st.sync()
            dve.wait_ge(ln_in, (l * 3 + n + 1) * 16)
            st.link(dve.tensor_tensor(x[:], x[:], ln[:, 0].unsqueeze(1).to_broadcast([P, NT, D]), ALU.mult))
            dve.tensor_tensor(x[:], x[:], ln[:, 1].unsqueeze(1).to_broadcast([P, NT, D]), ALU.add).then_inc(x_ok, 1)

        CQ = D0 + 768

        def pe_layers(pe, tokens):
            with pe.Fori(0, LAYERS) as l:
                pe_ffn(pe, l, 0, tokens)
                tb = l * T2 + (T1 + 4)
                used = l * DENSE2 + DENSE1
                pe.wait_ge(x_ok, l * 3 + 4)
                pe_T(pe, tokens(x), tb)
                pe.wait_ge(t_out, tb + 4)
                for n, width in enumerate((D, D, W3)):
                    if n == 2:
                        pe.wait_ge(den_a, l * 3 + 7)
                        pe.wait_ge(den_v, l * 3 + 7)
                    pe_part(pe, xT, [dense_ready(l, c) for c in range(PART2[n], PART2[n + 1])], 0, n, d_land, d_used, width)
                pe.wait_ge(den_a, l * 3 + 8)
                pe.wait_ge(t_src, l * 2 + 5)
                pe_T(pe, [[proj2[:, i, CQ + b * P:CQ + (b + 1) * P] for i in range(NT)] for b in range(3)], tb + 4)
                pe.wait_ge(t_out, tb + 6)
                s, value = dense_ready(l, PART2[3])
                pe.wait_ge(d_land[s], value)
                pe.wait_ge(den_a, l * 3 + 9)
                for i in range(NT):
                    for k in range(2):
                        pe.matmul(bank[i][:, 0:BH * BQ], cT[:, k, tok(i)], slot[s][:, k * BH * BQ:(k + 1) * BH * BQ],
                                  start=(k == 0), stop=(k == 1))
                    ins = pe.matmul(bank[2 + i][:], cT[:, 2, tok(i)], slot[s][:, 2 * BH * BQ:2 * BH * BQ + 512],
                                    start=True, stop=True)
                ins.then_inc(d_used, 1)
                pe.wait_ge(rope_ok, l * 2 + 1)
                cols = [A0, A0 + P, A0 + 2 * P, C0, C0 + P, C0 + 2 * P, D0, D0 + P, D0 + 2 * P, D0 + 3 * P]
                pe_T(pe, [[proj2[:, i, c:c + P] for i in range(NT)] for c in cols], tb + 6)
                pe.wait_ge(t_out, tb + 11)
                pe.wait_ge(rope_ok, l * 2 + 2)
                pe_T(pe, [[m[:, i, h] for i in range(NT)] for m in (qm, km) for h in range(BH)], tb + 11, rows=BQ)
                pe.wait_ge(t_out, tb + 15)
                pe_units(pe, units2, lg2, l * UNITS2 + UNITS1, old=1)
                pe.wait_ge(t_src, l * 2 + 6)
                pe_T(pe, tokens(cat2), tb + 15)
                pe.wait_ge(t_out, tb + 19)
                pe_part(pe, xT, [dense_ready(l, c) for c in range(PART2[4], PART2[5])], 0, 0, d_land, d_used)
                pe_ffn(pe, l, 1, tokens)

        def act_layers(act, st):
            with act.Fori(0, LAYERS) as l:
                act.wait_ge(x_ok, l * 3 + 3)
                act.dma_start(row2[:], d_row2[l]).then_inc(row_in, 16)
                act.dma_start(colw2[:], d_cT2[l]).then_inc(row_in, 16)
                load_ln(act, l, 0)
                act_ffn(act, l, 0)
                act.wait_ge(x_ok, l * 3 + 4)
                act.dma_start(bias[:].rearrange("p h t s -> p (h t s)"), d_bias[1]).then_inc(bias_in, 16)
                used = l * DENSE2 + DENSE1
                for n, width in enumerate((D, D, W3)):
                    evac_act(act, n, used + PART2[n + 1], 0, proj2[:, 0, n * D:n * D + width], width)
                act.wait_ge(lam_in, l + 1)
                act.activation(lam2, lam2, ACT.Exp).then_inc(lam_ex, 1)
                act.wait_ge(d_used, used + PART2[4])
                for i in range(NT):
                    ins = act.activation(qm[:, i].rearrange("p h d -> p (h d)"), bank[i][:, 0:BH * BQ], ACT.Copy)
                ins.then_inc(c_a, 1)
                act_units(act, units2, lg2, l * UNITS2 + UNITS1, old=1)
                act.wait_ge(t_src, l * 2 + 6)
                load_ln(act, l, 1)
                act_ffn(act, l, 1)

        def dve_layers(dve, st):
            before_layers = st.n
            with dve.Fori(0, LAYERS) as l:
                st.base, st.n = l * DVE_PAD + before_layers, 0
                dve_ffn(dve, st, l, 0)
                tb = l * T2 + (T1 + 4)
                used = l * DENSE2 + DENSE1
                dve_T(dve, xT, KD, tb)
                st.link(dve.tensor_scalar(x[:], x[:], ALPHA, None, ALU.mult))
                dve.wait_ge(row_in, (l + 1) * 32)
                lp = row2[:, 388:516].rearrange("p (a b d) -> p a b d", a=2, b=2)
                prod = tmp2[:, 0:64].rearrange("p (a d) -> p a d", a=2)
                st.link(dve.tensor_tensor(prod, lp[:, :, 0], lp[:, :, 1], ALU.mult))
                dve.tensor_reduce(lam2, prod, X, ALU.add).then_inc(lam_in, 1)
                for n, width in enumerate((D, D, W3)):
                    evac_dve(dve, n, used + PART2[n + 1], proj2[:, 1, n * D:n * D + width], width)
                dve.wait_ge(lam_ex, l + 1)
                st.link(dve.tensor_tensor(nlam[:, 0:1], lam2[:, 1:2], lam2[:, 0:1], ALU.subtract))
                st.link(dve.tensor_tensor(nlam[:, 0:1], nlam[:, 0:1], row2[:, 516:517], ALU.subtract))
                dve.wait_ge(den_a, l * 3 + 9)
                dve.wait_ge(den_v, l * 3 + 9)
                for i in range(NT):
                    lat, ax = tmp2[:, 0:384], tmp2[:, 384:768]
                    st.then(dve.tensor_tensor(lat, proj2[:, i, CQ:CQ + 384], proj2[:, i, CQ:CQ + 384], ALU.mult))
                    st.link(dve.tensor_tensor(ax, proj2[:, i, C0:C0 + 384], proj2[:, i, C0:C0 + 384], ALU.mult))
                    st.then(dve.tensor_reduce(ssq[:, i, 0:1], lat[:, 0:QW], X, ALU.add))
                    st.then(dve.tensor_reduce(ssq[:, i, 1:2], lat[:, QW:384], X, ALU.add))
                    st.link(dve.tensor_reduce(ssq[:, i, 2:8], ax.rearrange("p (h d) -> p h d", h=6), X, ALU.add))
                for a, b, width in ((0, 1, QW), (1, 2, KVW), (2, 8, 64)):
                    ins = dve.tensor_scalar(rsq[:, :, a:b], ssq[:, :, a:b], 1.0 / width, EPS2, ALU.mult, ALU.add)
                    if a < 2:
                        st.then(ins)
                ins.then_inc(var_ok, 1)
                dve.wait_ge(pow_ok, l * POW2 + (POW1 + 2))
                for i in range(NT):
                    st.then(dve.tensor_scalar(proj2[:, i, CQ:CQ + QW], proj2[:, i, CQ:CQ + QW], rsq[:, i, 0:1], None, ALU.mult))
                    ins = dve.tensor_scalar(proj2[:, i, CQ + QW:CQ + 384], proj2[:, i, CQ + QW:CQ + 384],
                                            rsq[:, i, 1:2], None, ALU.mult)
                    if i < NT - 1:
                        st.then(ins)
                st.sync()
                ins.then_inc(t_src, 1)
                for i in range(NT):
                    ax = proj2[:, i, C0:C0 + 384].rearrange("p (h d) -> p h d", h=6)
                    st.then(dve.tensor_tensor(ax, ax, bc(rsq[:, i, 2:8], 64), ALU.mult))
                st.sync()
                for i in range(NT):
                    ins = dve.tensor_tensor(proj2[:, i, C0:C0 + 384], proj2[:, i, C0:C0 + 384], row2[:, 0:384], ALU.mult)
                    if i < NT - 1:
                        st.link(ins)
                ins.then_inc(ax_ok, 1)
                dve_T(dve, cT, 3, tb + 4, colw2[:, KD:KD + 3])
                dve.wait_ge(d_used, used + PART2[4])
                for i in range(NT):
                    kv = bank[2 + i][:].rearrange("p (h d) -> p h d", h=BH)
                    st.then(dve.tensor_copy(km[:, i, :, 0:64], kv[:, :, 0:64]))
                    ins = dve.tensor_copy(vm[:, i], kv[:, :, 64:128])
                    if i < NT - 1:
                        st.then(ins)
                ins.then_inc(kv_ok, 1)
                dve_T(dve, qkT2, 10, tb + 6)
                for j in range(0, 8, 2):
                    dve.wait_ge(t_ps, tb + (11 + j // 2 + 1))
                    dve.tensor_copy(qkT2[0:BQ, 10 + j:12 + j, :],
                                    bank[4 + j // 2][0:BQ].rearrange("p (b s) -> p b s", b=2)).then_inc(t_out, 1)
                dve.wait_ge(bias_in, l * 16 + 32)
                dve_units(dve, st, units2, lg2, l * UNITS2 + UNITS1, old=1)
                dve.wait_ge(o_ok, (l + 1) * UNITS2 + UNITS1)
                sq = tmp2[:, 0:512].rearrange("p (t d) -> p t d", t=NT)
                st.link(dve.tensor_tensor(sq, cat2[:, :, 768:1024], cat2[:, :, 768:1024], ALU.mult))
                st.link(dve.tensor_reduce(ssq[:, :, 0:4], sq.rearrange("p t (h d) -> p t h d", h=4), X, ALU.add))
                dve.tensor_scalar(rsq[:, :, 0:4], ssq[:, :, 0:4], 1.0 / 64, EPS2, ALU.mult, ALU.add).then_inc(var_ok, 1)
                dve.wait_ge(pow_ok, l * POW2 + (POW1 + 3))
                st.link(dve.tensor_scalar(rsq[:, :, 0:4], rsq[:, :, 0:4], row2[:, 517:518], None, ALU.mult))
                for i in range(NT):
                    od = cat2[:, i, 768:1024].rearrange("p (h d) -> p h d", h=4)
                    ins = dve.tensor_tensor(od, od, bc(rsq[:, i, 0:4], 64), ALU.mult)
                    if i < NT - 1:
                        st.link(ins)
                ins.then_inc(t_src, 1)
                dve_T(dve, xT, KD, tb + 15, colw2[:, 0:KD])
                dve.wait_ge(d_used, used + DENSE2)
                layer_norm(dve, st, l, 1, 1.0)
                dve_ffn(dve, st, l, 1)
                st.sync()
                st.pad(DVE_PAD)

        def pool_layers(pool, st):
            before_layers = st.n

            def rotate(x1, x2, cos, sin, y1, y2, t):
                st.then(pool.tensor_tensor(t[0], x1, cos, ALU.mult))
                st.then(pool.tensor_tensor(t[1], x2, sin, ALU.mult))
                st.then(pool.tensor_tensor(t[2], x1, sin, ALU.mult))
                st.link(pool.tensor_tensor(t[3], x2, cos, ALU.mult))
                st.then(pool.tensor_tensor(y1, t[0], t[1], ALU.subtract))
                return pool.tensor_tensor(y2, t[2], t[3], ALU.add)

            def scratch(at_c, shape):
                n = int(np.prod(shape))
                names = "abc"[:len(shape)]
                pattern = f"p ({' '.join(names)}) -> p {' '.join(names)}"
                return [tmp2[:, at_c + r * n:at_c + (r + 1) * n].rearrange(pattern, **dict(zip(names, shape)))
                        for r in range(4)]

            with pool.Fori(0, LAYERS) as l:
                st.base, st.n = l * POOL_PAD + before_layers, 0
                pool.wait_ge(var_ok, l * VAR2 + (VAR1 + 1))
                inverse_root(pool, rs)
                pool.wait_ge(var_ok, l * VAR2 + (VAR1 + 2))
                inverse_root(pool, rsq[:, :, 0:8])
                pool.wait_ge(ax_ok, l + 1)
                for i in range(NT):
                    v = proj2[:, i, C0:C0 + 384].rearrange("p (h a b d) -> p h a b d", h=6, a=2, b=2)
                    cos, sin = (rope[:, i, c:c + 32].rearrange("p (a d) -> p a d", a=2).unsqueeze(1)
                                .to_broadcast([P, 6, 2, 16]) for c in (32, 64))
                    ins = rotate(v[:, :, :, 0], v[:, :, :, 1], cos, sin, v[:, :, :, 0], v[:, :, :, 1],
                                 scratch(i * 768, (6, 2, 16)))
                    if i < NT - 1:
                        st.then(ins)
                ins.then_inc(rope_ok, 1)
                pool.wait_ge(rope_ok, l * 2 + 1)
                pool.wait_ge(c_a, l + 1)
                pool.wait_ge(kv_ok, l + 1)
                for i in range(NT):
                    q = qm[:, i, :, 64:96].rearrange("p h (b d) -> p h b d", b=2)
                    k = km[:, i, :, 64:96].rearrange("p h (b d) -> p h b d", b=2)
                    r = proj2[:, i, CQ + 384:CQ + 416].rearrange("p (b d) -> p b d", b=2)
                    cos, sin = (rope[:, i, c:c + 16].unsqueeze(1).to_broadcast([P, BH, 16]) for c in (0, 16))
                    r1, r2 = (r[:, b].unsqueeze(1).to_broadcast([P, BH, 16]) for b in range(2))
                    st.then(rotate(q[:, :, 0], q[:, :, 1], cos, sin, q[:, :, 0], q[:, :, 1], scratch(i * 512, (BH, 16))))
                    ins = rotate(r1, r2, cos, sin, k[:, :, 0], k[:, :, 1], scratch(i * 512 + 256, (BH, 16)))
                    if i < NT - 1:
                        st.then(ins)
                ins.then_inc(rope_ok, 1)
                pool.wait_ge(var_ok, l * VAR2 + (VAR1 + 3))
                inverse_root(pool, rsq[:, :, 0:4])
                for n in (4, 5):
                    pool.wait_ge(var_ok, l * VAR2 + (VAR1 + n))
                    inverse_root(pool, rs)
                st.sync()
                st.pad(POOL_PAD)

        @block.sync
        def _(sp):
            sp.dma_start(memt[:], d_mem.rearrange("(t p) d -> p t d", p=P)).then_inc(mem_in, 16)
            loads = [(x, d_x.rearrange("(t p) d -> p t d", p=P)), (colw, d_cT1), (row1, d_row1), (wr, d_wr)]
            at_c = 0
            for t in (ident, before, ones, iota, rel, desc, rope):
                n = int(np.prod(t.shape[1:]))
                dst = t[:] if len(t.shape) == 2 else t[:].rearrange(
                    {3: "p a b -> p (a b)", 4: "p a b c -> p (a b c)"}[len(t.shape)])
                loads.append((dst, d_tab[:, at_c:at_c + n]))
                at_c += n
            for dst, src in loads:
                sp.dma_start(dst[:] if not isinstance(dst, bass.AP) else dst, src).then_inc(consts_in, 16)
            for c in range(DENSE1):
                if c >= SLOTS:
                    sp.wait_ge(d_used, c - SLOTS + 1)
                sp.dma_start(slot[c % SLOTS], d_w1[c]).then_inc(d_land[c % SLOTS], 16)
                if c == 8:
                    sp.dma_start(bias[:], d_bias[0]).then_inc(bias_in, 16)
            def expert_chunk(turn, j):
                e, c = TEAM_CHUNKS[j]
                src = d_we[((turn % TEAMS) * TEAM + e) * 6 + c]
                sp.dma_start(slot[(e0 + j) % SLOTS], src).then_inc(e_land[(e0 + j) % SLOTS], 16)

            for j in range(SLOTS):
                sp.wait_ge(d_used, DENSE1 - SLOTS + j + 1)
                expert_chunk(0, j)
            last = load_turns(sp)
            with sp.Fori(0, last) as it:
                for j in range(SLOTS, 2 * SLOTS):
                    sp.wait_ge(e_used, it * 24 + (j - SLOTS + 1))
                    expert_chunk(it, j)
                for j in range(SLOTS):
                    sp.wait_ge(e_used, it * 24 + (j + SLOTS + 1))
                    expert_chunk(it + 1, j)
            for j in range(SLOTS, 2 * SLOTS):
                sp.wait_ge(e_used, last * 24 + (j - SLOTS + 1))
                expert_chunk(last, j)
            sp.wait_ge(e_used, last * 24 + 24)
            layer_loads(sp)
            sp.wait_ge(x_ok, 3 + 3 * LAYERS)
            sp.dma_start(d_out.rearrange("(t p) d -> p t d", p=P), x[:]).then_inc(out_done, 16)
            sp.wait_ge(out_done, 16)

        def pe_T(pe, srcs, base, rows=P, credit=0):
            for j in range(0, len(srcs), 2):
                n = j // 2
                if n >= 4:
                    pe.wait_ge(t_out, base + (n - 3))
                for b, src in enumerate(srcs[j:j + 2]):
                    for i in range(NT):
                        ins = pe.transpose(bank[4 + n % 4][0:rows, b * S + i * P:b * S + (i + 1) * P], src[i], ident[:])
                ins.then_inc(t_ps, 1)

        def pe_part(pe, lhs, chunks, n0, n, land, used, width=D):
            sel = 4 * (n % 2)
            k = 0
            for s, value in chunks:
                pe.wait_ge(land[s], value)
                per = KD // len(chunks)
                w = slot[s][:, 0:per * width].rearrange("p (k n) -> p k n", k=per)
                for kk in range(per):
                    for i in range(NT):
                        for c0 in range(0, width, 512):
                            c1 = min(c0 + 512, width)
                            ins = pe.matmul(bank[sel + 2 * i + c0 // 512][:, 0:c1 - c0], lhs[:, k, tok(i)],
                                            w[:, kk, c0:c1], start=(k == 0), stop=(k == KD - 1))
                    k += 1
                ins.then_inc(used, 1)

        def evac_act(act, n, base_used, copied, dst, width=D):
            act.wait_ge(d_used, base_used)
            sel = 4 * (n % 2)
            for c0 in range(0, width, 512):
                c1 = min(c0 + 512, width)
                ins = act.activation(dst[:, c0:c1], bank[sel + c0 // 512][:, 0:c1 - c0], ACT.Copy)
            ins.then_inc(den_a, 1)

        def evac_dve(dve, n, base_used, dst, width=D):
            dve.wait_ge(d_used, base_used)
            sel = 4 * (n % 2) + 2
            for c0 in range(0, width, 512):
                c1 = min(c0 + 512, width)
                ins = dve.tensor_copy(dst[:, c0:c1], bank[sel + c0 // 512][:, 0:c1 - c0])
            ins.then_inc(den_v, 1)

        def dve_T(dve, dst, nblocks, base, weights=None, rows=P):
            for j in range(0, nblocks, 2):
                b = min(2, nblocks - j)
                dve.wait_ge(t_ps, base + (j // 2 + 1))
                src = bank[4 + (j // 2) % 4][0:rows, 0:b * S].rearrange("p (b s) -> p b s", b=b)
                if weights is None:
                    ins = dve.tensor_copy(dst[0:rows, j:j + b, :], src)
                else:
                    ins = dve.tensor_tensor(dst[0:rows, j:j + b, :], src, bc(weights[0:rows, j:j + b], S), ALU.mult)
                ins.then_inc(t_out, 1)

        def pe_scores(pe, u, n, unit):
            pe.wait_ge(ex_ok, n - 1) if n is not None else None
            for i in range(NT):
                for b in range(len(unit.q)):
                    ins = pe.matmul(bank[u % 2][:, i * S:(i + 1) * S], unit.q[b][i], unit.k[b],
                                    start=(b == 0), stop=(b == len(unit.q) - 1))
            ins.then_inc(sc_ps, 1)

        def pe_probs_T(pe, u, n, lg):
            pe.wait_ge(ex_ok, n + 1)
            for t in range(NT):
                for i in range(NT):
                    ins = pe.transpose(bank[2 + u % 2][:, t * S + i * P:t * S + (i + 1) * P],
                                       lg[:, u % 2, i, t * P:(t + 1) * P], ident[:])
            ins.then_inc(pt_ps, 1)

        def pe_values(pe, u, n, unit):
            pe.wait_ge(pt_ok, n + 1)
            for i in range(NT):
                for t in range(NT):
                    ins = pe.matmul(bank[4 + u % 2][:, i * unit.dv:(i + 1) * unit.dv],
                                    pT_at[:, u % 2, t, tok(i)], unit.v[t], start=(t == 0), stop=(t == NT - 1))
            ins.then_inc(pv_ps, 1)

        def pe_units(pe, units, lg, n0, old=0, between=None):
            for u in range(len(units)):
                n = n0 + u
                if u == 0:
                    if old:
                        pe.wait_ge(ex_ok, n)
                    pe_scores(pe, u, None, units[u])
                if u + 1 < len(units):
                    if old or u >= 1:
                        pe.wait_ge(ex_ok, n)
                    pe_scores(pe, u + 1, None, units[u + 1])
                if between:
                    between(u)
                if old or u >= 2:
                    pe.wait_ge(pt_ok, n - 1)
                pe_probs_T(pe, u, n, lg)
                if old or u >= 2:
                    pe.wait_ge(o_ok, n - 1)
                pe_values(pe, u, n, units[u])

        def act_units(act, units, lg, n0, old=0, between=None):
            for u, unit in enumerate(units):
                n = n0 + u
                b = u % 2
                act.wait_ge(lg_ok, n + 1)
                if old or u >= 2:
                    act.wait_ge(o_ok, n - 1)
                    act.wait_ge(pt_ps, n - 1)
                for i in range(NT):
                    if unit.bias is None:
                        src, dst, scale = bank[b][:, i * S:(i + 1) * S], lg[:, b, i, 0:S], unit.scale
                    else:
                        w = S + (unit.sink is not None)
                        src = dst = lg[:, b, i, 0:w]
                        scale = 1.0
                    ins = act.activation(dst, src, ACT.Exp, bias=nmax[:, b, i:i + 1], scale=scale,
                                         accum_out=den[:, b, i:i + 1])
                ins.then_inc(ex_ok, 1)
                act.wait_ge(pt_ps, n + 1)
                if old or u >= 2:
                    act.wait_ge(pv_ps, n - 1)
                act.activation(pT_at[:, b].rearrange("p t s -> p (t s)"), bank[2 + b][:], ACT.Copy).then_inc(pt_ok, 1)
                if between:
                    between(u)

        def dve_logits(dve, st, u, n, unit, lg, old):
            b = u % 2
            dve.wait_ge(sc_ps, n + 1)
            if old or u >= 2:
                dve.wait_ge(ex_ok, n - 1)
                dve.wait_ge(pt_ps, n - 1)
            src = bank[b][:].rearrange("p (i s) -> p i s", i=NT)
            if unit.bias is None:
                st.link(dve.tensor_reduce(nmax[:, b], src, X, ALU.max, negate=True))
                dve.tensor_scalar(nmax[:, b], nmax[:, b], unit.scale, None, ALU.mult).then_inc(lg_ok, 1)
                return
            w = S + (unit.sink is not None)
            st.then(dve.scalar_tensor_tensor(lg[:, b, :, 0:S], src, unit.scale, unit.bias, ALU.mult, ALU.add))
            if unit.sink is not None:
                st.then(dve.tensor_copy(lg[:, b, :, S:w], unit.sink.unsqueeze(1).to_broadcast([P, NT, 1])))
            st.sync()
            dve.tensor_reduce(nmax[:, b], lg[:, b, :, 0:w], X, ALU.max, negate=True).then_inc(lg_ok, 1)

        def dve_output(dve, st, u, n, unit):
            b = u % 2
            dve.wait_ge(pv_ps, n + 1)
            st.link(dve.reciprocal(rden[:, b], den[:, b]))
            src = bank[4 + b][:, 0:NT * unit.dv].rearrange("p (i d) -> p i d", i=NT)
            if unit.half == 1:
                st.link(dve.tensor_scalar(nrd[:, b], rden[:, b], nlam[:, 0:1], None, ALU.mult))
                for i in range(NT):
                    ins = dve.scalar_tensor_tensor(unit.out[:, i], src[:, i], nrd[:, b, i:i + 1], unit.out[:, i],
                                                   ALU.mult, ALU.add)
                    if i < NT - 1:
                        st.then(ins)
            else:
                ins = dve.tensor_tensor(unit.out, src, bc(rden[:, b], unit.dv), ALU.mult)
            ins.then_inc(o_ok, 1)
            if unit.half == 0:
                dve.wait_ge(o_ok, n + 1)

        def dve_units(dve, st, units, lg, n0, old=0, between=None):
            dve_logits(dve, st, 0, n0, units[0], lg, old)
            for u in range(len(units)):
                if u + 1 < len(units):
                    dve_logits(dve, st, u + 1, n0 + u + 1, units[u + 1], lg, old)
                if between:
                    between(u)
                dve_output(dve, st, u, n0 + u, units[u])

        def ret_rows(h, blk):
            r = 64 * (h % 2)
            return qkT[r:r + 64, blk + h // 2, :]

        def pe_ret_scores(pe, h):
            if h >= 1:
                pe.wait_ge(rp_ok, h)
            for t in range(NT):
                ins = pe.matmul(bank[6][:, t * S:(t + 1) * S], ret_rows(h, 10)[:, tok(t)], ret_rows(h, 8),
                                start=True, stop=True)
            ins.then_inc(rs_ps, 1)

        def pe_ret_values(pe, h):
            pe.wait_ge(rp_ok, h + 1)
            if h >= 1:
                pe.wait_ge(ro_ok, h)
            c = 3 * AH * AD + 2 * RH * 64 + h * RV
            for i in range(NT):
                for t in range(NT):
                    ins = pe.matmul(bank[7][:, i * RV:(i + 1) * RV], dec[:, h % 2, t, tok(i)], proj[:, t, c:c + RV],
                                    start=(t == 0), stop=(t == NT - 1))
            ins.then_inc(rv_ps, 1)

        POW_NORM = [1, 2, 9, 11]
        POW1 = 11

        def power(pool, st, dst, src, scale, eps):
            st.link(pool.tensor_scalar(dst, src, scale, eps, ALU.mult, ALU.add))
            inverse_root(pool, dst)

        @block.gpsimd
        def _(pool):
            st = Steps(pool, pool_step)
            st.link(pool.memset(minus_half[:], -0.5))

            def rows(k):
                pool.wait_ge(sumsq, k + 1)
                power(pool, st, rs, ss, 1.0 / D, EPS1)

            def heads(k, n, width):
                pool.wait_ge(var_ok, k)
                power(pool, st, rsq[:, :, 0:n], ssq[:, :, 0:n], 1.0 / width, EPS1)

            rows(0)
            rows(1)
            heads(1, MH, MD)
            heads(2, 2 * AH, AD)
            for h in range(RH):
                pool.wait_ge(var_ok, 3 + h)
                power(pool, st, rs, mean[:, :, 1], 1.0, GN_EPS)
            rows(2)
            heads(7, MH, MD)
            rows(3)
            pool_layers(pool, st)

        @block.tensor
        def _(pe):
            pe.wait_ge(consts_in, 16 * N_CONST)
            pe.wait_ge(z_ok, 1)

            def tokens(t):
                return [[t[:, i, b * P:(b + 1) * P] for i in range(NT)] for b in range(KD)]

            pe.wait_ge(xn_ok, 1)
            pe_T(pe, tokens(memt), 0)
            pe.wait_ge(t_out, 4)
            pe_part(pe, memT, [(c % SLOTS, 16 * (c // SLOTS + 1)) for c in range(0, 4)], 0, 0, d_land, d_used)
            pe_part(pe, memT, [(c % SLOTS, 16 * (c // SLOTS + 1)) for c in range(4, 8)], 0, 1, d_land, d_used)
            pe.wait_ge(den_a, 2)
            pe.wait_ge(den_v, 2)
            pe.wait_ge(xn_ok, 2)
            pe_T(pe, tokens(xn), 4)
            pe.wait_ge(t_src, 1)
            pe.wait_ge(t_out, 8)
            pe_T(pe, tokens(mk), 8)
            for n in (2, 3, 4):
                if n == 3:
                    pe.wait_ge(t_out, 12)
                if n == 4:
                    pe.wait_ge(den_a, 3)
                    pe.wait_ge(den_v, 3)
                pe_part(pe, xT, [(c % SLOTS, 16 * (c // SLOTS + 1)) for c in range(PART1[n], PART1[n + 1])],
                        0, n, d_land, d_used)
            pe.wait_ge(den_a, 5)
            pe.wait_ge(t_src, 2)
            pe_T(pe, [[proj[:, i, c:c + P] for i in range(NT)]
                      for c in [*range(0, 1024, P), *range(1536, 2048, P)]], 12)
            pe.wait_ge(t_out, 18)
            pe_ret_scores(pe, 0)

            def between(u):
                if u < 2 * RH:
                    if u % 2 == 1:
                        pe_ret_values(pe, u // 2)
                    elif u > 0:
                        pe_ret_scores(pe, u // 2)

            pe.wait_ge(bias_in, 16)
            pe_units(pe, units1[:AH], lg1, 0, between=between)
            pe.wait_ge(t_src, 3)
            pe_T(pe, tokens(cat), 18)
            pe.wait_ge(t_out, 22)
            n = 5
            pe_part(pe, xT, [(c % SLOTS, 16 * (c // SLOTS + 1)) for c in range(PART1[n], PART1[n + 1])],
                    0, 4, d_land, d_used)
            pe.wait_ge(xn_ok, 3)
            pe_T(pe, tokens(xn), 22)
            pe.wait_ge(t_out, 26)
            n = 6
            pe_part(pe, xT, [(c % SLOTS, 16 * (c // SLOTS + 1)) for c in range(PART1[n], PART1[n + 1])],
                    0, 4, d_land, d_used)
            pe.wait_ge(t_src, 4)
            pe_T(pe, tokens(mq), 26)
            pe.wait_ge(t_out, 30)
            pe_units(pe, units1[AH:], lg1, AH, old=1)
            pe.wait_ge(o_ok, UNITS1)
            pe_T(pe, tokens(cat), 30)
            pe.wait_ge(t_out, 34)
            n = 7
            pe_part(pe, xT, [(c % SLOTS, 16 * (c // SLOTS + 1)) for c in range(PART1[n], PART1[n + 1])],
                    0, 4, d_land, d_used)
            pe_moe(pe, tokens)
            pe_layers(pe, tokens)

        @block.scalar
        def _(act):
            st = Steps(act, act_step)
            act.wait_ge(consts_in, 16 * N_CONST)

            def norm(k, src, dst):
                for i in range(NT):
                    ins = act.activation(tmp[:], src[:, i], ACT.Square, accum_out=ss[:, i:i + 1])
                    if i < NT - 1:
                        st.link(ins)
                ins.then_inc(sumsq, 1)
                act.wait_ge(pow_ok, POW_NORM[k])
                for i in range(NT):
                    ins = act.activation(dst[:, i], src[:, i], ACT.Copy, scale=rs[:, i:i + 1])
                ins.then_inc(xn_ok, 1)

            act.wait_ge(mem_in, 16)
            norm(0, memt, memt)
            norm(1, x, xn)
            act.wait_ge(t_ps, 4)
            evac_act(act, 0, PART1[1], 0, mk[:, 0])
            evac_act(act, 1, PART1[2], 0, mv[:, 0])
            act.wait_ge(t_ps, 8)
            for n in (2, 3, 4):
                evac_act(act, n, PART1[n + 1], 0, proj[:, 0, (n - 2) * D:(n - 1) * D])
            act.wait_ge(lgam, 1)
            act.activation(lt[:, 1], lt[:, 0], ACT.Exp).then_inc(lgam, 1)
            act.wait_ge(lgam, 3)
            act.activation(lt[:, 3], lt[:, 2], ACT.Ln).then_inc(lgam, 1)
            act.wait_ge(den_v, 5)
            act.wait_ge(den_a, 5)
            act.activation(proj[:, :, 2560:3072], proj[:, :, 2560:3072], ACT.Silu).then_inc(gate_ok, 1)

            def decay(h):
                act.wait_ge(rd_in, h + 1)
                act.activation(dec[:, h % 2], dec[:, h % 2], ACT.Exp).then_inc(rd_ok, 1)

            decay(0)

            def between(u):
                if u % 2 == 1 and u // 2 + 1 < RH:
                    decay(u // 2 + 1)

            act_units(act, units1[:AH], lg1, 0, between=between)
            act.wait_ge(x_ok, 1)
            norm(2, x, xn)
            evac_act(act, 0, PART1[7], 0, mq[:, 0])
            act_units(act, units1[AH:], lg1, AH, old=1)
            act.wait_ge(x_ok, 2)
            norm(3, x, xn)
            act_moe(act, st)
            act_layers(act, st)

        @block.vector
        def _(dve):
            st = Steps(dve, dve_step)
            dve.sem_inc(wl_ok, 2 * FT)
            dve.memset(zeros[:], 0.0).then_inc(z_ok, 1)

            def head_norm(k, src, heads, width, post):
                for i in range(NT):
                    t = tmp[:, 0:heads * width].rearrange("p (h w) -> p h w", h=heads)
                    st.link(dve.tensor_tensor(t, src[i], src[i], ALU.mult))
                    ins = dve.tensor_reduce(ssq[:, i, 0:heads], t, X, ALU.add)
                    if i < NT - 1:
                        st.link(ins)
                ins.then_inc(var_ok, 1)
                dve.wait_ge(pow_ok, k)
                for i in range(NT):
                    ins = dve.tensor_tensor(src[i], src[i], bc(rsq[:, i, 0:heads], width), ALU.mult)
                    if i < NT - 1:
                        st.link(ins)
                ins.then_inc(post, 1)

            def residual(n, base_used, post_value):
                dve.wait_ge(d_used, base_used)
                for i in range(NT):
                    for j in range(2):
                        ins = dve.tensor_tensor(x[:, i, j * 512:(j + 1) * 512], bank[4 * (n % 2) + 2 * i + j][:],
                                                x[:, i, j * 512:(j + 1) * 512], ALU.add)
                        if i + j < 2:
                            st.then(ins)
                st.sync()
                ins.then_inc(x_ok, 1)

            dve.wait_ge(consts_in, 16 * N_CONST)
            dve_T(dve, memT, KD, 0, colw[:, 0])
            dve.wait_ge(t_ps, 4)
            evac_dve(dve, 0, PART1[1], mk[:, 1])
            evac_dve(dve, 1, PART1[2], mv[:, 1])
            dve_T(dve, xT, KD, 4, colw[:, 1])
            dve.wait_ge(den_a, 1)
            dve.wait_ge(den_v, 1)
            head_norm(3, [mk[:, i].rearrange("p (h w) -> p h w", h=MH) for i in range(NT)], MH, MD, t_src)
            dve_T(dve, mkT, KD, 8, colw[:, 2])
            a = row1[:]
            st.link(dve.tensor_scalar(lt[:, 4], a, -1.0, None, ALU.mult))
            st.link(dve.tensor_tensor(lt[:, 0], a, lt[:, 4], ALU.max))
            dve.tensor_scalar(lt[:, 0], lt[:, 0], -1.0, None, ALU.mult).then_inc(lgam, 1)
            for n in (2, 3, 4):
                evac_dve(dve, n, PART1[n + 1], proj[:, 1, (n - 2) * D:(n - 1) * D])
            dve.wait_ge(den_a, 3)
            dve.wait_ge(den_v, 5)
            head_norm(4, [proj[:, i, 0:D].rearrange("p (h w) -> p h w", h=2 * AH) for i in range(NT)],
                      2 * AH, AD, t_src)
            dve_T(dve, qkT, 12, 12, colw[:, 3:5].rearrange("p a b -> p (a b)"))
            dve.wait_ge(lgam, 2)
            dve.tensor_scalar(lt[:, 2], lt[:, 1], 1.0, None, ALU.add).then_inc(lgam, 1)
            dve.wait_ge(lgam, 4)
            st.link(dve.tensor_scalar(lt[:, 4], lt[:, 4], 0.0, None, ALU.max))
            st.link(dve.tensor_tensor(lgm, lt[:, 3], lt[:, 4], ALU.add))
            st.link(dve.tensor_scalar(lgm, lgm, -1.0, None, ALU.mult))

            def exponents(h):
                if h >= 2:
                    dve.wait_ge(rv_ps, h - 1)
                st.link(dve.tensor_scalar(dec[:, h % 2], rel[:, 0], lgm[:, h:h + 1], None, ALU.mult))
                dve.scalar_tensor_tensor(dec[:, h % 2], rel[:, 1], lgm[:, RH + h:RH + h + 1], dec[:, h % 2],
                                         ALU.mult, ALU.add).then_inc(rd_in, 1)

            def decayed(h):
                dve.wait_ge(rd_ok, h + 1)
                dve.wait_ge(rs_ps, h + 1)
                dve.scalar_tensor_tensor(dec[:, h % 2], bank[6][:].rearrange("p (t s) -> p t s", t=NT), 64 ** -0.5,
                                         dec[:, h % 2], ALU.mult, ALU.mult).then_inc(rp_ok, 1)

            def ret_out(h):
                dve.wait_ge(rv_ps, h + 1)
                for i in range(NT):
                    st.then(dve.bn_stats(bn[:, i, 0, :], bank[7][:, i * RV:(i + 1) * RV]))
                st.sync()
                for i in range(NT):
                    ins = dve.bn_aggr(mean[:, i, :], bn[:, i, 0, :])
                    if i < NT - 1:
                        st.link(ins)
                ins.then_inc(var_ok, 1)
                dve.wait_ge(pow_ok, 5 + h)
                for i in range(NT):
                    ins = dve.tensor_scalar(cat[:, i, 512 + h * RV:512 + (h + 1) * RV], bank[7][:, i * RV:(i + 1) * RV],
                                            mean[:, i, 0:1], rs[:, i:i + 1], ALU.subtract, ALU.mult)
                    if i < NT - 1:
                        st.then(ins)
                ins.then_inc(ro_ok, 1)

            exponents(0)
            dve.wait_ge(bias_in, 16)

            def between(u):
                if u % 2 == 0:
                    decayed(u // 2)
                    if u // 2 + 1 < RH:
                        exponents(u // 2 + 1)
                else:
                    ret_out(u // 2)

            dve_units(dve, st, units1[:AH], lg1, 0, between=between)
            dve.wait_ge(gate_ok, 1)
            dve.wait_ge(ro_ok, RH)
            dve.wait_ge(o_ok, AH)
            dve.tensor_tensor(cat[:, :, 512:1024], cat[:, :, 512:1024], proj[:, :, 2560:3072], ALU.mult).then_inc(t_src, 1)
            dve_T(dve, xT, KD, 18, colw[:, 5])
            residual(0, PART1[6], 1)
            dve_T(dve, xT, KD, 22, colw[:, 6])
            evac_dve(dve, 0, PART1[7], mq[:, 1])
            dve.wait_ge(den_a, 6)
            dve.wait_ge(den_v, 6)
            head_norm(10, [mq[:, i].rearrange("p (h w) -> p h w", h=MH) for i in range(NT)], MH, MD, t_src)
            dve_T(dve, mqT, KD, 26, colw[:, 7])
            dve_units(dve, st, units1[AH:], lg1, AH, old=1)
            dve_T(dve, xT, KD, 30)
            residual(0, PART1[8], 2)
            dve_moe(dve, st)
            dve_layers(dve, st)


def lay_out(a):
    f32 = np.float32
    a = {k: np.asarray(v) for k, v in a.items()}

    def chunks(w, widths):
        out, c = [], 0
        for n in widths:
            per = CH // n if n == D else KD
            part = w[:, c:c + n].reshape(KD // per, per, P, n).transpose(0, 2, 1, 3).reshape(KD // per, P, per * n)
            if part.shape[2] < CH:
                part = np.concatenate([part, np.zeros((part.shape[0], P, CH - part.shape[2]), w.dtype)], 2)
            out.append(part)
            c += n
        return np.concatenate(out)

    w1 = np.concatenate([chunks(a["w_mkv"][0], [D, D]), chunks(a["w_in"][0], [D] * 3), chunks(a["w_out"][0], [D]),
                         chunks(a["w_mq"][0], [D]), chunks(a["w_mo"][0], [D])])
    gate = a["w_exp_gate"][0].reshape(NE, 4, 2, P, 4, P)
    up = a["w_exp_up"][0].reshape(NE, 4, 2, P, 4, P)
    gu = np.stack([gate, up], 5).transpose(0, 1, 3, 2, 4, 5, 6).reshape(NE, 4, P, CH)
    down = a["w_exp_down"][0].reshape(NE, 2, 2, P, D).transpose(0, 1, 3, 2, 4).reshape(NE, 2, P, CH)
    we = np.concatenate([gu, down], 1).reshape(NE * 6, P, CH)
    g = a["ffn_w_gu_2"].reshape(LAYERS, 2, KD, P, 2, FT, P).transpose(0, 1, 5, 3, 2, 4, 6).reshape(LAYERS * 2, FT, P, 2 * D)
    dn = a["ffn_w_down_2"].reshape(LAYERS * 2, FT, P, D)
    wf = np.concatenate([g, dn], 3).reshape(LAYERS * 2 * FT, P, FTW)
    heads = np.array([0, 2, 1, 3])
    q64 = (heads[:, None] * 64 + np.arange(64)).ravel()
    oa, ob, oc, od = 0, 512, 512 + 416, 512 + 416 + 512
    cols = np.concatenate([oa + q64, oa + np.arange(256, 512), oc + q64, oc + np.arange(256, 512),
                           od + np.arange(768), ob + np.arange(416)])
    w2 = []
    for l in range(LAYERS):
        dense = chunks(a["w_in_2"][l][:, cols], [D, D, W3])
        mla = np.concatenate([a["mla_w_uq_2"][l].reshape(2, P, 384).transpose(1, 0, 2).reshape(P, 768),
                              a["mla_w_ukv_2"][l]], 1)
        mla = np.concatenate([mla, np.zeros((P, CH - mla.shape[1]), f32)], 1)[None]
        w2.append(np.concatenate([dense, mla, chunks(a["w_out_2"][l], [D])]))
    w2 = np.concatenate(w2)

    def col(v):
        return v.reshape(-1, P).T

    def rep(v, n):
        return np.tile(v, (n,) + (1,) * (v.ndim - 1))

    one = np.ones((P, 1), f32)
    aq, ak = (np.concatenate([a[n][0]] * 2)[:, None] for n in ("attn_q_norm_w", "attn_k_norm_w"))
    cT1 = np.concatenate([
        col(a["norm_memkv_w"][0]), col(a["norm_mix_w"][0]), np.tile(col(a["mem_k_norm_w"][0]), (1, 4)),
        np.tile(aq, (1, 4)), np.tile(ak, (1, 4)), np.tile(one, (1, 8)),
        np.tile(one, (1, 4)), col(a["ret_gn_w"][0]),
        col(a["norm_mem_w"][0]), np.tile(col(a["mem_q_norm_w"][0]), (1, 4)), col(a["norm_moe_w"][0])], 1)
    row1 = np.tile(np.concatenate([a["ret_decay_f"][0], a["ret_decay_b"][0]])[None], (P, 1))
    router = np.concatenate([a["w_group"][0], a["w_router"][0].transpose(1, 0, 2).reshape(D, NE)], 1)
    wr = router.reshape(KD, P, NG + NE).transpose(1, 0, 2).reshape(P, -1)
    cT2, row2 = [], []
    for l in range(LAYERS):
        sub = np.concatenate([a["diff_subln_2"][l]] * 2)[:, None]
        cT2.append(np.concatenate([np.tile(one, (1, 6)), np.tile(sub, (1, 2)), col(a["mla_q_norm_2"][l]),
                                   col(a["mla_kv_norm_2"][l])], 1))
        init = 0.8 - 0.6 * np.exp(-0.3 * l)
        row2.append(np.tile(np.concatenate([np.tile(a["ax_q_norm_2"][l], 4), np.tile(a["ax_k_norm_2"][l], 2),
                                            a["win_sink_2"][l], a["diff_lambda_2"][l].ravel(),
                                            np.array([init, 1 - init], f32)])[None], (P, 1)))
    lnp = np.stack([a["ln_g_2"], a["ln_b_2"]], 2).reshape(LAYERS * 3, 1, 2 * D)
    ln = np.broadcast_to(lnp, (LAYERS * 3, P, 2 * D))
    t = np.arange(S)
    dist = np.abs(t[:, None] - t[None, :]).astype(f32)

    def tiled(m):
        return m.reshape(NT, P, -1).transpose(1, 0, 2).reshape(P, -1)

    diff = (t[None, :] - t[:, None]).astype(f32)
    inv16 = 10000.0 ** (-np.arange(0, 32, 2) / 32)
    ang = t[:, None] * inv16
    row_a, col_a = (t // 64)[:, None] * inv16, (t % 64)[:, None] * inv16
    tab_rope = np.concatenate([np.cos(ang), np.sin(ang), np.cos(row_a), np.cos(col_a), np.sin(row_a), np.sin(col_a)], 1)
    tab = np.concatenate([
        np.eye(P), (np.arange(P)[:, None] < np.arange(P)[None, :]), np.ones((P, P)), np.tile(t[None], (P, 1)),
        tiled(np.maximum(diff, 0)), tiled(np.maximum(-diff, 0)),
        np.tile(np.concatenate([NG - np.arange(NG), NE - np.arange(NE)])[None], (P, 1)), tiled(tab_rope)], 1).astype(f32)
    slopes = 2.0 ** -(np.arange(8) + 1.0)
    times = (dist <= 64).astype(int) + (dist % 4 == 0) + (dist % 16 == 0)
    log_times = np.where(times > 0, np.log(np.maximum(times, 1)), NEG)
    window = np.where(dist <= 128, 0.0, NEG)
    b1 = np.stack([tiled(-s * dist + log_times) for s in slopes], 1)
    b2 = np.stack([tiled(-s * dist + (window if i < 4 else 0.0)) for i, s in enumerate(slopes)], 1)
    biases = np.stack([b1, b2]).reshape(2, P, -1).astype(f32)
    return dict(x=a["x"][0], mem=a["mem"][0], w1=w1, we=we, wf=wf, w2=w2, cT1=cT1, row1=row1, wr=wr,
                cT2=np.stack(cT2), row2=np.stack(row2), ln=ln, tab=tab, bias=biases)


ORDER = ["x", "mem", "w1", "we", "wf", "w2", "cT1", "row1", "wr", "cT2", "row2", "ln", "tab", "bias"]


def kernel(**inputs):
    import concourse.bacc as bacc
    from concourse.bass_utils import run_bass_kernel_spmd

    arrays = {f"in_{k}": np.ascontiguousarray(v) for k, v in lay_out(inputs).items()}
    nc = bacc.Bacc("TRN2", target_bir_lowering=False, num_devices=1)
    args = [nc.dram_tensor(f"in_{k}", arrays[f"in_{k}"].shape, mybir.dt.from_np(arrays[f"in_{k}"].dtype),
                           kind="ExternalInput").ap() for k in ORDER]
    out = nc.dram_tensor("out_x", (S, D), F32, kind="ExternalOutput").ap()
    build(nc, *args, out)
    r = run_bass_kernel_spmd(nc, [arrays], core_ids=[0])
    return r.results[0]["out_x"].reshape(1, S, D)
```

```python
from contextlib import ExitStack

import numpy as np

import concourse.bass as bass
from concourse import mybir

F32 = mybir.dt.float32
F32R = mybir.dt.float32r
I32 = mybir.dt.int32
ALU = mybir.AluOpType
ACT = mybir.ActivationFunctionType
X = mybir.AxisListType.X

P = 128
S = 256
NT = S // P
D = 1024
KD = D // P
CH = 2048
SLOTS = 12
ESLOTS = 16
SLOTS1 = 10
AH, AD = 8, 64
RH, RV = 4, 128
MH, MD = 4, 256
PROJ1 = 3 * AH * AD + 2 * RH * 64 + 2 * RH * RV
NE, EG, NG = 32, 8, 4
CAP = 32
TEAM = P // CAP
TEAMS = NE // TEAM
EPS1, EPS2, GN_EPS = 1e-6, 1e-5, 1e-5
NEG = -1e30
LAYERS = 2
DFF = 2816
FT = DFF // P
FTW = 3 * D
FSLOTS = SLOTS * CH // FTW
ALPHA = (2 * LAYERS) ** 0.25
PROJ2 = 2208
W3 = PROJ2 - 2 * D
B0, C0, A0, D0 = 0, 416, 928, 1440
QW, KVW, ROPE = 256, 128, 32
BH, BQ = 4, 96
N_CONST = 9
LROW = 384 + 4 + 128 + 2
DENSE1, DENSE2 = 32, 14
UNITS1, UNITS2 = 12, 20
T1, T2 = 38, 27
TEAM_ORDER = [(0, "u"), (1, "u"), (0, "d"), (2, "u"), (1, "d"), (3, "u"), (2, "d"), (3, "d")]
TURN = 6 * TEAM
TEAM_CHUNKS = [(e, c) for e, part in TEAM_ORDER for c in (range(4) if part == "u" else range(4, 6))]


def bc(ap, n):
    return ap.unsqueeze(len(ap.shape)).to_broadcast(list(ap.shape) + [n])


class Steps:

    def __init__(self, eng, sem):
        self.eng, self.sem, self.n, self.base = eng, sem, 0, 0

    def then(self, ins):
        ins.then_inc(self.sem, 1)
        self.n += 1
        return ins

    def sync(self):
        self.eng.wait_ge(self.sem, self.base + self.n)

    def link(self, ins):
        self.then(ins)
        self.sync()

    def pad(self, to):
        assert self.n <= to, self.n
        self.eng.sem_inc(self.sem, to - self.n)


def build(nc, d_x, d_mem, d_w1, d_we, d_wf, d_w2, d_cT1, d_row1, d_wr, d_cT2, d_row2, d_ln, d_tab, d_bias, d_out):
    ctx = ExitStack()
    with ctx:
        here = [16640]

        def at(name, offset, shape, dt=F32):
            return nc.alloc_sbuf_tensor_at(name, shape, dt, offset=offset)

        def sb(name, shape, dt=F32):
            size = int(np.prod(shape[1:])) * 4
            offset = here[0]
            here[0] += -(-size // 32) * 32
            return at(name, offset, shape, dt)

        ring = sb("ring", [P, SLOTS * CH])
        x = sb("x", [P, NT, D])
        xT_at = here[0]
        xT = sb("xT", [P, KD, S])
        bias_at = here[0]
        bias = sb("bias", [P, 8, NT, S])
        ident = sb("ident", [P, P])
        before = sb("before", [P, P])
        ones = sb("ones", [P, P])
        iota = sb("iota", [P, S])
        rel = sb("rel", [P, 2, NT, S])
        desc = sb("desc", [P, NG + NE])
        rope = sb("rope", [P, NT, 96])
        colw = sb("colw", [P, 9, KD])
        row1 = sb("row1", [P, 8])
        wr = sb("wr", [P, KD, NG + NE])
        colw2 = sb("colw2", [P, KD + 3])
        row2 = sb("row2", [P, LROW])
        small = sb("small", [P, 256])
        zeros = sb("zeros", [P, 512], mybir.dt.bfloat16)
        minus_half = sb("minus_half", [P, 8])
        last_turn = sb("last_turn", [P, 1], I32)
        last_pair_at = sb("last_pair_at", [P, 1], I32)
        work = here[0]
        assert work + 59680 + 6144 <= nc.sbuf_usable_end, (work, nc.sbuf_usable_end)
        slot = [ring[:, s * CH:(s + 1) * CH] for s in range(SLOTS)]
        slot += [at(f"more{i}", offset, [P, CH])[:]
                 for i, offset in enumerate((bias_at, bias_at + 4 * CH, work + 32768, work + 32768 + 4 * CH))]
        ring_r = at("ring_r", 16640, [P, SLOTS * CH], F32R)
        slot_r = [ring_r[:, s * CH:(s + 1) * CH] for s in range(SLOTS)]
        xTh = at("xTh", xT_at, [P, KD, S], F32R)
        xTl1 = at("xTl1", work + 24576, [P, KD, S], F32R)
        xTl2 = at("xTl2", work + 25856, [P, KD, S], F32R)
        high2 = [at("high2_0", work + 36096, [P, CH], F32R)[:], at("high2_1", work + 17664, [P, CH], F32R)[:]]
        proj = at("proj", work, [P, NT, PROJ1])
        xn = at("xn", work, [P, NT, D])
        mq = at("mq", work + 8192, [P, NT, D])
        qkT = at("qkT", work + 24576, [P, 12, S])
        mqT = at("mqT", work + 24576, [P, KD, S])
        mkT = at("mkT", work + 36864, [P, KD, S])
        mv = at("mv", work + 45056, [P, NT, D])
        cat = at("cat", work + 53248, [P, NT, D])
        memt = at("memt", work + 53248, [P, NT, D])
        mk = at("mk", work + 53248, [P, NT, D])
        tmp = at("tmp", work + 61440, [P, D])
        dec = xT[:, 0:4, :].rearrange("p (b t) s -> p b t s", b=2)
        pT_at = xT[:, 4:8, :].rearrange("p (b t) s -> p b t s", b=2)
        xg = at("xg", work + 8192, [P, KD, P])
        yg = at("yg", work + 12288, [P, D])
        oh = at("oh", work + 16384, [P, NT, TEAM, CAP])
        ohg = at("ohg", work + 17408, [P, NT, TEAM, CAP])
        sT = at("sT", work + 18432, [P, S])
        hmid = at("hmid", work + 19456, [P, 2, P])
        hact = at("hact", work + 20480, [P, 2, P])
        hTe = at("hTe", work + 21504, [P, 2, P])
        route = at("route", work + 22528, [P, 5, NT, NE])
        chosen = at("chosen", work + 24576, [P, NT, NE])[:]
        gates = at("gates", work + 24832, [P, NT, NE])[:]
        ranks = at("ranks", work + 25088, [P, NT, NE])[:]
        wh = [at(f"wh{i}", work + i * 4 * FTW, [P, FTW], F32R) for i in range(2)]
        wl = [at(f"wl{i}", work + (2 + i) * 4 * FTW, [P, FTW], F32R) for i in range(2)]
        xh = at("xh", work + 16 * FTW, [P, KD, S], F32R)
        xl = at("xl", work + 16 * FTW + 8192, [P, KD, S], F32R)
        hh = [at(f"hh{i}", bias_at + i * 1024, [P, S], F32R) for i in range(2)]
        hl = [at(f"hl{i}", bias_at + 2048 + i * 1024, [P, S], F32R) for i in range(2)]
        sg = at("sg", bias_at + 4096, [P, 2, S])
        hf = at("hf", bias_at + 6144, [P, 2, S])
        ln = at("ln", bias_at + 8192, [P, 2, D])
        proj2 = at("proj2", work, [P, NT, PROJ2])
        qkT2 = at("qkT2", work + 17664, [P, 18, S])
        cT = at("cT", work + 36096, [P, 3, S])
        qm = at("qm", work + 39168, [P, NT, BH, BQ])
        km = at("km", work + 42240, [P, NT, BH, BQ])
        vm = at("vm", work + 45312, [P, NT, BH, 64])
        cat2 = at("cat2", work + 47360, [P, NT, D])
        lg2 = at("lg2", work + 55552, [P, 2, NT, S + 1])
        tmp2 = at("tmp2", work + 59680, [P, 1536])
        lg1 = at("lg1", work + 61440, [P, 2, NT, S])

        bank = [ctx.enter_context(nc.psum_tensor(f"bank{i}", [P, 512], F32)) for i in range(8)]

        def sem(name):
            return ctx.enter_context(nc.semaphore(name))

        first_in = sem("first_in")
        consts_in = sem("consts_in")
        mem_in = sem("mem_in")
        bias_in = sem("bias_in")
        ln_in = sem("ln_in")
        row_in = sem("row_in")
        d_land = [sem(f"d_land{i}") for i in range(SLOTS)]
        e_land = [sem(f"e_land{i}") for i in range(ESLOTS)]
        dh_ok = sem("dh_ok")
        dlv_ok = sem("dlv_ok")
        dlp_ok = sem("dlp_ok")
        th_ok = sem("th_ok")
        f_land = [sem(f"f_land{i}") for i in range(2)]
        out_done = sem("out_done")
        d_used = sem("d_used")
        e_used = sem("e_used")
        dve_step = sem("dve_step")
        act_step = sem("act_step")
        sumsq = sem("sumsq")
        var_ok = sem("var_ok")
        pow_ok = sem("pow_ok")
        pool_step = sem("pool_step")
        xn_ok = sem("xn_ok")
        t_src = sem("t_src")
        t_ps = sem("t_ps")
        t_out = sem("t_out")
        den_a = sem("den_a")
        den_v = sem("den_v")
        sc_ps = sem("sc_ps")
        lg_ok = sem("lg_ok")
        ex_ok = sem("ex_ok")
        pt_ps = sem("pt_ps")
        pt_ok = sem("pt_ok")
        pv_ps = sem("pv_ps")
        o_ok = sem("o_ok")
        rs_ps = sem("rs_ps")
        rd_in = sem("rd_in")
        rd_ok = sem("rd_ok")
        rp_ok = sem("rp_ok")
        rv_ps = sem("rv_ps")
        ro_ok = sem("ro_ok")
        lgam = sem("lgam")
        gate_ok = sem("gate_ok")
        r_ps = sem("r_ps")
        r_ok = sem("r_ok")
        r_ex = sem("r_ex")
        n_ok = sem("n_ok")
        m_oh = sem("m_oh")
        m_ga = sem("m_ga")
        m_xg = sem("m_xg")
        m_st = sem("m_st")
        m_sT = sem("m_sT")
        m_sg = sem("m_sg")
        m_h = sem("m_h")
        m_hp = sem("m_hp")
        m_hT = sem("m_hT")
        m_yA = sem("m_yA")
        m_yV = sem("m_yV")
        m_sc = sem("m_sc")
        x_ok = sem("x_ok")
        x0_ok = sem("x0_ok")
        half_ok = sem("half_ok")
        fhalf_ok = sem("fhalf_ok")
        xn1_ok = sem("xn1_ok")
        sq_a = sem("sq_a")
        mq_a = sem("mq_a")
        xh_ok = sem("xh_ok")
        wh_ok = sem("wh_ok")
        wl_ok = sem("wl_ok")
        f_gu = sem("f_gu")
        f_sg = sem("f_sg")
        f_h = sem("f_h")
        f_dn = sem("f_dn")
        c_a = sem("c_a")
        lam_in = sem("lam_in")
        lam_ex = sem("lam_ex")

        block = ctx.enter_context(nc.Block())

        dve_loop = sem("dve_loop")
        rope_ok = sem("rope_ok")
        ax_ok = sem("ax_ok")
        kv_ok = sem("kv_ok")
        f_hv = sem("f_hv")
        z_ok = sem("z_ok")

        ss, rs = small[:, 0:2], small[:, 4:6]
        ssq = small[:, 8:40].rearrange("p (t h) -> p t h", t=NT)
        rsq = small[:, 40:72].rearrange("p (t h) -> p t h", t=NT)
        nmax = small[:, 72:76].rearrange("p (b t) -> p b t", b=2)
        den = small[:, 76:80].rearrange("p (b t) -> p b t", b=2)
        rden = small[:, 80:84].rearrange("p (b t) -> p b t", b=2)
        lgm = small[:, 84:92]
        lt = small[:, 92:132].rearrange("p (a h) -> p a h", h=8)
        bn = small[:, 132:156].rearrange("p (t c k) -> p t c k", t=NT, c=2)
        mean = small[:, 156:160].rearrange("p (t k) -> p t k", t=NT)
        lam2 = small[:, 160:162]
        nlam = small[:, 162:164]
        nrd = small[:, 164:168].rearrange("p (b t) -> p b t", b=2)
        gs = small[:, 168:232]

        def tok(i):
            return slice(i * P, (i + 1) * P)

        class Unit:

            def __init__(self, q, k, v, scale, out, bias=None, sink=None, half=None):
                self.q, self.k, self.v, self.scale, self.out = q, k, v, scale, out
                self.bias, self.sink, self.half = bias, sink, half
                self.dv = v[0].shape[-1]

        def head_rows(T, blk, first, n):
            return [T[first:first + n, blk, tok(i)] for i in range(NT)], T[first:first + n, blk, :]

        units1 = []
        for h in range(AH):
            rows = 64 * (h % 2)
            q, _ = head_rows(qkT, h // 2, rows, 64)
            _, k = head_rows(qkT, 4 + h // 2, rows, 64)
            c = 2 * AH * AD + h * AD
            units1.append(Unit([q], [k], [proj[:, t, c:c + AD] for t in range(NT)], AD ** -0.5,
                               cat[:, :, h * AD:(h + 1) * AD], bias=bias[:, h]))
        for h in range(MH):
            qs = [head_rows(mqT, 2 * h + b, 0, P)[0] for b in range(2)]
            ks = [head_rows(mkT, 2 * h + b, 0, P)[1] for b in range(2)]
            units1.append(Unit(qs, ks, [mv[:, t, h * MD:(h + 1) * MD] for t in range(NT)], MD ** -0.5,
                               cat[:, :, h * MD:(h + 1) * MD]))
        units2 = []
        for h in range(4):
            at_q, kv = [0, 2, 1, 3][h], h // 2
            q, _ = head_rows(qkT2, at_q // 2, 64 * (at_q % 2), 64)
            _, k = head_rows(qkT2, 2, 64 * kv, 64)
            c = A0 + 384 + 64 * kv
            units2.append(Unit([q], [k], [proj2[:, t, c:c + 64] for t in range(NT)], 64 ** -0.5,
                               cat2[:, :, h * 64:(h + 1) * 64], bias=bias[:, h], sink=row2[:, 384 + h:385 + h]))
        for n in range(8):
            h, m = n // 2, n % 2
            q, _ = head_rows(qkT2, 6 + n // 4, 32 * (n % 4), 32)
            _, k = head_rows(qkT2, 8 + n // 4, 32 * (n % 4), 32)
            c = D0 + 512 + 64 * h
            units2.append(Unit([q], [k], [proj2[:, t, c:c + 64] for t in range(NT)], 32 ** -0.5,
                               cat2[:, :, 768 + h * 64:768 + (h + 1) * 64], bias=bias[:, 4 + h], half=m))
        for h in range(4):
            at_q, kv = [0, 2, 1, 3][h], h // 2
            q, _ = head_rows(qkT2, 3 + at_q // 2, 64 * (at_q % 2), 64)
            _, k = head_rows(qkT2, 5, 64 * kv, 64)
            c = C0 + 384 + 64 * kv
            units2.append(Unit([q], [k], [proj2[:, t, c:c + 64] for t in range(NT)], 64 ** -0.5,
                               cat2[:, :, 512 + h * 64:512 + (h + 1) * 64]))
        for h in range(BH):
            q, _ = head_rows(qkT2, 10 + h, 0, BQ)
            _, k = head_rows(qkT2, 14 + h, 0, BQ)
            units2.append(Unit([q], [k], [vm[:, t, h, :] for t in range(NT)], BQ ** -0.5,
                               cat2[:, :, 256 + h * 64:256 + (h + 1) * 64]))

        order = [0, 1, 2, 3, 12, 13, *sum([[4 + 2 * n, 5 + 2 * n, 16 + n] for n in range(4)], []), 14, 15]
        units2 = [units2[n] for n in order]
        DIFF_DONE = order.index(11) + 1

        PART1 = [0, 4, 8, 12, 16, 20, 24, 28, 32]
        PART2 = [0, 4, 8, 9, 10, 14]
        X01 = 2

        def tiles_in(s):
            return range(s * CH // FTW, ((s + 1) * CH - 1) // FTW + 1)

        def chunks_in(v):
            return range(v * FTW // CH, ((v + 1) * FTW - 1) // CH + 1)

        last_tile = {v % FSLOTS: v for v in range(FT)}
        D_AT = 9
        e_slot = [(DENSE1 + j) % SLOTS1 for j in range(SLOTS1)]
        e_slot = e_slot[:6] + list(range(SLOTS, ESLOTS)) + e_slot[6:] + list(range(SLOTS1, SLOTS))
        dense_slot = [(D_AT + c) % SLOTS for c in range(DENSE2)]
        last_dense = {s: c for c, s in enumerate(dense_slot)}

        class Run:

            def __init__(self, slots, lands, parts, highs, used, high, low_v, low_p, t, th):
                self.slots, self.lands, self.parts, self.highs = slots, lands, parts, highs
                self.used, self.high, self.low_v, self.low_p, self.t, self.th = used, high, low_v, low_p, t, th

            def width(self, c):
                return next(w for e, w in self.parts if c < e) * (KD if self.short(c) else 2)

            def short(self, c):
                return next(w for e, w in self.parts if c < e) < D

        def run1(r):
            first = [0, 8, 20, 24, 28]
            ends = [[4, 8], [4, 8, 12], [4], [4], [4]][r]
            chunks = range(first[r], first[r] + ends[-1])
            return Run([c % SLOTS1 for c in chunks], [16 * (c // SLOTS1 + 1) for c in chunks], [(e, D) for e in ends],
                       [slot_r[SLOTS1][:], slot_r[SLOTS1 + 1][:]], first[r], first[r], first[r] - 2 * r, 2 * r,
                       [0, 4, 18, 22, 30][r], 4 * r)

        runs1 = [run1(r) for r in range(5)]

        def run2(l, r):
            chunks = [range(0, PART2[3]), range(PART2[4], DENSE2)][r]
            land = [dense_ready(l, c) for c in chunks]
            done = l * (DENSE2 - 1) + DENSE1 + r * PART2[3]
            low_v = l * (DENSE2 - 5) + (DENSE1 - 10 + r * (PART2[3] - 2))
            return Run([s for s, _ in land], [v for _, v in land], [[(4, D), (8, D), (9, W3)], [(4, D)]][r], high2,
                       l * DENSE2 + (DENSE1 + chunks[0]), done, low_v, l * 4 + (10 + 2 * r),
                       l * T2 + (T1 + [4, 19][r]), l * 8 + (20 + 4 * r))

        def act_high(act, run, c):
            act.wait_ge(d_land[run.slots[c]], run.lands[c])
            if c >= 2:
                act.wait_ge(d_used, run.used + (c - 1))
            elif run is not runs1[0]:
                act.wait_ge(d_used, run.used)
            n = run.width(c)
            act.activation(run.highs[c % 2][:, 0:n], slot[run.slots[c]][:, 0:n], ACT.Copy).then_inc(dh_ok, 1)

        def low(eng, run, c):
            eng.wait_ge(dh_ok, run.high + (c + 1))
            n, s = run.width(c), run.slots[c]
            eng.tensor_tensor(slot_r[s][:, 0:n], slot[s][:, 0:n], run.highs[c % 2][:, 0:n].bitcast(F32),
                              ALU.subtract).then_inc(dlp_ok if c < 2 else dlv_ok, 1)

        def act_high_T(act, run, weights=None):
            for j in range(4):
                act.wait_ge(t_ps, run.t + (j + 1))
                if weights is None:
                    ins = act.activation(xTh[:, 2 * j:2 * j + 2].rearrange("p k s -> p (k s)"), bank[4 + j][:], ACT.Copy)
                else:
                    for b in range(2):
                        k = 2 * j + b
                        ins = act.activation(xTh[:, k], bank[4 + j][:, b * S:(b + 1) * S], ACT.Copy,
                                             scale=weights[:, k:k + 1])
                ins.then_inc(th_ok, 1)

        def dve_low_T(dve, run, dst, weights=None):
            for j in range(4):
                dve.wait_ge(th_ok, run.th + (j + 1))
                if weights is None:
                    ins = dve.tensor_tensor(dst[:, 2 * j:2 * j + 2].rearrange("p k s -> p (k s)"), bank[4 + j][:],
                                            xTh[:, 2 * j:2 * j + 2].rearrange("p k s -> p (k s)").bitcast(F32), ALU.subtract)
                else:
                    for b in range(2):
                        k = 2 * j + b
                        ins = dve.scalar_tensor_tensor(dst[:, k], bank[4 + j][:, b * S:(b + 1) * S], weights[:, k:k + 1],
                                                       xTh[:, k].bitcast(F32), ALU.mult, ALU.subtract)
                ins.then_inc(t_out, 1)

        def stream(step, run, first, evacs):
            ends = [e for e, _ in run.parts]
            for c in range(first, ends[-1]):
                step(c)
                if c in ends:
                    evacs[ends.index(c)]()
            evacs[-1]()

        def inverse_root(pool, dst):
            half = minus_half[:, 0:1]
            for _ in range(len(dst.shape) - 2):
                half = half.unsqueeze(1)
            pool.tensor_tensor(dst, dst, half.to_broadcast(list(dst.shape)), ALU.pow).then_inc(pow_ok, 1)

        LAST = {}
        for n_c, (e, c) in enumerate(TEAM_CHUNKS):
            LAST[e, "u" if c < 4 else "d"] = n_c + 1

        def load_turns(eng):
            eng.wait_ge(n_ok, 1)
            return eng.value_load(last_turn[0:1, 0:1], min_val=TEAMS - 1, max_val=TEAMS * (S // CAP) - 1)

        def load_pairs(eng):
            eng.wait_ge(n_ok, 2)
            return eng.value_load(last_pair_at[0:1, 0:1], min_val=TEAMS // 2 - 1,
                                  max_val=TEAMS * (S // CAP) // 2 - 1)

        def pe_moe(pe, tokens):
            pe_tiles_T(pe, xn, 34, (xn_ok, 4), (xn1_ok, 2))
            pe.wait_ge(t_out, 38)
            for i in range(NT):
                for k in range(KD):
                    ins = pe.matmul(bank[0][:, i * 64:i * 64 + NG + NE], xT[:, k, tok(i)], wr[:, k],
                                    start=(k == 0), stop=(k == KD - 1))
            ins.then_inc(r_ps, 1)
            pe.wait_ge(r_ok, 2)
            pe.matmul(bank[1][:, 0:NE], before[:], chosen[:, 0], start=True, stop=True)
            pe.matmul(bank[1][:, NE:2 * NE], ones[:], chosen[:, 0], start=True, stop=False)
            pe.matmul(bank[1][:, NE:2 * NE], before[:], chosen[:, 1], start=False, stop=True)
            pe.matmul(bank[1][:, 2 * NE:3 * NE], ones[:], chosen[:, 0], start=True, stop=False)
            pe.matmul(bank[1][:, 2 * NE:3 * NE], ones[:], chosen[:, 1], start=False, stop=True).then_inc(r_ps, 1)
            last_pair = load_pairs(pe)
            for b in range(4):
                ins = pe.matmul(bank[b][:], zeros[:, 0:P], zeros[:], start=True, stop=False, skip_group_check=True)
            ins.then_inc(m_sc, 1)
            with pe.Fori(0, last_pair + 1) as pair:
                for t in range(2):
                    it = pair * 2 + t
                    pe.wait_ge(m_oh, it * 2 + 1)
                    for half in range(2):
                        for k in range(4):
                            for i in range(NT):
                                ins = pe.matmul(bank[4 + half][:, k * P:(k + 1) * P],
                                                xn[:, i, (4 * half + k) * P:(4 * half + k + 1) * P],
                                                oh[:, i].rearrange("p e s -> p (e s)"), start=(i == 0), stop=(i == 1))
                        ins.then_inc(m_ga, 1)
                    pe.wait_ge(m_oh, it * 2 + 2)
                    for i in range(NT):
                        ins = pe.transpose(bank[7][:, tok(i)], ohg[:, i].rearrange("p e s -> p (e s)"), ident[:])
                    ins.then_inc(m_st, 1)
                    pe.wait_ge(m_xg, it * 2 + 2)
                    j = 0
                    for e, part in TEAM_ORDER:
                        if part == "u":
                            for c in range(4):
                                s = e_slot[(t * TURN + j) % ESLOTS]
                                pe.wait_ge(e_land[s], (pair * (2 * TURN // ESLOTS) + ((t * TURN + j) // ESLOTS + 1)) * 16)
                                w = slot[s].rearrange("p (k q n) -> p k q n", k=2, q=4)
                                for kk in range(2):
                                    k = 2 * c + kk
                                    for q in range(4):
                                        ins = pe.matmul(bank[4 + e % 2][q * CAP:(q + 1) * CAP, 0:2 * P],
                                                        xg[:, k, e * CAP:(e + 1) * CAP], w[:, kk, q],
                                                        start=(k == 0), stop=(k == KD - 1), skip_group_check=True)
                                ins.then_inc(e_used, 1)
                                j += 1
                            continue
                        pe.wait_ge(m_h, it * 4 + (e + 1))
                        if e == 0:
                            pe.wait_ge(m_sT, it + 1)
                        pe.transpose(bank[7][:, 0:P], hmid[:, e % 2], ident[:]).then_inc(m_hp, 1)
                        pe.wait_ge(m_hT, it * 4 + (e + 1))
                        if e >= 1:
                            pe.wait_ge(m_yA, it * 4 + e)
                            pe.wait_ge(m_yV, it * 4 + e)
                        for c in range(2):
                            s = e_slot[(t * TURN + j) % ESLOTS]
                            pe.wait_ge(e_land[s], (pair * (2 * TURN // ESLOTS) + ((t * TURN + j) // ESLOTS + 1)) * 16)
                            w = slot[s].rearrange("p (k q n) -> p k q n", k=2, q=4)
                            for kk in range(2):
                                k = 2 * c + kk
                                for q in range(4):
                                    ins = pe.matmul(bank[6][q * CAP:(q + 1) * CAP, 0:2 * P],
                                                    hTe[:, e % 2, k * CAP:(k + 1) * CAP], w[:, kk, q],
                                                    start=(k == 0), stop=(k == 3), skip_group_check=True)
                            ins.then_inc(e_used, 1)
                            j += 1
                    pe.wait_ge(m_yA, it * 4 + TEAM)
                    pe.wait_ge(m_yV, it * 4 + TEAM)
                    for i in range(NT):
                        for c in range(2):
                            ins = pe.matmul(bank[2 * i + c][:], sT[:, tok(i)], yg[:, c * 512:(c + 1) * 512],
                                            start=False, stop=False, skip_group_check=True)
                    ins.then_inc(m_sc, 1)

        def out_rows(eng, it, e, quarters, copy, post):
            eng.wait_ge(e_used, it * 24 + LAST[e, "d"])
            for q in quarters:
                ins = copy(yg[e * CAP:(e + 1) * CAP, q * 2 * P:(q + 1) * 2 * P], bank[6][q * CAP:(q + 1) * CAP, 0:2 * P])
            ins.then_inc(post, 1)

        def act_moe(act, st):
            act.wait_ge(r_ok, 1)
            act.activation(gs[:, 0:10], gs[:, 0:10], ACT.Exp).then_inc(r_ex, 1)
            last = load_turns(act)

            def silu(it, e):
                act.wait_ge(e_used, it * 24 + LAST[e, "u"])
                act.activation(hact[:, e % 2], bank[4 + e % 2][:, 0:P], ACT.Silu).then_inc(m_sg, 1)

            def hidden_T(it, e):
                act.wait_ge(m_hp, it * 4 + (e + 1))
                act.activation(hTe[:, e % 2], bank[7][:, 0:P], ACT.Copy).then_inc(m_hT, 1)

            def out(it, e):
                out_rows(act, it, e, (0, 1), lambda o, i: act.activation(o, i, ACT.Copy), m_yA)

            with act.Fori(0, last + 1) as it:
                act.wait_ge(m_st, it + 1)
                act.wait_ge(m_sc, it + 1)
                act.activation(sT[:], bank[7][:, 0:S], ACT.Copy).then_inc(m_sT, 1)
                silu(it, 0)
                silu(it, 1)
                hidden_T(it, 0)
                out(it, 0)
                silu(it, 2)
                hidden_T(it, 1)
                out(it, 1)
                silu(it, 3)
                hidden_T(it, 2)
                out(it, 2)
                hidden_T(it, 3)
                out(it, 3)

        def dve_moe(dve, st):
            dve_T(dve, xT, KD, 34, colw[:, 8])
            el, em, key = route[:, 0], route[:, 1], route[:, 2]
            first, second = route[:, 3], route[:, 4]
            gl = gs[:, 16:24].rearrange("p (t g) -> p t g", t=NT)
            gd = gs[:, 0:8].rearrange("p (t g) -> p t g", t=NT)
            gkey = gs[:, 24:32].rearrange("p (t g) -> p t g", t=NT)
            top_g, top_k = gs[:, 32:34], gs[:, 34:36]
            v1, v2, ggate, p1, p2 = (gs[:, c:c + 2] for c in (36, 38, 40, 42, 44))
            desc_g = desc[:, 0:NG].unsqueeze(1).to_broadcast([P, NT, NG])
            desc_e = desc[:, NG:].unsqueeze(1).to_broadcast([P, NT, NE])
            dve.wait_ge(r_ps, 1)
            logits = bank[0][:, 0:P].rearrange("p (t n) -> p t n", t=NT)
            st.then(dve.tensor_copy(gl, logits[:, :, 0:NG]))
            st.link(dve.tensor_copy(el, logits[:, :, NG:NG + NE]))

            def first_max(top, key_, vals, order, n, onehot):
                st.link(dve.tensor_reduce(top, vals, X, ALU.max))
                st.link(dve.tensor_tensor(key_, vals, bc(top, n), ALU.is_equal))
                st.link(dve.tensor_tensor(key_, key_, order, ALU.mult))
                st.link(dve.tensor_reduce(top_k, key_, X, ALU.max))
                st.link(dve.tensor_tensor(onehot, key_, bc(top_k, n), ALU.is_equal))

            first_max(top_g, gkey, gl, desc_g, NG, gkey)
            st.then(dve.tensor_tensor(gd, gl, bc(top_g, NG), ALU.subtract))
            st.link(dve.tensor_scalar(gkey, gkey, -1.0, -NEG, ALU.add, ALU.mult))
            em4 = em.rearrange("p t (g e) -> p t g e", g=NG)
            st.link(dve.tensor_tensor(em4, el.rearrange("p t (g e) -> p t g e", g=NG), bc(gkey, EG), ALU.add))
            first_max(v1, key, em, desc_e, NE, first)
            st.link(dve.scalar_tensor_tensor(em, first, NEG, em, ALU.mult, ALU.add))
            first_max(v2, key, em, desc_e, NE, second)
            dve.tensor_tensor(gs[:, 8:10], v2, v1, ALU.subtract).then_inc(r_ok, 1)
            st.then(dve.tensor_tensor(chosen, first, second, ALU.add))
            st.sync()
            dve.wait_ge(r_ex, 1)
            dve.tensor_reduce(ggate, gd, X, ALU.add).then_inc(r_ok, 1)
            dve.wait_ge(r_ok, 2)
            st.then(dve.tensor_scalar(p1, gs[:, 8:10], 1.0, None, ALU.add))
            st.link(dve.reciprocal(ggate, ggate))
            st.link(dve.reciprocal(p1, p1))
            st.link(dve.tensor_tensor(p1, p1, ggate, ALU.mult))
            st.link(dve.tensor_tensor(p2, gs[:, 8:10], p1, ALU.mult))
            st.then(dve.tensor_tensor(gates, first, bc(p1, NE), ALU.mult))
            st.link(dve.tensor_tensor(key, second, bc(p2, NE), ALU.mult))
            st.then(dve.tensor_tensor(gates, gates, key, ALU.add))
            dve.wait_ge(r_ps, 2)
            rank = bank[1][:, 0:2 * NE].rearrange("p (t n) -> p t n", t=NT)
            st.link(dve.scalar_tensor_tensor(ranks, rank, 1.0, chosen, ALU.add, ALU.mult))
            st.link(dve.tensor_scalar(ranks, ranks, -1.0, None, ALU.add))
            st.link(dve.tensor_reduce(gs[:, 46:47], bank[1][:, 2 * NE:3 * NE], X, ALU.max))
            st.link(dve.tensor_scalar(gs[:, 48:56], iota[:, 0:S:CAP], gs[:, 46:47], float(TEAMS), ALU.is_lt, ALU.mult))
            st.link(dve.tensor_reduce(gs[:, 47:48], gs[:, 48:56], X, ALU.add))
            dve.tensor_scalar(last_turn[:], gs[:, 47:48], -1.0, None, ALU.add).then_inc(n_ok, 1)
            dve.tensor_scalar(last_pair_at[:], gs[:, 47:48], 0.5, -1.0, ALU.mult, ALU.add).then_inc(n_ok, 1)
            last = load_turns(dve)

            def hidden(it, e):
                dve.wait_ge(m_sg, it * 4 + (e + 1))
                dve.tensor_tensor(hmid[:, e % 2], hact[:, e % 2], bank[4 + e % 2][:, P:2 * P], ALU.mult).then_inc(m_h, 1)

            def out(it, e):
                out_rows(dve, it, e, (2, 3), dve.tensor_copy, m_yV)

            with dve.Fori(0, last + 1) as it:
                team, lap = it % TEAMS, it // TEAMS
                slots = iota[:, bass.ds(lap * CAP, CAP)].unsqueeze(1).to_broadcast([P, TEAM, CAP])
                for i in range(NT):
                    ins = dve.tensor_tensor(oh[:, i], bc(ranks[:, i, bass.ds(team * TEAM, TEAM)], CAP), slots, ALU.is_equal)
                    if i == 0:
                        ins.then_inc(dve_loop, 1)
                ins.then_inc(m_oh, 1)
                dve.wait_ge(dve_loop, it + 1)
                dve.wait_ge(m_oh, it * 2 + 1)
                for i in range(NT):
                    ins = dve.tensor_tensor(ohg[:, i], oh[:, i], bc(gates[:, i, bass.ds(team * TEAM, TEAM)], CAP), ALU.mult)
                ins.then_inc(m_oh, 1)
                for half in range(2):
                    dve.wait_ge(m_ga, it * 2 + (half + 1))
                    dve.tensor_tensor(xg[:, 4 * half:4 * half + 4], bank[4 + half][:].rearrange("p (k s) -> p k s", k=4),
                                      bc(colw[:, 8, 4 * half:4 * half + 4], P), ALU.mult).then_inc(m_xg, 1)
                hidden(it, 0)
                hidden(it, 1)
                dve.wait_ge(m_sc, it + 1)
                out(it, 0)
                hidden(it, 2)
                out(it, 1)
                hidden(it, 3)
                out(it, 2)
                out(it, 3)
            dve.wait_ge(m_sc, last + 2)
            for i in range(NT):
                for c in range(2):
                    ins = dve.tensor_tensor(x[:, i, c * 512:(c + 1) * 512], bank[2 * i + c][:],
                                            x[:, i, c * 512:(c + 1) * 512], ALU.add)
                    if i + c < 2:
                        st.then(ins)
            st.sync()
            ins.then_inc(x_ok, 1)

        FFN_W = 2 * FT
        DVE_PAD, POOL_PAD = 256, 48
        POW2, VAR1, VAR2 = 5, 7, 5
        fills1 = [sum(c % SLOTS1 == s for c in range(DENSE1)) for s in range(SLOTS)]
        fills2 = [dense_slot.count(s) for s in range(SLOTS)]

        def dense_ready(l, c):
            s = dense_slot[c]
            return s, (l * fills2[s] + fills1[s] + dense_slot[:c + 1].count(s)) * 16

        def ring_tile(v):
            return (v % FSLOTS) * FTW

        def layer_loads(sp):
            for p in range(2):
                sp.sem_inc(f_land[p], 16)
            with sp.Fori(0, LAYERS) as l:
                for f in range(2):
                    g = l * 2 + f

                    def tile(v, p):
                        sp.wait_ge(f_land[p], (g * (FT // 2) + v // 2 + 1) * 16)
                        sp.dma_start(ring[:, bass.ds(ring_tile(v), FTW)], d_wf[g * FT + v]).then_inc(f_land[p], 16)

                    for v in range(FSLOTS):
                        if f == 0:
                            sp.wait_ge(wl_ok, g * FFN_W + (2 * last_tile[v] + 2))
                        else:
                            sp.wait_ge(d_used, l * DENSE2 + (DENSE1 + 1 + max(last_dense[s] for s in chunks_in(v))))
                        tile(v, v % 2)
                    with sp.Fori(FSLOTS // 2, FT // 2) as i:
                        for p in range(2):
                            sp.wait_ge(wl_ok, g * FFN_W + i * 4 + (2 * p + FFN_W + 2 - 2 * FSLOTS))
                            sp.wait_ge(f_land[p], (g * (FT // 2) + i + 1) * 16)
                            sp.dma_start(ring[:, bass.ds(ring_tile(i * 2 + p), FTW)],
                                         d_wf[g * FT + i * 2 + p]).then_inc(f_land[p], 16)
                    if f == 0:
                        for c in range(DENSE2):
                            s = dense_slot[c]
                            if c < SLOTS:
                                sp.wait_ge(wl_ok, g * FFN_W + (FFN_W + 2 * max(last_tile[q] for q in tiles_in(s)) + 2))
                            else:
                                sp.wait_ge(d_used, l * DENSE2 + (DENSE1 + c - SLOTS + 1))
                            sp.dma_start(slot[s], d_w2[l * DENSE2 + c]).then_inc(d_land[s], 16)

        def pe_ffn(pe, l, f, tokens):
            g = l * 2 + f
            tb = l * T2 + (T1 + (0 if f == 0 else T2 - 4))
            if f == 0:
                pe.wait_ge(x_ok, l * 3 + 3)
                pe_T(pe, tokens(x), tb)
            else:
                pe_tiles_T(pe, x, tb, (x0_ok, l * 3 + (X01 + 2)), (x_ok, l * 3 + 5))
            for b in range(4):
                ins = pe.matmul(bank[b][:], zeros[:, 0:P], zeros[:], start=True, stop=False, skip_group_check=True)
            ins.then_inc(f_dn, 1)
            pe.wait_ge(t_out, tb + 4)

            def up(t, p):
                pe.wait_ge(wl_ok, g * FFN_W + t * 2 + (FFN_W + 1))
                for m in range(2):
                    for k in range(KD):
                        cols = slice(k * 2 * P + m * P, k * 2 * P + (m + 1) * P)
                        for n, (w, v) in enumerate(((wh, xh), (wh, xl), (wl, xh))):
                            ins = pe.matmul(bank[4 + p][:, m * S:(m + 1) * S], w[p][:, cols], v[:, k],
                                            start=(k == 0 and n == 0), stop=(k == KD - 1 and n == 2))
                ins.then_inc(f_gu, 1)

            def down(t, p, last=False):
                pe.wait_ge(f_h, g * FT + t + 1)
                pe.wait_ge(wl_ok, g * FFN_W + t * 2 + (FFN_W + 2))
                for i in range(NT):
                    for v, w in ((hh, wh), (hl, wh), (hh, wl)):
                        for c in range(2):
                            ins = pe.matmul(bank[2 * i + c][:], v[p][:, tok(i)],
                                            w[p][:, 2 * D + c * 512:2 * D + (c + 1) * 512],
                                            start=False, stop=False, skip_group_check=True)
                    if last and i == 0:
                        ins.then_inc(fhalf_ok, 1)
                ins.then_inc(f_dn, 1)

            up(0, 0)
            with pe.Fori(0, FT // 2 - 1) as i:
                for p in range(2):
                    up(i * 2 + (p + 1), 1 - p)
                    down(i * 2 + p, p)
            up(FT - 1, 1)
            down(FT - 2, 0)
            down(FT - 1, 1, last=True)

        def act_ffn(act, l, f):
            g = l * 2 + f
            tb = l * T2 + (T1 + (0 if f == 0 else T2 - 4))
            for j in range(4):
                act.wait_ge(t_ps, tb + (j + 1))
                act.activation(xh[:, 2 * j:2 * j + 2].rearrange("p k s -> p (k s)"), bank[4 + j][:], ACT.Copy)\
                   .then_inc(xh_ok, 1)
            if f == 1:
                load_ln(act, l, 2)

            def high(t, p, down):
                cols = slice(2 * D, FTW) if down else slice(0, 2 * D)
                n = cols.stop - cols.start
                act.activation(wh[p][:, cols], ring[:, bass.ds(ring_tile(t) + cols.start, n)], ACT.Copy).then_inc(wh_ok, 1)

            def landed(t, half, p):
                act.wait_ge(f_land[p], (g * (FT // 2) + half + 2) * 16)

            def silu(t, p):
                act.wait_ge(f_gu, g * FT + t + 1)
                act.activation(sg[:, p], bank[4 + p][:, 0:S], ACT.Silu).then_inc(f_sg, 1)

            def down_free(t):
                act.wait_ge(f_dn, g * (FT + 1) + t + 1)

            landed(0, 0, 0)
            high(0, 0, False)
            high(0, 0, True)
            landed(1, 0, 1)
            high(1, 1, False)
            with act.Fori(0, FT // 2 - 1) as i:
                for p in range(2):
                    silu(i * 2 + p, p)
                    down_free(i * 2 + p)
                    high(i * 2 + (p + 1), 1 - p, True)
                    landed(None, i + 1, p)
                    high(i * 2 + (p + 2), p, False)
            silu(FT - 2, 0)
            down_free(FT - 2)
            high(FT - 1, 1, True)
            silu(FT - 1, 1)

        def dve_ffn(dve, st, l, f):
            g = l * 2 + f
            tb = l * T2 + (T1 + (0 if f == 0 else T2 - 4))
            for j in range(4):
                dve.wait_ge(t_ps, tb + (j + 1))
                dve.wait_ge(xh_ok, g * 4 + (j + 1))
                dve.tensor_tensor(xl[:, 2 * j:2 * j + 2].rearrange("p k s -> p (k s)"), bank[4 + j][:],
                                  xh[:, 2 * j:2 * j + 2].rearrange("p k s -> p (k s)").bitcast(F32),
                                  ALU.subtract).then_inc(t_out, 1)

            def low(t, half, p, down):
                cols = slice(2 * D, FTW) if down else slice(0, 2 * D)
                n = cols.stop - cols.start
                dve.wait_ge(wh_ok, g * FFN_W + t * 2 + (2 if down else 1))
                dve.tensor_tensor(wl[p][:, cols], ring[:, bass.ds(ring_tile(t) + cols.start, n)],
                                  wh[p][:, cols].bitcast(F32), ALU.subtract).then_inc(wl_ok, 1)

            def hidden(t, p):
                dve.wait_ge(f_sg, g * FT + t + 1)
                dve.tensor_tensor(hf[:, p], sg[:, p], bank[4 + p][:, S:2 * S], ALU.mult).then_inc(f_hv, 1)
                dve.wait_ge(f_hv, (g * FT + t) * 2 + 1)
                dve.tensor_copy(hh[p][:], hf[:, p]).then_inc(f_hv, 1)
                dve.wait_ge(f_hv, (g * FT + t) * 2 + 2)
                dve.tensor_tensor(hl[p][:], hf[:, p], hh[p][:].bitcast(F32), ALU.subtract).then_inc(f_h, 1)

            low(0, 0, 0, False)
            low(0, 0, 0, True)
            low(1, 0, 1, False)
            st.then(dve.tensor_scalar(x[:], x[:], ALPHA, None, ALU.mult))
            with dve.Fori(0, FT // 2 - 1) as i:
                for p in range(2):
                    hidden(i * 2 + p, p)
                    low(i * 2 + (p + 1), 0, 1 - p, True)
                    low(i * 2 + (p + 2), 0, p, False)
            hidden(FT - 2, 0)
            low(FT - 1, 0, 1, True)
            hidden(FT - 1, 1)
            layer_norm(dve, st, l, 2 * f, 0.5, (fhalf_ok, g + 1), (f_dn, (g + 1) * (FT + 1)))

        def load_ln(act, l, n):
            act.dma_start(ln[:].rearrange("p a d -> p (a d)"), d_ln[l * 3 + n]).then_inc(ln_in, 16)

        def layer_norm(dve, st, l, n, scale, *waits):
            st.sync()
            for i in range(NT):
                dve.wait_ge(*waits[i])
                for c in range(2):
                    part = x[:, i, c * 512:(c + 1) * 512]
                    st.then(dve.scalar_tensor_tensor(part, bank[2 * i + c][:], scale, part, ALU.mult, ALU.add))
                st.sync()
                for c in range(2):
                    st.then(dve.bn_stats(bn[:, i, c], x[:, i, c * 512:(c + 1) * 512]))
            st.sync()
            st.then(dve.tensor_copy(nrd[:, 0, 0:1], bn[:, 0, 0, 0:1]))
            for i in range(NT):
                st.then(dve.bn_aggr(mean[:, i], bn[:, i].rearrange("p c k -> p (c k)")))
            st.sync()
            dve.tensor_scalar(rs, mean[:, :, 1], 1.0, EPS2, ALU.mult, ALU.add).then_inc(var_ok, 1)
            dve.wait_ge(ln_in, (l * 3 + n + 1) * 16)
            for i in range(NT):
                st.then(dve.scalar_tensor_tensor(x[:, i], x[:, i], mean[:, i, 0:1], ln[:, 0], ALU.subtract, ALU.mult))
            st.sync()
            dve.wait_ge(pow_ok, l * POW2 + (POW1 + [1, 4, 5][n]))
            for i in range(NT):
                ins = dve.scalar_tensor_tensor(x[:, i], x[:, i], rs[:, i:i + 1], ln[:, 1], ALU.mult, ALU.add)
                if i < NT - 1:
                    ins.then_inc(x0_ok, 1)
            ins.then_inc(x_ok, 1)

        CQ = B0

        def pe_layers(pe, tokens):
            with pe.Fori(0, LAYERS) as l:
                pe_ffn(pe, l, 0, tokens)
                tb = l * T2 + (T1 + 4)
                used = l * DENSE2 + DENSE1
                pe_tiles_T(pe, x, tb, (x0_ok, l * 3 + (X01 + 1)), (x_ok, l * 3 + 4))
                pe.wait_ge(t_out, tb + 4)
                for n in range(3):
                    if n == 2:
                        pe.wait_ge(den_a, l * 3 + 7)
                        pe.wait_ge(den_v, l * 3 + 7)
                    pe_part(pe, run2(l, 0), n, xTl2, n)
                pe.wait_ge(den_a, l * 3 + 8)
                pe.wait_ge(t_src, l * 2 + 5)
                pe_T(pe, [[proj2[:, i, CQ + b * P:CQ + (b + 1) * P] for i in range(NT)] for b in range(3)], tb + 4)
                pe.wait_ge(t_out, tb + 6)
                s, value = dense_ready(l, PART2[3])
                pe.wait_ge(d_land[s], value)
                pe.wait_ge(den_a, l * 3 + 9)
                for i in range(NT):
                    for k in range(2):
                        pe.matmul(bank[i][:, 0:BH * BQ], cT[:, k, tok(i)], slot[s][:, k * BH * BQ:(k + 1) * BH * BQ],
                                  start=(k == 0), stop=(k == 1))
                    ins = pe.matmul(bank[2 + i][:], cT[:, 2, tok(i)], slot[s][:, 2 * BH * BQ:2 * BH * BQ + 512],
                                    start=True, stop=True)
                ins.then_inc(d_used, 1)
                pe.wait_ge(rope_ok, l * 2 + 1)
                cols = [A0, A0 + P, A0 + 2 * P, C0, C0 + P, C0 + 2 * P, D0, D0 + P, D0 + 2 * P, D0 + 3 * P]
                pe_T(pe, [[proj2[:, i, c:c + P] for i in range(NT)] for c in cols], tb + 6)
                pe.wait_ge(t_out, tb + 11)

                def between(u):
                    if 1 <= u < 5:
                        j = u - 1
                        if j == 0:
                            pe.wait_ge(rope_ok, l * 2 + 2)
                        if j >= 2:
                            pe.wait_ge(t_out, tb + (10 + j))
                        for b in range(2):
                            for i in range(NT):
                                ins = pe.transpose(bank[6 + j % 2][0:BQ, b * S + i * P:b * S + (i + 1) * P],
                                                   (qm, km)[j // 2][:, i, 2 * (j % 2) + b], ident[:])
                        ins.then_inc(t_ps, 1)
                    if u == 6:
                        pe.wait_ge(t_out, tb + 15)

                pe.wait_ge(c_a, l + 1)
                pe.wait_ge(kv_ok, l + 1)
                pe_units(pe, units2, lg2, l * UNITS2 + UNITS1, old=1, between=between)
                pe.wait_ge(o_ok, (l + 1) * UNITS2 + UNITS1)
                pe.wait_ge(t_src, l * 2 + 6)
                pe_T(pe, tokens(cat2), tb + 15)
                pe.wait_ge(t_out, tb + 19)
                pe_part(pe, run2(l, 1), 0, xTl2, 0)
                pe_ffn(pe, l, 1, tokens)

        def act_layers(act, st):
            with act.Fori(0, LAYERS) as l:
                act.wait_ge(x_ok, l * 3 + 3)
                act.dma_start(row2[:], d_row2[l]).then_inc(row_in, 16)
                act.dma_start(colw2[:], d_cT2[l]).then_inc(row_in, 16)
                load_ln(act, l, 0)
                act_ffn(act, l, 0)
                act.wait_ge(x_ok, l * 3 + 4)
                act.dma_start(bias[:].rearrange("p h t s -> p (h t s)"), d_bias[1]).then_inc(bias_in, 16)
                tb = l * T2 + (T1 + 4)
                used = l * DENSE2 + DENSE1
                run = run2(l, 0)
                act.wait_ge(f_dn, (l * 2 + 1) * (FT + 1))
                act_high(act, run, 0)
                act_high(act, run, 1)
                act_high_T(act, run)
                stream(lambda c: act_high(act, run, c), run, 2,
                       [lambda n=n, width=width: evac_act(act, n, l * 4 + (9 + n), proj2[:, 0, n * D:n * D + width], width)
                        for n, width in enumerate((D, D, W3))])
                act.wait_ge(lam_in, l + 1)
                act.activation(lam2, lam2, ACT.Exp).then_inc(lam_ex, 1)
                act.wait_ge(d_used, used + PART2[4])
                for i in range(NT):
                    ins = act.activation(qm[:, i].rearrange("p h d -> p (h d)"), bank[i][:, 0:BH * BQ], ACT.Copy)
                ins.then_inc(c_a, 1)
                run = run2(l, 1)

                def between(u):
                    if u == 6:
                        act.wait_ge(t_ps, tb + 15)
                        act_high(act, run, 0)

                act_units(act, units2, lg2, l * UNITS2 + UNITS1, old=1, between=between)
                act.wait_ge(sc_ps, (l + 1) * UNITS2 + UNITS1)
                act_high(act, run, 1)
                act.wait_ge(t_src, l * 2 + 6)
                load_ln(act, l, 1)
                act_high_T(act, run, colw2[:, 0:KD])
                act_high(act, run, 2)
                act_high(act, run, 3)
                act_ffn(act, l, 1)

        def dve_layers(dve, st):
            before_layers = st.n
            with dve.Fori(0, LAYERS) as l:
                st.base, st.n = l * DVE_PAD + before_layers, 0
                dve_ffn(dve, st, l, 0)
                tb = l * T2 + (T1 + 4)
                used = l * DENSE2 + DENSE1
                run = run2(l, 0)
                dve_low_T(dve, run, xTl2)
                st.link(dve.tensor_scalar(x[:], x[:], ALPHA, None, ALU.mult))
                dve.wait_ge(row_in, (l + 1) * 32)
                lp = row2[:, 388:516].rearrange("p (a b d) -> p a b d", a=2, b=2)
                prod = tmp2[:, 0:64].rearrange("p (a d) -> p a d", a=2)
                st.link(dve.tensor_tensor(prod, lp[:, :, 0], lp[:, :, 1], ALU.mult))
                dve.tensor_reduce(lam2, prod, X, ALU.add).then_inc(lam_in, 1)

                def squares():
                    dve.wait_ge(den_a, l * 3 + 7)
                    dve.wait_ge(den_v, l * 3 + 7)
                    for i in range(NT):
                        lat, ax = tmp2[:, 0:384], tmp2[:, 384:768]
                        st.then(dve.tensor_tensor(lat, proj2[:, i, CQ:CQ + 384], proj2[:, i, CQ:CQ + 384], ALU.mult))
                        st.link(dve.tensor_tensor(ax, proj2[:, i, C0:C0 + 384], proj2[:, i, C0:C0 + 384], ALU.mult))
                        st.then(dve.tensor_reduce(ssq[:, i, 0:1], lat[:, 0:QW], X, ALU.add))
                        st.then(dve.tensor_reduce(ssq[:, i, 1:2], lat[:, QW:384], X, ALU.add))
                        st.link(dve.tensor_reduce(ssq[:, i, 2:8], ax.rearrange("p (h d) -> p h d", h=6), X, ALU.add))
                    for a, b, width in ((0, 1, QW), (1, 2, KVW), (2, 8, 64)):
                        ins = dve.tensor_scalar(rsq[:, :, a:b], ssq[:, :, a:b], 1.0 / width, EPS2, ALU.mult, ALU.add)
                        if a < 2:
                            st.then(ins)
                    ins.then_inc(var_ok, 1)

                def scales():
                    dve.wait_ge(pow_ok, l * POW2 + (POW1 + 2))
                    for i in range(NT):
                        st.then(dve.tensor_scalar(proj2[:, i, CQ:CQ + QW], proj2[:, i, CQ:CQ + QW], rsq[:, i, 0:1], None, ALU.mult))
                        ins = dve.tensor_scalar(proj2[:, i, CQ + QW:CQ + 384], proj2[:, i, CQ + QW:CQ + 384],
                                                rsq[:, i, 1:2], None, ALU.mult)
                        if i < NT - 1:
                            st.then(ins)
                    st.sync()
                    ins.then_inc(t_src, 1)
                    for i in range(NT):
                        ax = proj2[:, i, C0:C0 + 384].rearrange("p (h d) -> p h d", h=6)
                        st.then(dve.tensor_tensor(ax, ax, bc(rsq[:, i, 2:8], 64), ALU.mult))
                    st.sync()
                    for i in range(NT):
                        ins = dve.tensor_tensor(proj2[:, i, C0:C0 + 384], proj2[:, i, C0:C0 + 384], row2[:, 0:384], ALU.mult)
                        if i < NT - 1:
                            st.link(ins)
                    ins.then_inc(ax_ok, 1)

                def project(c):
                    low(dve, run, c)
                    if c == 5:
                        squares()
                    if c == 6:
                        scales()

                stream(project, run, 2,
                       [lambda n=n, width=width: evac_dve(dve, n, used + PART2[n + 1],
                                                          proj2[:, 1, n * D:n * D + width], width)
                        for n, width in enumerate((D, D, W3))])
                dve.wait_ge(lam_ex, l + 1)
                st.link(dve.tensor_tensor(nlam[:, 0:1], lam2[:, 1:2], lam2[:, 0:1], ALU.subtract))
                st.link(dve.tensor_tensor(nlam[:, 0:1], nlam[:, 0:1], row2[:, 516:517], ALU.subtract))
                dve_T(dve, cT, 3, tb + 4, colw2[:, KD:KD + 3])
                dve.wait_ge(d_used, used + PART2[4])
                for i in range(NT):
                    kv = bank[2 + i][:].rearrange("p (h d) -> p h d", h=BH)
                    st.then(dve.tensor_copy(km[:, i, :, 0:64], kv[:, :, 0:64]))
                    ins = dve.tensor_copy(vm[:, i], kv[:, :, 64:128])
                    if i < NT - 1:
                        st.then(ins)
                ins.then_inc(kv_ok, 1)
                dve_T(dve, qkT2, 10, tb + 6)
                dve.wait_ge(bias_in, l * 16 + 32)

                def between(u):
                    if 1 <= u < 5:
                        j = u - 1
                        dve.wait_ge(t_ps, tb + (12 + j))
                        dve.tensor_copy(qkT2[0:BQ, 10 + 2 * j:12 + 2 * j, :],
                                        bank[6 + j % 2][0:BQ].rearrange("p (b s) -> p b s", b=2)).then_inc(t_out, 1)
                    if u == DIFF_DONE + 1:
                        dve.wait_ge(o_ok, l * UNITS2 + (UNITS1 + DIFF_DONE))
                        sq = tmp2[:, 0:512].rearrange("p (t d) -> p t d", t=NT)
                        st.link(dve.tensor_tensor(sq, cat2[:, :, 768:1024], cat2[:, :, 768:1024], ALU.mult))
                        st.link(dve.tensor_reduce(ssq[:, :, 0:4], sq.rearrange("p t (h d) -> p t h d", h=4), X, ALU.add))
                        dve.tensor_scalar(rsq[:, :, 0:4], ssq[:, :, 0:4], 1.0 / 64, EPS2, ALU.mult, ALU.add).then_inc(var_ok, 1)
                    if u == DIFF_DONE + 2:
                        dve.wait_ge(pow_ok, l * POW2 + (POW1 + 3))
                        st.link(dve.tensor_scalar(rsq[:, :, 0:4], rsq[:, :, 0:4], row2[:, 517:518], None, ALU.mult))
                        for i in range(NT):
                            od = cat2[:, i, 768:1024].rearrange("p (h d) -> p h d", h=4)
                            ins = dve.tensor_tensor(od, od, bc(rsq[:, i, 0:4], 64), ALU.mult)
                            if i < NT - 1:
                                st.link(ins)
                        ins.then_inc(t_src, 1)

                dve_units(dve, st, units2, lg2, l * UNITS2 + UNITS1, old=1, between=between)
                run = run2(l, 1)
                dve_low_T(dve, run, xTl2, colw2[:, 0:KD])
                low(dve, run, 2)
                low(dve, run, 3)
                layer_norm(dve, st, l, 1, 1.0, (half_ok, l * 4 + 12), (d_used, used + DENSE2))
                dve_ffn(dve, st, l, 1)
                st.sync()
                st.pad(DVE_PAD)

        def pool_layers(pool, st):
            before_layers = st.n

            def rotate(x1, x2, cos, sin, y1, y2, t):
                st.then(pool.tensor_tensor(t[0], x1, cos, ALU.mult))
                st.then(pool.tensor_tensor(t[1], x2, sin, ALU.mult))
                st.then(pool.tensor_tensor(t[2], x1, sin, ALU.mult))
                st.link(pool.tensor_tensor(t[3], x2, cos, ALU.mult))
                st.then(pool.tensor_tensor(y1, t[0], t[1], ALU.subtract))
                return pool.tensor_tensor(y2, t[2], t[3], ALU.add)

            def scratch(at_c, shape):
                n = int(np.prod(shape))
                names = "abc"[:len(shape)]
                pattern = f"p ({' '.join(names)}) -> p {' '.join(names)}"
                return [tmp2[:, at_c + r * n:at_c + (r + 1) * n].rearrange(pattern, **dict(zip(names, shape)))
                        for r in range(4)]

            with pool.Fori(0, LAYERS) as l:
                st.base, st.n = l * POOL_PAD + before_layers, 0
                pool.wait_ge(var_ok, l * VAR2 + (VAR1 + 1))
                inverse_root(pool, rs)
                for c in range(2):
                    low(pool, run2(l, 0), c)
                pool.wait_ge(var_ok, l * VAR2 + (VAR1 + 2))
                inverse_root(pool, rsq[:, :, 0:8])
                pool.wait_ge(ax_ok, l + 1)
                for i in range(NT):
                    v = proj2[:, i, C0:C0 + 384].rearrange("p (h a b d) -> p h a b d", h=6, a=2, b=2)
                    cos, sin = (rope[:, i, c:c + 32].rearrange("p (a d) -> p a d", a=2).unsqueeze(1)
                                .to_broadcast([P, 6, 2, 16]) for c in (32, 64))
                    ins = rotate(v[:, :, :, 0], v[:, :, :, 1], cos, sin, v[:, :, :, 0], v[:, :, :, 1],
                                 scratch(i * 768, (6, 2, 16)))
                    if i < NT - 1:
                        st.then(ins)
                ins.then_inc(rope_ok, 1)
                pool.wait_ge(rope_ok, l * 2 + 1)
                pool.wait_ge(c_a, l + 1)
                pool.wait_ge(kv_ok, l + 1)
                for i in range(NT):
                    q = qm[:, i, :, 64:96].rearrange("p h (b d) -> p h b d", b=2)
                    k = km[:, i, :, 64:96].rearrange("p h (b d) -> p h b d", b=2)
                    r = proj2[:, i, CQ + 384:CQ + 416].rearrange("p (b d) -> p b d", b=2)
                    cos, sin = (rope[:, i, c:c + 16].unsqueeze(1).to_broadcast([P, BH, 16]) for c in (0, 16))
                    r1, r2 = (r[:, b].unsqueeze(1).to_broadcast([P, BH, 16]) for b in range(2))
                    st.then(rotate(q[:, :, 0], q[:, :, 1], cos, sin, q[:, :, 0], q[:, :, 1], scratch(i * 512, (BH, 16))))
                    ins = rotate(r1, r2, cos, sin, k[:, :, 0], k[:, :, 1], scratch(i * 512 + 256, (BH, 16)))
                    if i < NT - 1:
                        st.then(ins)
                ins.then_inc(rope_ok, 1)
                low(pool, run2(l, 1), 0)
                pool.wait_ge(var_ok, l * VAR2 + (VAR1 + 3))
                inverse_root(pool, rsq[:, :, 0:4])
                low(pool, run2(l, 1), 1)
                for n in (4, 5):
                    pool.wait_ge(var_ok, l * VAR2 + (VAR1 + n))
                    inverse_root(pool, rs)
                st.sync()
                st.pad(POOL_PAD)

        @block.sync
        def _(sp):
            sp.dma_start(memt[:], d_mem.rearrange("(t p) d -> p t d", p=P)).then_inc(mem_in, 16)
            sp.dma_start(ident[:], d_tab[:, 0:P]).then_inc(first_in, 16)
            sp.dma_start(colw[:], d_cT1).then_inc(first_in, 16)
            for c in range(2):
                sp.dma_start(slot[c], d_w1[c]).then_inc(d_land[c], 16)
            loads = [(x, d_x.rearrange("(t p) d -> p t d", p=P)), (row1, d_row1), (wr, d_wr)]
            at_c = P
            for t in (before, ones, iota, rel, desc, rope):
                n = int(np.prod(t.shape[1:]))
                dst = t[:] if len(t.shape) == 2 else t[:].rearrange(
                    {3: "p a b -> p (a b)", 4: "p a b c -> p (a b c)"}[len(t.shape)])
                loads.append((dst, d_tab[:, at_c:at_c + n]))
                at_c += n
            for dst, src in loads:
                sp.dma_start(dst[:] if not isinstance(dst, bass.AP) else dst, src).then_inc(consts_in, 16)
            for c in range(2, DENSE1):
                if c >= SLOTS1:
                    sp.wait_ge(d_used, c - SLOTS1 + 1)
                sp.dma_start(slot[c % SLOTS1], d_w1[c]).then_inc(d_land[c % SLOTS1], 16)
                if c == 8:
                    sp.dma_start(bias[:], d_bias[0]).then_inc(bias_in, 16)
            def expert_chunk(pair, j):
                e, c = TEAM_CHUNKS[j % TURN]
                src = d_we[((pair % (TEAMS // 2)) * 2 * TEAM + (j // TURN * TEAM + e)) * 6 + c]
                s = e_slot[j % ESLOTS]
                sp.dma_start(slot[s], src).then_inc(e_land[s], 16)

            for j in range(ESLOTS):
                if e_slot[j] < SLOTS1:
                    sp.wait_ge(d_used, DENSE1 - SLOTS1 + (e_slot[j] - DENSE1) % SLOTS1 + 1)
                elif e_slot[j] < SLOTS:
                    sp.wait_ge(d_used, DENSE1)
                elif e_slot[j] == SLOTS:
                    sp.wait_ge(o_ok, UNITS1)
                expert_chunk(0, j)
            last_pair = load_pairs(sp)
            used = 2 * TURN
            with sp.Fori(0, last_pair) as pair:
                for j in range(ESLOTS, used):
                    sp.wait_ge(e_used, pair * used + (j - ESLOTS + 1))
                    expert_chunk(pair, j)
                for j in range(ESLOTS):
                    sp.wait_ge(e_used, pair * used + (used - ESLOTS + j + 1))
                    expert_chunk(pair + 1, j)
            for j in range(ESLOTS, used):
                sp.wait_ge(e_used, last_pair * used + (j - ESLOTS + 1))
                expert_chunk(last_pair, j)
            sp.wait_ge(e_used, last_pair * used + used)
            layer_loads(sp)
            sp.wait_ge(x_ok, 3 + 3 * LAYERS)
            sp.dma_start(d_out.rearrange("(t p) d -> p t d", p=P), x[:]).then_inc(out_done, 16)
            sp.wait_ge(out_done, 16)

        def pe_T(pe, srcs, base, rows=P):
            for j in range(0, len(srcs), 2):
                n = j // 2
                if n >= 4:
                    pe.wait_ge(t_out, base + (n - 3))
                for b, src in enumerate(srcs[j:j + 2]):
                    for i in range(NT):
                        ins = pe.transpose(bank[4 + n % 4][0:rows, b * S + i * P:b * S + (i + 1) * P], src[i], ident[:])
                ins.then_inc(t_ps, 1)

        def pe_tiles_T(pe, src, base, wait0, wait1):
            for i, (ready, value) in enumerate((wait0, wait1)):
                pe.wait_ge(ready, value)
                for b in range(KD):
                    ins = pe.transpose(bank[4 + b // 2][:, (b % 2) * S + i * P:(b % 2) * S + (i + 1) * P],
                                       src[:, i, b * P:(b + 1) * P], ident[:])
                    if i == NT - 1 and b % 2 == 1:
                        ins.then_inc(t_ps, 1)

        def pe_part(pe, run, part, xl, n):
            sel = 4 * (n % 2)
            end, width = run.parts[part]
            first = run.parts[part - 1][0] if part else 0
            for c in range(first, end):
                if c < 2:
                    pe.wait_ge(dlp_ok, run.low_p + (c + 1))
                else:
                    pe.wait_ge(dlv_ok, run.low_v + (c - 1))
                per = KD // (end - first)
                wh, wl = (w[:, 0:per * width].rearrange("p (k n) -> p k n", k=per)
                          for w in (run.highs[c % 2], slot_r[run.slots[c]]))
                steps = [(kk, i) for kk in range(per) for i in range(NT)]
                if c == end - 1:
                    steps.sort(key=lambda s: s[1])
                for kk, i in steps:
                    k = (c - first) * per + kk
                    for m, (v, w) in enumerate(((xTh, wh), (xTh, wl), (xl, wh))):
                        for c0 in range(0, width, 512):
                            c1 = min(c0 + 512, width)
                            ins = pe.matmul(bank[sel + 2 * i + c0 // 512][:, 0:c1 - c0], v[:, k, tok(i)],
                                            w[:, kk, c0:c1], start=(k == 0 and m == 0),
                                            stop=(k == KD - 1 and m == 2))
                    if c == end - 1 and (kk, i) == (per - 1, 0):
                        ins.then_inc(half_ok, 1)
                ins.then_inc(d_used, 1)

        def evac_act(act, n, parts, dst, width=D):
            act.wait_ge(half_ok, parts)
            sel = 4 * (n % 2)
            for c0 in range(0, width, 512):
                c1 = min(c0 + 512, width)
                ins = act.activation(dst[:, c0:c1], bank[sel + c0 // 512][:, 0:c1 - c0], ACT.Copy)
            ins.then_inc(den_a, 1)

        def evac_dve(dve, n, base_used, dst, width=D):
            dve.wait_ge(d_used, base_used)
            sel = 4 * (n % 2) + 2
            for c0 in range(0, width, 512):
                c1 = min(c0 + 512, width)
                ins = dve.tensor_copy(dst[:, c0:c1], bank[sel + c0 // 512][:, 0:c1 - c0])
            ins.then_inc(den_v, 1)

        def dve_T(dve, dst, nblocks, base, weights=None, rows=P):
            for j in range(0, nblocks, 2):
                b = min(2, nblocks - j)
                dve.wait_ge(t_ps, base + (j // 2 + 1))
                src = bank[4 + (j // 2) % 4][0:rows, 0:b * S].rearrange("p (b s) -> p b s", b=b)
                if weights is None:
                    ins = dve.tensor_copy(dst[0:rows, j:j + b, :], src)
                else:
                    ins = dve.tensor_tensor(dst[0:rows, j:j + b, :], src, bc(weights[0:rows, j:j + b], S), ALU.mult)
                ins.then_inc(t_out, 1)

        def pe_scores(pe, u, unit):
            for i in range(NT):
                for b in range(len(unit.q)):
                    ins = pe.matmul(bank[u % 2][:, i * S:(i + 1) * S], unit.q[b][i], unit.k[b],
                                    start=(b == 0), stop=(b == len(unit.q) - 1))
            ins.then_inc(sc_ps, 1)

        def pe_probs_T(pe, u, n, lg):
            pe.wait_ge(ex_ok, n + 1)
            for t in range(NT):
                for i in range(NT):
                    ins = pe.transpose(bank[2 + u % 2][:, t * S + i * P:t * S + (i + 1) * P],
                                       lg[:, u % 2, i, t * P:(t + 1) * P], ident[:])
            ins.then_inc(pt_ps, 1)

        def pe_values(pe, u, n, unit):
            pe.wait_ge(pt_ok, n + 1)
            for i in range(NT):
                for t in range(NT):
                    ins = pe.matmul(bank[4 + u % 2][:, i * unit.dv:(i + 1) * unit.dv],
                                    pT_at[:, u % 2, t, tok(i)], unit.v[t], start=(t == 0), stop=(t == NT - 1))
            ins.then_inc(pv_ps, 1)

        def pe_units(pe, units, lg, n0, old=0, between=None):
            def values(u):
                if old or u >= 2:
                    pe.wait_ge(o_ok, n0 + u - 1)
                pe_values(pe, u, n0 + u, units[u])

            for u in range(len(units)):
                n = n0 + u
                if u == 0:
                    if old:
                        pe.wait_ge(ex_ok, n)
                    pe_scores(pe, u, units[u])
                if u + 1 < len(units):
                    if old or u >= 1:
                        pe.wait_ge(ex_ok, n)
                    pe_scores(pe, u + 1, units[u + 1])
                if between:
                    between(u)
                if u >= 1:
                    values(u - 1)
                if old or u >= 2:
                    pe.wait_ge(pt_ok, n - 1)
                pe_probs_T(pe, u, n, lg)
            values(len(units) - 1)

        def act_units(act, units, lg, n0, old=0, between=None):
            for u, unit in enumerate(units):
                n = n0 + u
                b = u % 2
                act.wait_ge(lg_ok, n + 1)
                if old or u >= 2:
                    act.wait_ge(o_ok, n - 1)
                    act.wait_ge(pt_ps, n - 1)
                for i in range(NT):
                    if unit.bias is None:
                        src, dst, scale = bank[b][:, i * S:(i + 1) * S], lg[:, b, i, 0:S], unit.scale
                    else:
                        w = S + (unit.sink is not None)
                        src = dst = lg[:, b, i, 0:w]
                        scale = 1.0
                    ins = act.activation(dst, src, ACT.Exp, bias=nmax[:, b, i:i + 1], scale=scale,
                                         accum_out=den[:, b, i:i + 1])
                ins.then_inc(ex_ok, 1)
                act.wait_ge(pt_ps, n + 1)
                if old or u >= 2:
                    act.wait_ge(pv_ps, n - 1)
                act.activation(pT_at[:, b].rearrange("p t s -> p (t s)"), bank[2 + b][:], ACT.Copy).then_inc(pt_ok, 1)
                if between:
                    between(u)

        def dve_logits(dve, st, u, n, unit, lg, old):
            b = u % 2
            dve.wait_ge(sc_ps, n + 1)
            if old or u >= 2:
                dve.wait_ge(ex_ok, n - 1)
                dve.wait_ge(pt_ps, n - 1)
            src = bank[b][:].rearrange("p (i s) -> p i s", i=NT)
            if unit.bias is None:
                st.link(dve.tensor_reduce(nmax[:, b], src, X, ALU.max, negate=True))
                dve.tensor_scalar(nmax[:, b], nmax[:, b], unit.scale, None, ALU.mult).then_inc(lg_ok, 1)
                return
            w = S + (unit.sink is not None)
            st.then(dve.scalar_tensor_tensor(lg[:, b, :, 0:S], src, unit.scale, unit.bias, ALU.mult, ALU.add))
            if unit.sink is not None:
                st.then(dve.tensor_copy(lg[:, b, :, S:w], unit.sink.unsqueeze(1).to_broadcast([P, NT, 1])))
            st.sync()
            dve.tensor_reduce(nmax[:, b], lg[:, b, :, 0:w], X, ALU.max, negate=True).then_inc(lg_ok, 1)

        def dve_output(dve, st, u, n, unit):
            b = u % 2
            dve.wait_ge(pv_ps, n + 1)
            st.link(dve.reciprocal(rden[:, b], den[:, b]))
            src = bank[4 + b][:, 0:NT * unit.dv].rearrange("p (i d) -> p i d", i=NT)
            if unit.half == 1:
                st.link(dve.tensor_scalar(nrd[:, b], rden[:, b], nlam[:, 0:1], None, ALU.mult))
                for i in range(NT):
                    ins = dve.scalar_tensor_tensor(unit.out[:, i], src[:, i], nrd[:, b, i:i + 1], unit.out[:, i],
                                                   ALU.mult, ALU.add)
                    if i < NT - 1:
                        st.then(ins)
            else:
                ins = dve.tensor_tensor(unit.out, src, bc(rden[:, b], unit.dv), ALU.mult)
            ins.then_inc(o_ok, 1)
            if unit.half == 0:
                dve.wait_ge(o_ok, n + 1)

        def dve_units(dve, st, units, lg, n0, old=0, between=None):
            dve_logits(dve, st, 0, n0, units[0], lg, old)
            for u in range(len(units)):
                if u + 1 < len(units):
                    dve_logits(dve, st, u + 1, n0 + u + 1, units[u + 1], lg, old)
                if between:
                    between(u)
                if u >= 1:
                    dve_output(dve, st, u - 1, n0 + u - 1, units[u - 1])
            dve_output(dve, st, len(units) - 1, n0 + len(units) - 1, units[-1])

        def ret_rows(h, blk):
            r = 64 * (h % 2)
            return qkT[r:r + 64, blk + h // 2, :]

        def pe_ret_scores(pe, h):
            if h >= 1:
                pe.wait_ge(rp_ok, h)
            for t in range(NT):
                ins = pe.matmul(bank[6][:, t * S:(t + 1) * S], ret_rows(h, 10)[:, tok(t)], ret_rows(h, 8),
                                start=True, stop=True)
            ins.then_inc(rs_ps, 1)

        def pe_ret_values(pe, h):
            pe.wait_ge(rp_ok, h + 1)
            if h >= 1:
                pe.wait_ge(ro_ok, h)
            c = 3 * AH * AD + 2 * RH * 64 + h * RV
            for i in range(NT):
                for t in range(NT):
                    ins = pe.matmul(bank[7][:, i * RV:(i + 1) * RV], dec[:, h % 2, t, tok(i)], proj[:, t, c:c + RV],
                                    start=(t == 0), stop=(t == NT - 1))
            ins.then_inc(rv_ps, 1)

        POW_NORM = [1, 2, 9, 11]
        POW1 = 11

        def power(pool, st, dst, src, scale, eps):
            st.link(pool.tensor_scalar(dst, src, scale, eps, ALU.mult, ALU.add))
            inverse_root(pool, dst)

        @block.gpsimd
        def _(pool):
            st = Steps(pool, pool_step)
            st.link(pool.memset(minus_half[:], -0.5))

            def rows(k):
                pool.wait_ge(sumsq, k + 1)
                power(pool, st, rs, ss, 1.0 / D, EPS1)

            def heads(k, n, width):
                pool.wait_ge(var_ok, k)
                power(pool, st, rsq[:, :, 0:n], ssq[:, :, 0:n], 1.0 / width, EPS1)

            def lows(run):
                for c in range(2):
                    low(pool, run, c)

            rows(0)
            lows(runs1[0])
            rows(1)
            heads(1, MH, MD)
            lows(runs1[1])
            heads(2, 2 * AH, AD)
            lows(runs1[2])
            for h in range(RH):
                pool.wait_ge(var_ok, 3 + h)
                power(pool, st, rs, mean[:, :, 1], 1.0, GN_EPS)
            rows(2)
            lows(runs1[3])
            pool.wait_ge(sq_a, 1)
            heads(7, MH, MD)
            lows(runs1[4])
            rows(3)
            pool_layers(pool, st)

        @block.tensor
        def _(pe):
            pe.wait_ge(first_in, 32)
            pe.wait_ge(z_ok, 1)

            def tokens(t):
                return [[t[:, i, b * P:(b + 1) * P] for i in range(NT)] for b in range(KD)]

            pe.wait_ge(xn_ok, 1)
            pe_T(pe, tokens(memt), 0)
            pe.wait_ge(t_out, 4)
            pe_part(pe, runs1[0], 0, xTl1, 0)
            pe_part(pe, runs1[0], 1, xTl1, 1)
            pe.wait_ge(den_a, 2)
            pe.wait_ge(den_v, 2)
            pe.wait_ge(xn_ok, 2)
            pe_T(pe, tokens(xn), 4)
            pe.wait_ge(t_src, 1)
            pe.wait_ge(t_out, 8)
            pe_T(pe, tokens(mk), 8)
            for n in (2, 3, 4):
                if n == 3:
                    pe.wait_ge(t_out, 12)
                if n == 4:
                    pe.wait_ge(den_a, 3)
                    pe.wait_ge(den_v, 3)
                pe_part(pe, runs1[1], n - 2, xTl1, n)
            pe.wait_ge(den_a, 5)
            pe.wait_ge(t_src, 2)
            pe_T(pe, [[proj[:, i, c:c + P] for i in range(NT)]
                      for c in [*range(0, 1024, P), *range(1536, 2048, P)]], 12)
            pe.wait_ge(t_out, 18)
            pe_ret_scores(pe, 0)

            def between(u):
                if u < 2 * RH:
                    if u % 2 == 1:
                        pe_ret_values(pe, u // 2)
                    elif u > 0:
                        pe_ret_scores(pe, u // 2)

            pe.wait_ge(consts_in, 16 * N_CONST)
            pe_units(pe, units1[:AH], lg1, 0, between=between)
            pe.wait_ge(t_src, 3)
            pe_T(pe, tokens(cat), 18)
            pe.wait_ge(t_out, 22)
            pe_part(pe, runs1[2], 0, xTl1, 0)
            pe_tiles_T(pe, xn, 22, (xn_ok, 3), (xn1_ok, 1))
            pe.wait_ge(t_out, 26)
            pe_part(pe, runs1[3], 0, xTl1, 0)
            pe.wait_ge(t_src, 4)
            pe.wait_ge(mq_a, 1)
            pe_T(pe, tokens(mq), 26)
            pe.wait_ge(t_out, 30)
            pe_units(pe, units1[AH:], lg1, AH, old=1)
            pe.wait_ge(o_ok, UNITS1)
            pe_T(pe, tokens(cat), 30)
            pe.wait_ge(t_out, 34)
            pe_part(pe, runs1[4], 0, xTl1, 0)
            pe_moe(pe, tokens)
            pe_layers(pe, tokens)

        @block.scalar
        def _(act):
            st = Steps(act, act_step)

            def norm(k, src, dst):
                for i in range(NT):
                    ins = act.activation(tmp[:], src[:, i], ACT.Square, accum_out=ss[:, i:i + 1])
                    if i < NT - 1:
                        st.link(ins)
                ins.then_inc(sumsq, 1)
                act.wait_ge(pow_ok, POW_NORM[k])
                for i in range(NT):
                    ins = act.activation(dst[:, i], src[:, i], ACT.Copy, scale=rs[:, i:i + 1])
                ins.then_inc(xn_ok, 1)

            def norm_tile(k):
                for i in range(NT):
                    act.wait_ge((x0_ok, x_ok)[i], k - 1)
                    ins = act.activation(tmp[:], x[:, i], ACT.Square, accum_out=ss[:, i:i + 1])
                    if i < NT - 1:
                        st.link(ins)
                ins.then_inc(sumsq, 1)
                act.wait_ge(pow_ok, POW_NORM[k])
                act.activation(xn[:, 0], x[:, 0], ACT.Copy, scale=rs[:, 0:1]).then_inc(xn_ok, 1)

            act.wait_ge(mem_in, 16)
            norm(0, memt, memt)
            act.wait_ge(first_in, 32)
            for c in range(2):
                act_high(act, runs1[0], c)
            act_high_T(act, runs1[0], colw[:, 0])
            for c in range(2, 4):
                act_high(act, runs1[0], c)
            act.wait_ge(consts_in, 16 * N_CONST)
            norm(1, x, xn)
            stream(lambda c: act_high(act, runs1[0], c), runs1[0], 4,
                   [lambda: evac_act(act, 0, 1, mk[:, 0]), lambda: evac_act(act, 1, 2, mv[:, 0])])
            act_high(act, runs1[1], 0)
            act_high_T(act, runs1[1], colw[:, 1])
            act_high(act, runs1[1], 1)
            stream(lambda c: act_high(act, runs1[1], c), runs1[1], 2,
                   [lambda n=n: evac_act(act, n, n + 1, proj[:, 0, (n - 2) * D:(n - 1) * D])
                    for n in (2, 3, 4)])
            act.wait_ge(lgam, 1)
            act.activation(lt[:, 1], lt[:, 0], ACT.Exp).then_inc(lgam, 1)
            act.wait_ge(lgam, 3)
            act.activation(lt[:, 3], lt[:, 2], ACT.Ln).then_inc(lgam, 1)
            act.wait_ge(den_v, 5)
            act.wait_ge(den_a, 5)
            act.activation(proj[:, :, 2560:3072], proj[:, :, 2560:3072], ACT.Silu).then_inc(gate_ok, 1)

            def decay(h):
                act.wait_ge(rd_in, h + 1)
                act.activation(dec[:, h % 2], dec[:, h % 2], ACT.Exp).then_inc(rd_ok, 1)

            decay(0)

            def between(u):
                if u % 2 == 1 and u // 2 + 1 < RH:
                    decay(u // 2 + 1)

            for c in range(2):
                act_high(act, runs1[2], c)
            act_units(act, units1[:AH], lg1, 0, between=between)
            act_high_T(act, runs1[2], colw[:, 5])
            for c in range(2, 4):
                act_high(act, runs1[2], c)
            norm_tile(2)
            act_high(act, runs1[3], 0)
            act_high(act, runs1[3], 1)
            act_high_T(act, runs1[3], colw[:, 6])
            for c in range(2, 4):
                act_high(act, runs1[3], c)
            evac_act(act, 0, 7, mq[:, 0])
            for h in range(MH):
                ins = act.activation(tmp[:, h * MD:(h + 1) * MD], bank[h // 2][:, h % 2 * MD:(h % 2 + 1) * MD],
                                     ACT.Square, accum_out=ssq[:, 0, h:h + 1])
            ins.then_inc(sq_a, 1)
            act.wait_ge(pow_ok, 10)
            act.wait_ge(den_a, 6)
            for h in range(MH):
                head = mq[:, 0, h * MD:(h + 1) * MD]
                ins = act.activation(head, head, ACT.Copy, scale=rsq[:, 0, h:h + 1])
            ins.then_inc(mq_a, 1)
            for c in range(2):
                act_high(act, runs1[4], c)
            act_units(act, units1[AH:], lg1, AH, old=1)
            act_high_T(act, runs1[4])
            for c in range(2, 4):
                act_high(act, runs1[4], c)
            norm_tile(3)
            act_moe(act, st)
            act_layers(act, st)

        @block.vector
        def _(dve):
            st = Steps(dve, dve_step)
            dve.sem_inc(wl_ok, 2 * FT)
            dve.memset(zeros[:], 0.0).then_inc(z_ok, 1)

            def head_squares(src, heads, width):
                for i in range(NT):
                    t = tmp[:, 0:heads * width].rearrange("p (h w) -> p h w", h=heads)
                    st.link(dve.tensor_tensor(t, src[i], src[i], ALU.mult))
                    ins = dve.tensor_reduce(ssq[:, i, 0:heads], t, X, ALU.add)
                    if i < NT - 1:
                        st.link(ins)
                ins.then_inc(var_ok, 1)

            def head_scale(k, src, heads, width, post):
                dve.wait_ge(pow_ok, k)
                for i in range(NT):
                    ins = dve.tensor_tensor(src[i], src[i], bc(rsq[:, i, 0:heads], width), ALU.mult)
                    if i < NT - 1:
                        st.link(ins)
                ins.then_inc(post, 1)

            def residual(parts, k):
                dve.wait_ge(consts_in, 16 * N_CONST)
                for i in range(NT):
                    if i == 0:
                        dve.wait_ge(half_ok, parts)
                    else:
                        dve.wait_ge(d_used, PART1[parts])
                    for j in range(2):
                        ins = dve.tensor_tensor(x[:, i, j * 512:(j + 1) * 512], bank[2 * i + j][:],
                                                x[:, i, j * 512:(j + 1) * 512], ALU.add)
                        if j == 0:
                            st.link(ins)
                    ins.then_inc((x0_ok, x_ok)[i], 1)
                dve.wait_ge(x_ok, k - 1)
                dve.wait_ge(pow_ok, POW_NORM[k])
                dve.tensor_scalar(xn[:, 1], x[:, 1], rs[:, 1:2], None, ALU.mult).then_inc(xn1_ok, 1)

            dve.wait_ge(first_in, 32)
            dve_low_T(dve, runs1[0], xTl1, colw[:, 0])
            for c in range(2, 5):
                low(dve, runs1[0], c)
            evac_dve(dve, 0, PART1[1], mk[:, 1])
            low(dve, runs1[0], 5)
            dve.wait_ge(den_a, 1)
            dve.wait_ge(den_v, 1)
            mk_heads = [mk[:, i].rearrange("p (h w) -> p h w", h=MH) for i in range(NT)]
            head_squares(mk_heads, MH, MD)
            low(dve, runs1[0], 6)
            head_scale(3, mk_heads, MH, MD, t_src)
            low(dve, runs1[0], 7)
            evac_dve(dve, 1, PART1[2], mv[:, 1])
            dve_low_T(dve, runs1[1], xTl1, colw[:, 1])
            dve_T(dve, mkT, KD, 8, colw[:, 2])
            dve.wait_ge(consts_in, 16 * N_CONST)
            a = row1[:]
            st.link(dve.tensor_scalar(lt[:, 4], a, -1.0, None, ALU.mult))
            st.link(dve.tensor_tensor(lt[:, 0], a, lt[:, 4], ALU.max))
            dve.tensor_scalar(lt[:, 0], lt[:, 0], -1.0, None, ALU.mult).then_inc(lgam, 1)
            qk_heads = [proj[:, i, 0:D].rearrange("p (h w) -> p h w", h=2 * AH) for i in range(NT)]

            def project(c):
                low(dve, runs1[1], c)
                if c == 5:
                    dve.wait_ge(den_a, 3)
                    dve.wait_ge(den_v, 3)
                    head_squares(qk_heads, 2 * AH, AD)
                if c == 6:
                    head_scale(4, qk_heads, 2 * AH, AD, t_src)

            stream(project, runs1[1], 2,
                   [lambda n=n: evac_dve(dve, n, PART1[n + 1], proj[:, 1, (n - 2) * D:(n - 1) * D])
                    for n in (2, 3, 4)])
            dve_T(dve, qkT, 12, 12, colw[:, 3:5].rearrange("p a b -> p (a b)"))
            dve.wait_ge(lgam, 2)
            dve.tensor_scalar(lt[:, 2], lt[:, 1], 1.0, None, ALU.add).then_inc(lgam, 1)
            dve.wait_ge(lgam, 4)
            st.link(dve.tensor_scalar(lt[:, 4], lt[:, 4], 0.0, None, ALU.max))
            st.link(dve.tensor_tensor(lgm, lt[:, 3], lt[:, 4], ALU.add))
            st.link(dve.tensor_scalar(lgm, lgm, -1.0, None, ALU.mult))

            def exponents(h):
                if h >= 2:
                    dve.wait_ge(rv_ps, h - 1)
                st.link(dve.tensor_scalar(dec[:, h % 2], rel[:, 0], lgm[:, h:h + 1], None, ALU.mult))
                dve.scalar_tensor_tensor(dec[:, h % 2], rel[:, 1], lgm[:, RH + h:RH + h + 1], dec[:, h % 2],
                                         ALU.mult, ALU.add).then_inc(rd_in, 1)

            def decayed(h):
                dve.wait_ge(rd_ok, h + 1)
                dve.wait_ge(rs_ps, h + 1)
                dve.scalar_tensor_tensor(dec[:, h % 2], bank[6][:].rearrange("p (t s) -> p t s", t=NT), 64 ** -0.5,
                                         dec[:, h % 2], ALU.mult, ALU.mult).then_inc(rp_ok, 1)

            def ret_out(h):
                dve.wait_ge(rv_ps, h + 1)
                for i in range(NT):
                    st.then(dve.bn_stats(bn[:, i, 0, :], bank[7][:, i * RV:(i + 1) * RV]))
                st.sync()
                for i in range(NT):
                    ins = dve.bn_aggr(mean[:, i, :], bn[:, i, 0, :])
                    if i < NT - 1:
                        st.link(ins)
                ins.then_inc(var_ok, 1)
                dve.wait_ge(pow_ok, 5 + h)
                for i in range(NT):
                    ins = dve.tensor_scalar(cat[:, i, 512 + h * RV:512 + (h + 1) * RV], bank[7][:, i * RV:(i + 1) * RV],
                                            mean[:, i, 0:1], rs[:, i:i + 1], ALU.subtract, ALU.mult)
                    if i < NT - 1:
                        st.then(ins)
                ins.then_inc(ro_ok, 1)

            exponents(0)
            dve.wait_ge(bias_in, 16)

            def between(u):
                if u % 2 == 0:
                    decayed(u // 2)
                    if u // 2 + 1 < RH:
                        exponents(u // 2 + 1)
                else:
                    ret_out(u // 2)

            dve_units(dve, st, units1[:AH], lg1, 0, between=between)
            dve.wait_ge(gate_ok, 1)
            dve.wait_ge(ro_ok, RH)
            dve.wait_ge(o_ok, AH)
            dve.tensor_tensor(cat[:, :, 512:1024], cat[:, :, 512:1024], proj[:, :, 2560:3072], ALU.mult).then_inc(t_src, 1)
            dve_low_T(dve, runs1[2], xTl1, colw[:, 5])
            for c in range(2, 4):
                low(dve, runs1[2], c)
            residual(6, 2)
            dve_low_T(dve, runs1[3], xTl1, colw[:, 6])
            for c in range(2, 4):
                low(dve, runs1[3], c)
            evac_dve(dve, 0, PART1[7], mq[:, 1])
            dve.wait_ge(den_v, 6)
            head = mq[:, 1].rearrange("p (h w) -> p h w", h=MH)
            squares = proj[:, 1, D:2 * D].rearrange("p (h w) -> p h w", h=MH)
            st.link(dve.tensor_tensor(squares, head, head, ALU.mult))
            dve.tensor_reduce(ssq[:, 1, 0:MH], squares, X, ALU.add).then_inc(var_ok, 1)
            dve.wait_ge(pow_ok, 10)
            dve.tensor_tensor(head, head, bc(rsq[:, 1, 0:MH], MD), ALU.mult).then_inc(t_src, 1)
            dve_T(dve, mqT, KD, 26, colw[:, 7])
            dve_units(dve, st, units1[AH:], lg1, AH, old=1)
            dve_low_T(dve, runs1[4], xTl1)
            for c in range(2, 4):
                low(dve, runs1[4], c)
            residual(8, 3)
            dve_moe(dve, st)
            dve_layers(dve, st)


def lay_out(a):
    f32 = np.float32
    a = {k: np.asarray(v) for k, v in a.items()}

    def chunks(w, widths):
        out, c = [], 0
        for n in widths:
            per = CH // n if n == D else KD
            part = w[:, c:c + n].reshape(KD // per, per, P, n).transpose(0, 2, 1, 3).reshape(KD // per, P, per * n)
            if part.shape[2] < CH:
                part = np.concatenate([part, np.zeros((part.shape[0], P, CH - part.shape[2]), w.dtype)], 2)
            out.append(part)
            c += n
        return np.concatenate(out)

    w1 = np.concatenate([chunks(a["w_mkv"][0], [D, D]), chunks(a["w_in"][0], [D] * 3), chunks(a["w_out"][0], [D]),
                         chunks(a["w_mq"][0], [D]), chunks(a["w_mo"][0], [D])])
    gate = a["w_exp_gate"][0].reshape(NE, 4, 2, P, 4, P)
    up = a["w_exp_up"][0].reshape(NE, 4, 2, P, 4, P)
    gu = np.stack([gate, up], 5).transpose(0, 1, 3, 2, 4, 5, 6).reshape(NE, 4, P, CH)
    down = a["w_exp_down"][0].reshape(NE, 2, 2, P, D).transpose(0, 1, 3, 2, 4).reshape(NE, 2, P, CH)
    we = np.concatenate([gu, down], 1).reshape(NE * 6, P, CH)
    g = a["ffn_w_gu_2"].reshape(LAYERS, 2, KD, P, 2, FT, P).transpose(0, 1, 5, 3, 2, 4, 6).reshape(LAYERS * 2, FT, P, 2 * D)
    dn = a["ffn_w_down_2"].reshape(LAYERS * 2, FT, P, D)
    wf = np.concatenate([g, dn], 3).reshape(LAYERS * 2 * FT, P, FTW)
    heads = np.array([0, 2, 1, 3])
    q64 = (heads[:, None] * 64 + np.arange(64)).ravel()
    oa, ob, oc, od = 0, 512, 512 + 416, 512 + 416 + 512
    cols = np.concatenate([ob + np.arange(416), oc + q64, oc + np.arange(256, 512),
                           oa + q64, oa + np.arange(256, 512), od + np.arange(768)])
    w2 = []
    for l in range(LAYERS):
        dense = chunks(a["w_in_2"][l][:, cols], [D, D, W3])
        mla = np.concatenate([a["mla_w_uq_2"][l].reshape(2, P, 384).transpose(1, 0, 2).reshape(P, 768),
                              a["mla_w_ukv_2"][l]], 1)
        mla = np.concatenate([mla, np.zeros((P, CH - mla.shape[1]), f32)], 1)[None]
        w2.append(np.concatenate([dense, mla, chunks(a["w_out_2"][l], [D])]))
    w2 = np.concatenate(w2)

    def col(v):
        return v.reshape(-1, P).T

    def rep(v, n):
        return np.tile(v, (n,) + (1,) * (v.ndim - 1))

    one = np.ones((P, 1), f32)
    aq, ak = (np.concatenate([a[n][0]] * 2)[:, None] for n in ("attn_q_norm_w", "attn_k_norm_w"))
    cT1 = np.concatenate([
        col(a["norm_memkv_w"][0]), col(a["norm_mix_w"][0]), np.tile(col(a["mem_k_norm_w"][0]), (1, 4)),
        np.tile(aq, (1, 4)), np.tile(ak, (1, 4)), np.tile(one, (1, 8)),
        np.tile(one, (1, 4)), col(a["ret_gn_w"][0]),
        col(a["norm_mem_w"][0]), np.tile(col(a["mem_q_norm_w"][0]), (1, 4)), col(a["norm_moe_w"][0])], 1)
    row1 = np.tile(np.concatenate([a["ret_decay_f"][0], a["ret_decay_b"][0]])[None], (P, 1))
    router = np.concatenate([a["w_group"][0], a["w_router"][0].transpose(1, 0, 2).reshape(D, NE)], 1)
    wr = router.reshape(KD, P, NG + NE).transpose(1, 0, 2).reshape(P, -1)
    cT2, row2 = [], []
    for l in range(LAYERS):
        sub = np.concatenate([a["diff_subln_2"][l]] * 2)[:, None]
        cT2.append(np.concatenate([np.tile(one, (1, 6)), np.tile(sub, (1, 2)), col(a["mla_q_norm_2"][l]),
                                   col(a["mla_kv_norm_2"][l])], 1))
        init = 0.8 - 0.6 * np.exp(-0.3 * l)
        row2.append(np.tile(np.concatenate([np.tile(a["ax_q_norm_2"][l], 4), np.tile(a["ax_k_norm_2"][l], 2),
                                            a["win_sink_2"][l], a["diff_lambda_2"][l].ravel(),
                                            np.array([init, 1 - init], f32)])[None], (P, 1)))
    lnp = np.stack([a["ln_g_2"], a["ln_b_2"]], 2).reshape(LAYERS * 3, 1, 2 * D)
    ln = np.broadcast_to(lnp, (LAYERS * 3, P, 2 * D))
    t = np.arange(S)
    dist = np.abs(t[:, None] - t[None, :]).astype(f32)

    def tiled(m):
        return m.reshape(NT, P, -1).transpose(1, 0, 2).reshape(P, -1)

    diff = (t[None, :] - t[:, None]).astype(f32)
    inv16 = 10000.0 ** (-np.arange(0, 32, 2) / 32)
    ang = t[:, None] * inv16
    row_a, col_a = (t // 64)[:, None] * inv16, (t % 64)[:, None] * inv16
    tab_rope = np.concatenate([np.cos(ang), np.sin(ang), np.cos(row_a), np.cos(col_a), np.sin(row_a), np.sin(col_a)], 1)
    tab = np.concatenate([
        np.eye(P), (np.arange(P)[:, None] < np.arange(P)[None, :]), np.ones((P, P)), np.tile(t[None], (P, 1)),
        tiled(np.maximum(diff, 0)), tiled(np.maximum(-diff, 0)),
        np.tile(np.concatenate([NG - np.arange(NG), NE - np.arange(NE)])[None], (P, 1)), tiled(tab_rope)], 1).astype(f32)
    slopes = 2.0 ** -(np.arange(8) + 1.0)
    times = (dist <= 64).astype(int) + (dist % 4 == 0) + (dist % 16 == 0)
    log_times = np.where(times > 0, np.log(np.maximum(times, 1)), NEG)
    window = np.where(dist <= 128, 0.0, NEG)
    b1 = np.stack([tiled(-s * dist + log_times) for s in slopes], 1)
    b2 = np.stack([tiled(-s * dist + (window if i < 4 else 0.0)) for i, s in enumerate(slopes)], 1)
    biases = np.stack([b1, b2]).reshape(2, P, -1).astype(f32)
    return dict(x=a["x"][0], mem=a["mem"][0], w1=w1, we=we, wf=wf, w2=w2, cT1=cT1, row1=row1, wr=wr,
                cT2=np.stack(cT2), row2=np.stack(row2), ln=ln, tab=tab, bias=biases)


ORDER = ["x", "mem", "w1", "we", "wf", "w2", "cT1", "row1", "wr", "cT2", "row2", "ln", "tab", "bias"]


def kernel(**inputs):
    import concourse.bacc as bacc
    from concourse.bass_utils import run_bass_kernel_spmd

    arrays = {f"in_{k}": np.ascontiguousarray(v) for k, v in lay_out(inputs).items()}
    nc = bacc.Bacc("TRN2", target_bir_lowering=False, num_devices=1)
    args = [nc.dram_tensor(f"in_{k}", arrays[f"in_{k}"].shape, mybir.dt.from_np(arrays[f"in_{k}"].dtype),
                           kind="ExternalInput").ap() for k in ORDER]
    out = nc.dram_tensor("out_x", (S, D), F32, kind="ExternalOutput").ap()
    build(nc, *args, out)
    r = run_bass_kernel_spmd(nc, [arrays], core_ids=[0])
    return r.results[0]["out_x"].reshape(1, S, D)
```
